# Optimizing a Trainium2 kernel written in Bass

```python
import math
import jax
import jax.numpy as jnp
from jax import lax
import numpy as np

D_MODEL = 1024
BATCH = 1
SEQ = 1024
DEPTH = 1
DEC_BATCH = 1
DEC_SEQ = 2048
PAST_LEN = 128

D_MIX = D_MODEL
SSD_WIDTH = D_MIX // 2
SSD_HEADDIM = 64
SSD_HEADS = SSD_WIDTH // SSD_HEADDIM
SSD_GROUPS = 2
SSD_STATE = 128
SSD_CONV = 5
SSD_CHUNK = 128
SSD_CONV_CH = SSD_WIDTH + 2 * SSD_GROUPS * SSD_STATE
S5_WIDTH = D_MIX - SSD_WIDTH
S5_GROUP_CH = 16
S5_GROUPS = S5_WIDTH // S5_GROUP_CH
S5_STATE = 64
S5_MIN_DECAY = 1e-4
IN_COLS = SSD_WIDTH + SSD_CONV_CH + 2 * SSD_HEADS + S5_WIDTH
N_EXPERTS = 16
N_EXPERT_GROUPS = 4
EXPERTS_PER_GROUP = N_EXPERTS // N_EXPERT_GROUPS
TOP_K = 2
D_EXPERT = D_MODEL // 2
MOE_BLOCK = 128
DEEPNORM_ALPHA = (2 * DEPTH) ** 0.25
DEEPNORM_BETA = (8 * DEPTH) ** -0.25
LN_EPS = 1e-5
RMS_EPS = 1e-5

kernel_name = 'hymba_ssd_s5_deepnorm_moe_encoder'

def _layer_norm(x32, g, b):
    mu = jnp.mean(x32, axis=-1, keepdims=True)
    xc = x32 - mu
    var = jnp.mean(xc * xc, axis=-1, keepdims=True)
    return xc * lax.rsqrt(var + LN_EPS) * g.astype(jnp.float32) + b.astype(jnp.float32)

def _centred_depthwise_conv(x, w, b):
    out = lax.conv_general_dilated(
        x, w[:, None, :], window_strides=(1,),
        padding=[(SSD_CONV // 2, SSD_CONV // 2)],
        dimension_numbers=('NWC', 'WIO', 'NWC'),
        feature_group_count=x.shape[-1])
    return out + b

def _ssd_chunked_scan(x, dt, a, b_mat, c_mat):
    bsz, seqlen = x.shape[0], x.shape[1]
    nc = seqlen // SSD_CHUNK
    r = SSD_HEADS // SSD_GROUPS
    x = x.reshape(bsz, nc, SSD_CHUNK, SSD_GROUPS, r, SSD_HEADDIM)
    dt = dt.reshape(bsz, nc, SSD_CHUNK, SSD_GROUPS, r)
    b_mat = b_mat.reshape(bsz, nc, SSD_CHUNK, SSD_GROUPS, SSD_STATE)
    c_mat = c_mat.reshape(bsz, nc, SSD_CHUNK, SSD_GROUPS, SSD_STATE)
    a_cum = jnp.cumsum(dt * a.reshape(SSD_GROUPS, r), axis=2)
    xdt = x * dt[..., None]
    lower = jnp.tril(jnp.ones((SSD_CHUNK, SSD_CHUNK), bool))[None, None, :, :, None, None]
    seg = a_cum[:, :, :, None] - a_cum[:, :, None, :]
    decay = jnp.exp(jnp.where(lower, seg, -jnp.inf))
    cb = jnp.einsum('bcign,bcjgn->bcijg', c_mat, b_mat)
    y_diag = jnp.einsum('bcijgr,bcjgrp->bcigrp', cb[..., None] * decay, xdt)
    to_end = jnp.exp(a_cum[:, :, -1:] - a_cum)
    states = jnp.einsum('bcjgn,bcjgrp->bcgrpn', b_mat, xdt * to_end[..., None])
    chunk_decay = jnp.exp(a_cum[:, :, -1])

    def carry_fn(h, inp):
        s, d = inp
        return h * d[..., None, None] + s, h

    h0 = jnp.zeros((bsz, SSD_GROUPS, r, SSD_HEADDIM, SSD_STATE), x.dtype)
    _, h_in = lax.scan(carry_fn, h0, (jnp.moveaxis(states, 1, 0), jnp.moveaxis(chunk_decay, 1, 0)))
    h_in = jnp.moveaxis(h_in, 0, 1)
    y_off = jnp.einsum('bcign,bcgrpn->bcigrp', c_mat, h_in) * jnp.exp(a_cum)[..., None]
    return (y_diag + y_off).reshape(bsz, seqlen, SSD_HEADS, SSD_HEADDIM)

def _ssd_mixer(z, xbc, dt_raw, conv_w, conv_b, a_log, dt_bias, d_skip, norm_w):
    f32 = jnp.float32
    bsz, seqlen = z.shape[0], z.shape[1]
    xbc = jax.nn.silu(_centred_depthwise_conv(xbc.astype(f32), conv_w.astype(f32), conv_b.astype(f32)))
    xs, b_mat, c_mat = jnp.split(xbc, [SSD_WIDTH, SSD_WIDTH + SSD_GROUPS * SSD_STATE], axis=-1)
    xs = xs.reshape(bsz, seqlen, SSD_HEADS, SSD_HEADDIM)
    b_mat = b_mat.reshape(bsz, seqlen, SSD_GROUPS, SSD_STATE)
    c_mat = c_mat.reshape(bsz, seqlen, SSD_GROUPS, SSD_STATE)
    dt = jax.nn.softplus(dt_raw.astype(f32).reshape(bsz, seqlen, 2, SSD_HEADS) + dt_bias.astype(f32))
    a = -jnp.exp(a_log.astype(f32))
    rev = lambda t: jnp.flip(t, axis=1)
    y_fwd = _ssd_chunked_scan(xs, dt[:, :, 0], a[0], b_mat, c_mat)
    y_bwd = rev(_ssd_chunked_scan(rev(xs), rev(dt[:, :, 1]), a[1], rev(b_mat), rev(c_mat)))
    y = (y_fwd + y_bwd + xs * d_skip.astype(f32)[:, None]).reshape(bsz, seqlen, SSD_WIDTH)
    y = y * jax.nn.silu(z.astype(f32))
    return y * lax.rsqrt(jnp.mean(y * y, axis=-1, keepdims=True) + RMS_EPS) * norm_w.astype(f32)

def _diag_recurrence(e1, e2):
    a1, b1 = e1
    a2, b2 = e2
    return a2 * a1, a2 * b1 + b2

def _s5_mixer(u, lam_re, lam_im, log_step, b_re, b_im, c_re, c_im, d_skip, w_glu, b_glu):
    f32 = jnp.float32
    bsz, seqlen = u.shape[0], u.shape[1]
    ug = u.astype(f32).reshape(bsz, seqlen, S5_GROUPS, S5_GROUP_CH)
    b_in = lax.complex(b_re.astype(f32), b_im.astype(f32))
    y = ug * d_skip.astype(f32).reshape(S5_GROUPS, S5_GROUP_CH)
    ugc = ug.astype(jnp.complex64)
    for direction, reverse in ((0, False), (1, True)):
        lam = lax.complex(jnp.minimum(lam_re[direction].astype(f32), -S5_MIN_DECAY),
                          lam_im[direction].astype(f32))
        step = jnp.exp(log_step[direction].astype(f32))[:, None]
        lam_bar = jnp.exp(lam * step)
        b_bar = ((lam_bar - 1.0) / lam)[..., None] * b_in
        bu = jnp.einsum('blgi,gpi->blgp', ugc, b_bar)
        _, states = lax.associative_scan(
            _diag_recurrence, (jnp.broadcast_to(lam_bar, bu.shape), bu), axis=1, reverse=reverse)
        c_out = lax.complex(c_re[direction].astype(f32), c_im[direction].astype(f32))
        y = y + jnp.real(jnp.einsum('blgp,gip->blgi', states, c_out))
    y = jax.nn.gelu(y.reshape(bsz, seqlen, S5_WIDTH))
    return y * jax.nn.sigmoid(y @ w_glu.astype(f32) + b_glu.astype(f32))

def _moe(h, w_router, b_router, w_gate, w_up, w_down):
    f32 = jnp.float32
    bsz, seqlen, d = h.shape
    n_tok = bsz * seqlen
    xt = h.reshape(n_tok, d)
    probs = jax.nn.softmax(xt.astype(f32) @ w_router.astype(f32) + b_router.astype(f32), axis=-1)
    grp_score = probs.reshape(n_tok, N_EXPERT_GROUPS, EXPERTS_PER_GROUP).max(axis=-1)
    sel_grp = jnp.argmax(grp_score, axis=-1)
    in_grp = (jnp.arange(N_EXPERTS) // EXPERTS_PER_GROUP)[None, :] == sel_grp[:, None]
    top_v, top_i = lax.top_k(jnp.where(in_grp, probs, -1.0), TOP_K)
    gates = top_v / jnp.sum(top_v, axis=-1, keepdims=True)
    n_slots = n_tok * TOP_K
    flat_e = top_i.reshape(-1)
    flat_tok = jnp.arange(n_slots, dtype=jnp.int32) // TOP_K
    flat_w = gates.reshape(-1)
    order = jnp.argsort(flat_e)
    e_sorted = flat_e[order]
    counts = jnp.bincount(flat_e, length=N_EXPERTS)
    starts = jnp.cumsum(counts) - counts
    padded = (counts + MOE_BLOCK - 1) // MOE_BLOCK * MOE_BLOCK
    pend = jnp.cumsum(padded)
    pstart = pend - padded
    dest = pstart[e_sorted] + (jnp.arange(n_slots) - starts[e_sorted])
    n_blocks = -(-n_slots // MOE_BLOCK) + N_EXPERTS
    n_rows = n_blocks * MOE_BLOCK
    row_tok = jnp.zeros((n_rows,), jnp.int32).at[dest].set(flat_tok[order])
    row_w = jnp.zeros((n_rows,), f32).at[dest].set(flat_w[order])
    blk_e = jnp.minimum(jnp.searchsorted(pend, jnp.arange(n_blocks) * MOE_BLOCK, side='right'),
                        N_EXPERTS - 1)

    def expert_block(args):
        tok, e = args
        xb = jnp.take(xt, tok, axis=0)
        hid = jax.nn.silu(xb @ w_gate[e]) * (xb @ w_up[e])
        return hid @ w_down[e]

    out = lax.map(expert_block, (row_tok.reshape(n_blocks, MOE_BLOCK), blk_e))
    y = jnp.zeros((n_tok, d), f32).at[row_tok].add(out.reshape(n_rows, d).astype(f32) * row_w[:, None])
    return y.reshape(bsz, seqlen, d)

def _trunk(x, c, w_ada, b_ada, w_in, conv_w, conv_b, ssd_a_log, ssd_dt_bias, ssd_d, ssd_norm_w,
           s5_lam_re, s5_lam_im, s5_log_step, s5_b_re, s5_b_im, s5_c_re, s5_c_im, s5_d,
           s5_w_glu, s5_b_glu, w_out, ln1_g, ln1_b, ln2_g, ln2_b, w_router, b_router,
           w_gate, w_up, w_down):
    f32 = jnp.float32
    dtype = x.dtype
    c_act = jax.nn.silu(c.astype(f32))
    for i in range(DEPTH):
        mod = c_act @ w_ada[i].astype(f32) + b_ada[i].astype(f32)
        sh1, sc1, g1, sh2, sc2, g2 = [m[:, None, :] for m in jnp.split(mod, 6, axis=-1)]
        h = (x.astype(f32) * (1.0 + sc1) + sh1).astype(dtype)
        proj = h @ w_in[i]
        z, xbc, dt_raw, u = jnp.split(
            proj, [SSD_WIDTH, SSD_WIDTH + SSD_CONV_CH, SSD_WIDTH + SSD_CONV_CH + 2 * SSD_HEADS], axis=-1)
        y_ssd = _ssd_mixer(z, xbc, dt_raw, conv_w[i], conv_b[i], ssd_a_log[i], ssd_dt_bias[i],
                           ssd_d[i], ssd_norm_w[i])
        y_s5 = _s5_mixer(u, s5_lam_re[i], s5_lam_im[i], s5_log_step[i], s5_b_re[i], s5_b_im[i],
                         s5_c_re[i], s5_c_im[i], s5_d[i], s5_w_glu[i], s5_b_glu[i])
        mix = jnp.concatenate([y_ssd, y_s5], axis=-1).astype(dtype) @ w_out[i]
        x = _layer_norm(DEEPNORM_ALPHA * x.astype(f32) + g1 * mix.astype(f32), ln1_g[i], ln1_b[i]).astype(dtype)
        h = (x.astype(f32) * (1.0 + sc2) + sh2).astype(dtype)
        f = _moe(h, w_router, b_router, w_gate[i], w_up[i], w_down[i])
        x = _layer_norm(DEEPNORM_ALPHA * x.astype(f32) + g2 * f, ln2_g[i], ln2_b[i]).astype(dtype)
    return x

def setup_inputs(seed: int = 0) -> dict:
    key = jax.random.key(seed)
    ks = iter(jax.random.split(key, 48))
    f32 = jnp.float32

    def nrm(shape, scale):
        return jax.random.normal(next(ks), shape, f32) * scale

    def unif(shape, lo, hi):
        return jax.random.uniform(next(ks), shape, f32, lo, hi)

    inv_sqrt_d = D_MODEL ** -0.5
    dt0 = jnp.exp(unif((DEPTH, 2, SSD_HEADS), math.log(1e-3), math.log(1e-1)))
    lam_im0 = jnp.pi * jnp.arange(S5_STATE, dtype=f32)
    return {
        'x_prompt': nrm((BATCH, SEQ, D_MODEL), 1.0),
        'x_sample': nrm((DEC_BATCH, DEC_SEQ, D_MODEL), 1.0),
        'c_prompt': nrm((BATCH, D_MODEL), 1.0),
        'c_sample': nrm((DEC_BATCH, D_MODEL), 1.0),
        'w_ada': nrm((DEPTH, D_MODEL, 6 * D_MODEL), 0.5 * inv_sqrt_d),
        'b_ada': nrm((DEPTH, 6 * D_MODEL), 0.01),
        'w_in': nrm((DEPTH, D_MODEL, IN_COLS), inv_sqrt_d),
        'conv_w': nrm((DEPTH, SSD_CONV, SSD_CONV_CH), SSD_CONV ** -0.5),
        'conv_b': nrm((DEPTH, SSD_CONV_CH), 0.01),
        'ssd_a_log': jnp.log(unif((DEPTH, 2, SSD_HEADS), 1.0, 16.0)),
        'ssd_dt_bias': dt0 + jnp.log(-jnp.expm1(-dt0)),
        'ssd_d': 1.0 + nrm((DEPTH, SSD_HEADS), 0.01),
        'ssd_norm_w': 1.0 + nrm((DEPTH, SSD_WIDTH), 0.01),
        's5_lam_re': -0.5 + nrm((DEPTH, 2, S5_GROUPS, S5_STATE), 0.01),
        's5_lam_im': lam_im0 + nrm((DEPTH, 2, S5_GROUPS, S5_STATE), 0.01),
        's5_log_step': unif((DEPTH, 2, S5_GROUPS), math.log(1e-3), math.log(1e-1)),
        's5_b_re': nrm((DEPTH, S5_GROUPS, S5_STATE, S5_GROUP_CH), (2 * S5_GROUP_CH) ** -0.5),
        's5_b_im': nrm((DEPTH, S5_GROUPS, S5_STATE, S5_GROUP_CH), (2 * S5_GROUP_CH) ** -0.5),
        's5_c_re': nrm((DEPTH, 2, S5_GROUPS, S5_GROUP_CH, S5_STATE), (2 * S5_STATE) ** -0.5),
        's5_c_im': nrm((DEPTH, 2, S5_GROUPS, S5_GROUP_CH, S5_STATE), (2 * S5_STATE) ** -0.5),
        's5_d': nrm((DEPTH, S5_WIDTH), 1.0),
        's5_w_glu': nrm((DEPTH, S5_WIDTH, S5_WIDTH), S5_WIDTH ** -0.5),
        's5_b_glu': nrm((DEPTH, S5_WIDTH), 0.01),
        'w_out': nrm((DEPTH, D_MIX, D_MODEL), D_MIX ** -0.5 * DEEPNORM_BETA),
        'ln1_g': 1.0 + nrm((DEPTH, D_MODEL), 0.01),
        'ln1_b': nrm((DEPTH, D_MODEL), 0.01),
        'ln2_g': 1.0 + nrm((DEPTH, D_MODEL), 0.01),
        'ln2_b': nrm((DEPTH, D_MODEL), 0.01),
        'w_router': nrm((D_MODEL, N_EXPERTS), inv_sqrt_d),
        'b_router': nrm((N_EXPERTS,), 0.01),
        'w_gate': nrm((DEPTH, N_EXPERTS, D_MODEL, D_EXPERT), inv_sqrt_d),
        'w_up': nrm((DEPTH, N_EXPERTS, D_MODEL, D_EXPERT), inv_sqrt_d),
        'w_down': nrm((DEPTH, N_EXPERTS, D_EXPERT, D_MODEL), D_EXPERT ** -0.5 * DEEPNORM_BETA),
    }

def reference(x_prompt, x_sample, c_prompt, c_sample, w_ada, b_ada, w_in, conv_w, conv_b,
              ssd_a_log, ssd_dt_bias, ssd_d, ssd_norm_w, s5_lam_re, s5_lam_im, s5_log_step,
              s5_b_re, s5_b_im, s5_c_re, s5_c_im, s5_d, s5_w_glu, s5_b_glu, w_out,
              ln1_g, ln1_b, ln2_g, ln2_b, w_router, b_router, w_gate, w_up, w_down):
    weights = (w_ada, b_ada, w_in, conv_w, conv_b, ssd_a_log, ssd_dt_bias, ssd_d, ssd_norm_w,
               s5_lam_re, s5_lam_im, s5_log_step, s5_b_re, s5_b_im, s5_c_re, s5_c_im, s5_d,
               s5_w_glu, s5_b_glu, w_out, ln1_g, ln1_b, ln2_g, ln2_b, w_router, b_router,
               w_gate, w_up, w_down)
    y_prompt = _trunk(x_prompt, c_prompt, *weights)
    y_sample = _trunk(x_sample, c_sample, *weights)
    return (y_prompt, y_sample)


_drawn_inputs = setup_inputs


def setup_inputs(seed=0):
    import zlib

    import numpy as np

    out = dict(_drawn_inputs(seed))
    spreads = {}
    factors = {'b_ada': 4.687,
     'conv_b': 8.0,
     'ssd_d': 8.0,
     'ssd_norm_w': 8.0,
     's5_lam_re': 64.0,
     's5_lam_im': 59.208,
     's5_log_step': 64.0,
     's5_b_re': 64.0,
     's5_b_im': 64.0,
     's5_c_re': 64.0,
     's5_c_im': 64.0,
     's5_w_glu': 4.029,
     's5_b_glu': 30.973,
     'ln1_g': 4.376,
     'ln1_b': 4.023,
     'ln2_g': 31.165,
     'ln2_b': 34.875,
     'b_router': 7.373}
    for name, (base, spread) in spreads.items():
        noise = np.random.default_rng([zlib.crc32(name.encode()), seed]).standard_normal(out[name].shape)
        drawn = base * np.exp(spread * noise) if base else spread * noise
        out[name] = jnp.asarray(drawn.astype(out[name].dtype))
    for name, factor in factors.items():
        out[name] = (out[name] * factor).astype(out[name].dtype)
    return out
```

```python
from contextlib import ExitStack

import numpy as np

import concourse.bass as bass
from concourse import mybir

F32 = mybir.dt.float32
I32 = mybir.dt.int32
ALU = mybir.AluOpType
ACT = mybir.ActivationFunctionType
AX = mybir.AxisListType

P = 128
D = 1024
SAMPLE, PROMPT = 2048, 1024
TOK = SAMPLE + PROMPT
KT = D // P
WIDE = 512
NWIDE = TOK // WIDE
WIDE_SAMPLE = SAMPLE // WIDE
TPW = WIDE // P
NT = TOK // P
NT_SAMPLE = SAMPLE // P
EPS = 1e-5
ALPHA = 2.0 ** 0.25

SSD = 512
HEADS, HD = 8, 64
STATE = 128
CONV_CH, TAPS = 1024, 5
CT = CONV_CH // P
HALO = TAPS // 2
Z0, XBC0, DT0, U0 = 0, SSD, SSD + CONV_CH, SSD + CONV_CH + 2 * HEADS
IN_COLS = U0 + SSD
RAW_COLS = TOK + 4 * HALO

G5, CH5, N5 = 32, 16, 64
PAIRS = G5 // 2
T5 = 16
C_S, C_P = SAMPLE // T5, PROMPT // T5
C_ALL = C_S + C_P
HALF = T5 * CH5 // P
SPK = T5 // HALF

NE, NG, EPG, DE = 16, 4, 4, 512
BLK = 128
NBLK = 2 * TOK // BLK + NE
ROWS = NBLK * BLK


class Semaphores:

    def __init__(self, nc, ctx):
        self.nc, self.ctx, self.made = nc, ctx, 0
        self.free, self.used = [], []

    def __call__(self, name, pool_dma=False):
        if self.free and not pool_dma:
            s = self.free.pop()
        else:
            s = self.ctx.enter_context(self.nc.semaphore(f"count{self.made}_{name}"))
            self.made += 1
        if not pool_dma:
            self.used.append(s)
        return s

    def clear(self):
        with self.nc.Block() as block:
            @block.gpsimd
            def _(pool):
                for s in self.used:
                    pool.sem_clear(s)
        self.free += self.used[::-1]
        self.used = []


class Steps:

    def __init__(self, eng, sem, turn=None, per_turn=0, before=0):
        self.eng, self.sem, self.turn, self.per_turn, self.n, self.before = eng, sem, turn, per_turn, 0, before

    def done(self, ins):
        ins.then_inc(self.sem, 1)
        self.n += 1

    def wait(self, back=0):
        at = self.before + self.n - back
        self.eng.wait_ge(self.sem, at if self.turn is None else self.turn * self.per_turn + at)

    def then(self, ins):
        self.done(ins)
        self.wait()

    def end_turn(self):
        assert self.n == self.per_turn, (self.n, self.per_turn)


def seq_of(turn, turns_of_sample):
    return turn // turns_of_sample


def constants(nc, C, S):
    made = S("made")
    with nc.Block() as block:
        @block.gpsimd
        def _(pool):
            steps = Steps(pool, made)
            steps.done(pool.memset(C.ident[:], 0.0))
            for t in (C.le, C.ge, C.gt, C.lt, C.ones):
                steps.done(pool.memset(t[:], 1.0))
            steps.done(pool.memset(C.minus_half[:], -0.5))
            steps.wait()
            for t, sign, op, fill in ((C.ident, 1, ALU.not_equal, 1.0), (C.le, 1, ALU.is_ge, 0.0), (C.ge, -1, ALU.is_ge, 0.0),
                                      (C.gt, -1, ALU.is_gt, 0.0), (C.lt, 1, ALU.is_gt, 0.0)):
                steps.done(pool.affine_select(out=t[:], in_=t[:], compare_op=op, fill=fill, base=0, pattern=[[sign, P]],
                                              channel_multiplier=-sign))
            steps.wait()
    S.clear()


def adapt(nc, C, S, c_all, w_ada, b_ada, mod):
    PIECE = 512
    TURNS = 6 * D // PIECE // 2
    w = w_ada.rearrange("(p k) n -> p k n", p=P)
    with ExitStack() as ctx:
        sb = lambda n, s: ctx.enter_context(nc.sbuf_tensor("ada_" + n, s, F32))
        ct, cs = sb("ct", [P, 2, KT]), sb("cs", [P, KT, 2])
        wt = sb("wt", [P, 2, KT, PIECE])
        rows, bias = sb("rows", [2, 6 * D]), sb("bias", [2, 6 * D])
        acc = C.bank[0:2]
        c_in, b_in, act_c, mm, added, out = (S(n) for n in ("c_in", "b_in", "act_c", "mm", "added", "out"))
        w_in = [S(f"w_in{j}") for j in range(2)]
        with nc.Block() as block:
            @block.sync
            def _(sp):
                sp.dma_start(ct[:], c_all.rearrange("s (p k) -> p s k", p=P)).then_inc(c_in, 16)
                for s in range(2):
                    sp.dma_start(bias[s:s + 1, :], b_ada).then_inc(b_in, 16)
                for j in range(2):
                    sp.dma_start(wt[:, j], w[:, :, j * PIECE:(j + 1) * PIECE]).then_inc(w_in[j], 16)
                with sp.Fori(0, TURNS - 1) as t:
                    for j in range(2):
                        sp.wait_ge(mm, t * 2 + j + 1)
                        sp.dma_start(wt[:, j], w[:, :, bass.ds((t * 2 + j + 2) * PIECE, PIECE)]).then_inc(w_in[j], 16)
                sp.wait_ge(added, 2 * TURNS)
                sp.dma_start(mod, rows[:]).then_inc(out, 16)
                sp.wait_ge(out, 16)

            @block.scalar
            def _(act):
                act.wait_ge(c_in, 16)
                act.activation(cs[:], ct[:].rearrange("p s k -> p k s"), ACT.Silu).then_inc(act_c, 1)

            @block.tensor
            def _(pe):
                pe.wait_ge(act_c, 1)
                with pe.Fori(0, TURNS) as t:
                    for j in range(2):
                        pe.wait_ge(w_in[j], t * 16 + 16)
                        pe.wait_ge(added, t * 2)
                        for k in range(KT):
                            mul = pe.matmul(acc[j][0:2, :], cs[:, k, :], wt[:, j, k, :], start=k == 0, stop=k == KT - 1)
                        mul.then_inc(mm, 1)

            @block.vector
            def _(dve):
                dve.wait_ge(b_in, 32)
                with dve.Fori(0, TURNS) as t:
                    for j in range(2):
                        cols = bass.ds((t * 2 + j) * PIECE, PIECE)
                        dve.wait_ge(mm, t * 2 + j + 1)
                        dve.tensor_tensor(rows[:, cols], acc[j][0:2, :], bias[:, cols], ALU.add).then_inc(added, 1)
    S.clear()


def project(nc, C, S, x, mod, w_in, zs, raw, u):
    TURNS = NWIDE // 2
    SAMPLE_TURNS = WIDE_SAMPLE // 2
    RING = 4
    OUTS = CT + 2 * TPW
    with ExitStack() as ctx:
        sb = lambda n, s: ctx.enter_context(nc.sbuf_tensor("pro_" + n, s, F32))
        w = sb("w", [P, KT, IN_COLS])
        xt = sb("xt", [P, 2, TPW, D])
        ht = sb("ht", [P, 2, KT, WIDE])
        scale, shift = sb("scale", [P, 2, KT]), sb("shift", [P, 2, KT])
        zero = sb("zero", [P, CT, 2 * HALO])
        stage = sb("stage", [P, RING, WIDE])
        turned, acc, dt_acc = C.bank[0:2], C.bank[2:2 + RING], C.bank[6]
        w_here, mod_here, one_added, zeroed, padded = (S(n) for n in ("w_here", "mod_here", "one_added", "zeroed", "padded"))
        x_here = [S(f"x_here{j}", pool_dma=True) for j in range(2)]
        transposed, h_ready, product, staged, dt_mm, dt_kept = (
            S(n) for n in ("transposed", "h_ready", "product", "staged", "dt_mm", "dt_kept"))
        stored = [S(f"stored{r}") for r in range(RING)]
        wv = w_in.rearrange("(p k) n -> p k n", p=P)
        with nc.Block() as block:
            @block.gpsimd
            def _(pool):
                with pool.Fori(0, TURNS) as t:
                    for j in range(2):
                        pool.wait_ge(transposed, t * 2 * KT)
                        pool.dma_start(xt[:, j], x[bass.ds((t * 2 + j) * WIDE, WIDE), :].rearrange(
                            "(a p) n -> p a n", p=P)).then_inc(x_here[j], 16)

            @block.sync
            def _(sp):
                for kind, sc in ((1, scale), (0, shift)):
                    sp.dma_start(sc[:], mod[:, kind * D:(kind + 1) * D].rearrange("s (p k) -> p s k", p=P)).then_inc(mod_here, 16)
                sp.dma_start(w[:], wv).then_inc(w_here, 16)
                sp.wait_ge(zeroed, 1)
                rows = raw.rearrange("(c p) n -> p c n", p=P)
                for at, n in ((0, HALO), (HALO + SAMPLE, 2 * HALO), (RAW_COLS - HALO, HALO)):
                    sp.dma_start(rows[:, :, at:at + n], zero[:, :, 0:n]).then_inc(padded, 16)
                with sp.Fori(0, TURNS) as t:
                    for j in range(2):
                        m = t * 2 + j
                        col = m * WIDE + HALO + seq_of(t, SAMPLE_TURNS) * (2 * HALO)
                        for o in range(OUTS):
                            sp.wait_ge(staged, m * OUTS + o + 1)
                            r = o % RING
                            if o < CT:
                                to = raw[o * P:(o + 1) * P, bass.ds(col, WIDE)]
                            else:
                                to = (zs if o < CT + TPW else u)[bass.ds(m * WIDE + (o - CT) % TPW * P, P), :]
                            sp.dma_start(to, stage[:, r, :]).then_inc(stored[r], 16)
                sp.wait_ge(padded, 48)
                for r in range(RING):
                    sp.wait_ge(stored[r], 16 * NWIDE * OUTS // RING)

            @block.vector
            def _(dve):
                dve.memset(zero[:], 0.0).then_inc(zeroed, 1)
                dve.wait_ge(mod_here, 32)
                dve.tensor_scalar(scale[:], scale[:], 1.0, None, ALU.add).then_inc(one_added, 1)
                dve.wait_ge(one_added, 1)
                with dve.Fori(0, TURNS) as t:
                    s = seq_of(t, SAMPLE_TURNS)
                    for j in range(2):
                        m = t * 2 + j
                        dve.wait_ge(product, t * 2 * OUTS)
                        for k in range(KT):
                            dve.wait_ge(transposed, m * KT + k + 1)
                            dve.tensor_scalar(ht[:, j, k, :], turned[k % 2][:, :], scale[:, bass.ds(s, 1), k:k + 1].rearrange("p a b -> p (a b)"),
                                              shift[:, bass.ds(s, 1), k:k + 1].rearrange("p a b -> p (a b)"),
                                              ALU.mult, ALU.add).then_inc(h_ready, 1)
                        dve.wait_ge(dt_mm, m + 1)
                        dve.tensor_copy(C.dt_raw[:, bass.ds(m * TPW, TPW), :],
                                        dt_acc[:, 0:TPW * 2 * HEADS].rearrange("p (a c) -> p a c", a=TPW)).then_inc(dt_kept, 1)

            @block.tensor
            def _(pe):
                with pe.Fori(0, TURNS) as t:
                    for j in range(2):
                        m = t * 2 + j
                        pe.wait_ge(x_here[j], t * 16 + 16)
                        for k in range(KT):
                            if k >= 2:
                                pe.wait_ge(h_ready, m * KT + k - 1)
                            else:
                                pe.wait_ge(h_ready, m * KT)
                            for a in range(TPW):
                                tr = pe.transpose(turned[k % 2][:, a * P:(a + 1) * P], xt[:, j, a, k::KT], C.ident[:])
                            tr.then_inc(transposed, 1)
                        if j == 0:
                            pe.wait_ge(w_here, 16)
                        pe.wait_ge(h_ready, (m + 1) * KT)
                        pe.wait_ge(dt_kept, m)
                        for a in range(TPW):
                            for k in range(KT):
                                mul = pe.matmul(dt_acc[:, a * 2 * HEADS:(a + 1) * 2 * HEADS], ht[:, j, k, a * P:(a + 1) * P],
                                                w[:, k, DT0:DT0 + 2 * HEADS], start=k == 0, stop=k == KT - 1)
                        mul.then_inc(dt_mm, 1)
                        for o in range(OUTS):
                            if o >= RING:
                                pe.wait_ge(staged, m * OUTS + o - RING + 1)
                            else:
                                pe.wait_ge(staged, m * OUTS)
                            for k in range(KT):
                                if o < CT:
                                    left, right = w[:, k, XBC0 + o * P:XBC0 + (o + 1) * P], ht[:, j, k, :]
                                else:
                                    a = (o - CT) % TPW
                                    at = Z0 if o < CT + TPW else U0
                                    left, right = ht[:, j, k, a * P:(a + 1) * P], w[:, k, at:at + SSD]
                                mul = pe.matmul(acc[o % RING][:, :], left, right, start=k == 0, stop=k == KT - 1)
                            mul.then_inc(product, 1)

            @block.scalar
            def _(act):
                with act.Fori(0, TURNS) as t:
                    for j in range(2):
                        m = t * 2 + j
                        for o in range(OUTS):
                            r = o % RING
                            act.wait_ge(product, m * OUTS + o + 1)
                            act.wait_ge(stored[r], (m * (OUTS // RING) + o // RING) * 16)
                            act.activation(stage[:, r, :], acc[r][:, :],
                                           ACT.Silu if CT <= o < CT + TPW else ACT.Copy).then_inc(staged, 1)
    S.clear()


def convolve(nc, C, S, raw, conv_w, conv_b, xb, bc):
    TURNS = NWIDE // 2
    BY_DVE = 5
    BY_PE = CT - BY_DVE
    XB = SSD // P + 2
    with ExitStack() as ctx:
        sb = lambda n, s: ctx.enter_context(nc.sbuf_tensor("con_" + n, s, F32))
        cw, cb = sb("cw", [P, CT, TAPS]), sb("cb", [P, CT])
        diag = sb("diag", [P, BY_PE, TAPS, P])
        src = sb("src", [P, 2, CT, WIDE + 2 * HALO])
        acc = sb("acc", [P, 2, BY_DVE, WIDE])
        out = sb("out", [P, 2, CT, WIDE])
        rows = sb("rows", [P, 2, XB * P])
        sums, turned = C.bank[0:BY_PE], C.bank[4:8]
        w_here, diag_made, taps, summed, activated, transposed, rows_ready = (
            S(n) for n in ("w_here", "diag_made", "taps", "summed", "activated", "transposed", "rows_ready"))
        src_here, bc_stored, rows_stored = ([S(f"{n}{j}") for j in range(2)] for n in ("src_here", "bc_stored", "rows_stored"))
        order = [*range(BY_DVE, CT), *range(BY_DVE)]
        with nc.Block() as block:
            @block.sync
            def _(sp):
                sp.dma_start(cw[:], conv_w).then_inc(w_here, 16)
                sp.dma_start(cb[:], conv_b).then_inc(w_here, 16)
                with sp.Fori(0, TURNS) as t:
                    for j in range(2):
                        col = sp.snap((t * 2 + j) * WIDE + seq_of(t, WIDE_SAMPLE // 2) * (2 * HALO))
                        sp.wait_ge(taps, t * 2 * BY_DVE * TAPS)
                        sp.nop(nofuse=True)
                        sp.wait_ge(summed, t * 2 * BY_PE)
                        sp.nop(nofuse=True)
                        sp.dma_start(src[:, j], raw[:, bass.ds(col, WIDE + 2 * HALO)].rearrange(
                            "(c p) n -> p c n", p=P)).then_inc(src_here[j], 16)
                    for j in range(2):
                        m = t * 2 + j
                        sp.wait_ge(activated, (m + 1) * CT)
                        sp.nop(nofuse=True)
                        sp.dma_start(bc[:, :, bass.ds(m * WIDE, WIDE)].rearrange("c p n -> p c n"),
                                     out[:, j, SSD // P:CT, :]).then_inc(bc_stored[j], 16)
                        for a in range(TPW):
                            sp.wait_ge(rows_ready, m * TPW + a + 1)
                            sp.nop(nofuse=True)
                            sp.dma_start(xb[bass.ds(m * WIDE + a * P, P), :], rows[:, a % 2, :]).then_inc(rows_stored[a % 2], 16)
                for j in range(2):
                    sp.wait_ge(bc_stored[j], 16 * TURNS)
                    sp.wait_ge(rows_stored[j], 16 * NT // 2)

            @block.gpsimd
            def _(pool):
                pool.wait_ge(w_here, 32)
                for c in range(BY_PE):
                    for k in range(TAPS):
                        pool.tensor_scalar(diag[:, c, k, :], C.ident[:], cw[:, BY_DVE + c, k:k + 1], None, ALU.mult).then_inc(diag_made, 1)

            @block.vector
            def _(dve):
                dve.wait_ge(w_here, 32)
                with dve.Fori(0, TURNS) as t:
                    steps = Steps(dve, taps, t, 2 * BY_DVE * TAPS)
                    for j in range(2):
                        dve.wait_ge(src_here[j], t * 16 + 16)
                        dve.wait_ge(activated, t * 2 * CT)
                        for k in range(TAPS):
                            for c in range(BY_DVE):
                                x = src[:, j, c, k:k + WIDE]
                                if k == 0:
                                    steps.done(dve.tensor_scalar(acc[:, j, c, :], x, cw[:, c, 0:1], None, ALU.mult))
                                else:
                                    steps.wait(back=BY_DVE - 1)
                                    steps.done(dve.scalar_tensor_tensor(out=acc[:, j, c, :], in0=x, scalar=cw[:, c, k:k + 1],
                                                                        in1=acc[:, j, c, :], op0=ALU.mult, op1=ALU.add))
                    steps.end_turn()

            @block.tensor
            def _(pe):
                pe.wait_ge(diag_made, BY_PE * TAPS)
                with pe.Fori(0, TURNS) as t:
                    for j in range(2):
                        m = t * 2 + j
                        pe.wait_ge(src_here[j], t * 16 + 16)
                        pe.wait_ge(activated, m * CT)
                        for c in range(BY_PE):
                            for k in range(TAPS):
                                mul = pe.matmul(sums[c][:, :], diag[:, c, k, :], src[:, j, BY_DVE + c, k:k + WIDE],
                                                start=k == 0, stop=k == TAPS - 1)
                            mul.then_inc(summed, 1)
                        pe.wait_ge(activated, (m + 1) * CT)
                        for a in range(TPW):
                            if a >= 2:
                                pe.wait_ge(rows_ready, m * TPW + a - 1)
                            else:
                                pe.wait_ge(rows_ready, m * TPW)
                            for c in range(XB):
                                tr = pe.transpose(turned[a % 2 * 2 + c // 4][:, c % 4 * P:(c % 4 + 1) * P],
                                                  out[:, j, c, a * P:(a + 1) * P], C.ident[:])
                            tr.then_inc(transposed, 1)

            @block.scalar
            def _(act):
                act.wait_ge(w_here, 32)
                with act.Fori(0, TURNS) as t:
                    for j in range(2):
                        m = t * 2 + j
                        act.wait_ge(bc_stored[j], t * 16)
                        act.wait_ge(transposed, t * 2 * TPW)
                        for n, c in enumerate(order):
                            if c >= BY_DVE:
                                act.wait_ge(summed, m * BY_PE + c - BY_DVE + 1)
                                x = sums[c - BY_DVE][:, :]
                            else:
                                act.wait_ge(taps, m * BY_DVE * TAPS + BY_DVE * (TAPS - 1) + c + 1)
                                x = acc[:, j, c, :]
                            act.activation(out[:, j, c, :], x, ACT.Silu, bias=cb[:, c:c + 1]).then_inc(activated, 1)
                        for a in range(TPW):
                            act.wait_ge(transposed, m * TPW + a + 1)
                            act.wait_ge(rows_stored[a % 2], (m * TPW // 2 + a // 2) * 16)
                            act.activation(rows[:, a % 2, 0:4 * P], turned[a % 2 * 2][:, :], ACT.Copy)
                            act.activation(rows[:, a % 2, 4 * P:XB * P], turned[a % 2 * 2 + 1][:, 0:(XB - 4) * P],
                                           ACT.Copy).then_inc(rows_ready, 1)
    S.clear()


def decays(nc, C, S, dt_bias, a_log):
    H2 = 2 * HEADS
    with ExitStack() as ctx:
        sb = lambda n, s: ctx.enter_context(nc.sbuf_tensor("dec_" + n, s, F32))
        bias, alog, decay = sb("bias", [P, H2]), sb("alog", [P, H2]), sb("decay", [P, H2])
        v, w = sb("v", [P, NT, H2]), sb("w", [P, NT, H2])
        to_end = sb("to_end", [P, NT, H2])
        here, soft, expd, summed = (S(n) for n in ("here", "soft", "expd", "summed"))
        sums = [C.bank[n][:, 0:NT * HEADS].rearrange("p (c h) -> p c h", h=HEADS) for n in range(6)]
        fwd, bwd = slice(0, HEADS), slice(HEADS, H2)
        with nc.Block() as block:
            @block.sync
            def _(sp):
                sp.dma_start(bias[:], dt_bias.to_broadcast([P, H2])).then_inc(here, 16)
                sp.dma_start(alog[:], a_log.to_broadcast([P, H2])).then_inc(here, 16)

            @block.vector
            def _(dve):
                steps = Steps(dve, soft)
                wide = lambda t: t[:].unsqueeze(1).to_broadcast([P, NT, H2])
                dve.wait_ge(here, 32)
                steps.then(dve.tensor_tensor(v[:], C.dt_raw[:], wide(bias), ALU.add))
                steps.then(dve.tensor_scalar(w[:], v[:], -1.0, None, ALU.mult))
                steps.then(dve.tensor_tensor(w[:], w[:], v[:], ALU.min))
                dve.wait_ge(expd, 3)
                steps.then(dve.tensor_scalar(v[:], v[:], 0.0, None, ALU.max))
                steps.then(dve.tensor_tensor(C.dt[:], v[:], w[:], ALU.add))
                steps.then(dve.tensor_tensor(v[:], C.dt[:], wide(decay), ALU.mult))
                steps.then(dve.tensor_scalar(C.adt[:], v[:], -1.0, None, ALU.mult))
                dve.wait_ge(expd, 9)
                steps.done(dve.tensor_tensor(C.dt_to_end[:], C.dt[:], to_end[:], ALU.mult))

            @block.scalar
            def _(act):
                steps = Steps(act, expd)
                act.wait_ge(here, 32)
                steps.done(act.activation(decay[:], alog[:], ACT.Exp))
                act.wait_ge(soft, 3)
                steps.then(act.activation(w[:], w[:], ACT.Exp))
                steps.then(act.activation(w[:], w[:], ACT.Ln, bias=1.0))
                for n, to in enumerate((C.from_start[:, :, fwd], to_end[:, :, fwd], C.whole[:, :, fwd],
                                        C.from_start[:, :, bwd], to_end[:, :, bwd], C.whole[:, :, bwd])):
                    act.wait_ge(summed, n + 1)
                    steps.done(act.activation(to, sums[n], ACT.Exp))

            @block.tensor
            def _(pe):
                pe.wait_ge(soft, 7)
                for n, (mask, heads) in enumerate(((C.le, fwd), (C.gt, fwd), (C.ones, fwd), (C.ge, bwd), (C.lt, bwd), (C.ones, bwd))):
                    pe.matmul(sums[n], mask[:], C.adt[:, :, heads], start=True, stop=True).then_inc(summed, 1)
    S.clear()


def slot_of(chunk, turn):
    return chunk + seq_of(turn, NT_SAMPLE // 2)


def scan_back(nc, C, S, xb):
    TURNS = NT // 2
    with ExitStack() as ctx:
        sb = lambda n, s: ctx.enter_context(nc.sbuf_tensor("bac_" + n, s, F32))
        rows = sb("rows", [P, 2, SSD + 2 * STATE])
        xw, held = sb("xw", [P, 2, SSD]), sb("held", [P, SSD])
        rows_here = [S(f"rows_here{j}") for j in range(2)]
        weighted, states, carried, held_ready = (S(n) for n in ("weighted", "states", "carried", "held_ready"))
        wide = lambda t: t.rearrange("p a h -> p (a h)").unsqueeze(2).to_broadcast([P, HEADS, HD])
        by_head = lambda t: t.rearrange("p (h d) -> p h d", h=HEADS)
        back = slice(HEADS, 2 * HEADS)
        with nc.Block() as block:
            @block.sync
            def _(sp):
                with sp.Fori(0, TURNS) as t:
                    for j in range(2):
                        row = sp.snap((NT - 1 - t * 2 - j) * P)
                        sp.wait_ge(states, t * 2)
                        sp.nop(nofuse=True)
                        sp.wait_ge(weighted, t * 2)
                        sp.nop(nofuse=True)
                        sp.dma_start(rows[:, j, :], xb[bass.ds(row, P), :]).then_inc(rows_here[j], 16)

            @block.gpsimd
            def _(pool):
                with pool.Fori(0, TURNS) as t:
                    for j in range(2):
                        c = pool.snap(NT - 1 - t * 2 - j)
                        pool.wait_ge(rows_here[j], t * 16 + 16)
                        pool.nop(nofuse=True)
                        pool.wait_ge(states, t * 2)
                        pool.nop(nofuse=True)
                        pool.tensor_tensor(by_head(xw[:, j, :]), by_head(rows[:, j, 0:SSD]),
                                           wide(C.dt_to_end[:, bass.ds(c, 1), back]), ALU.mult).then_inc(weighted, 1)

            @block.tensor
            def _(pe):
                with pe.Fori(0, TURNS) as t:
                    for j in range(2):
                        pe.wait_ge(weighted, t * 2 + j + 1)
                        pe.wait_ge(carried, t * 2)
                        for g in range(2):
                            mul = pe.matmul(C.bank[j][:, g * 256:(g + 1) * 256], rows[:, j, SSD + g * STATE:SSD + (g + 1) * STATE],
                                            xw[:, j, g * 256:(g + 1) * 256], start=True, stop=True)
                        mul.then_inc(states, 1)

            @block.vector
            def _(dve):
                dve.memset(C.h_back[:, bass.ds(NT_SAMPLE, 1), :], 0.0).then_inc(held_ready, 1)
                dve.memset(C.h_back[:, bass.ds(NT + 1, 1), :], 0.0).then_inc(held_ready, 1)
                dve.wait_ge(held_ready, 2)
                with dve.Fori(0, TURNS) as t:
                    for j in range(2):
                        m = t * 2 + j
                        c = dve.snap(NT - 1 - m)
                        slot = dve.snap(c + seq_of(TURNS - 1 - t, NT_SAMPLE // 2))
                        dve.wait_ge(carried, m)
                        dve.nop(nofuse=True)
                        dve.tensor_tensor(by_head(held[:]), by_head(C.h_back[:, bass.ds(slot + 1, 1), :].rearrange("p a n -> p (a n)")),
                                          wide(C.whole[:, bass.ds(c, 1), back]), ALU.mult).then_inc(held_ready, 1)
                        dve.wait_ge(held_ready, m + 3)
                        dve.wait_ge(states, m + 1)
                        dve.nop(nofuse=True)
                        dve.tensor_tensor(C.h_back[:, bass.ds(slot, 1), :].rearrange("p a n -> p (a n)"), held[:], C.bank[j][:, :],
                                          ALU.add).then_inc(carried, 1)
    S.clear()


def scan_forward(nc, C, S, xb, bc, zs, d_skip, y_ssd):
    TURNS = NT // 2
    H4 = HEADS // 2 * P
    with ExitStack() as ctx:
        sb = lambda n, s: ctx.enter_context(nc.sbuf_tensor("fwd_" + n, s, F32))
        h_fore = sb("h_fore", [P, NT + 2, SSD])
        rows, chan, z = sb("rows", [P, 2, SSD + 2 * STATE]), sb("chan", [P, 2, 4, P]), sb("z", [P, 2, SSD])
        sums_f, sums_b = sb("sums_f", [P, HEADS, P]), sb("sums_b", [P, HEADS, P])
        decay, mix = sb("decay", [P, HEADS, P]), sb("mix", [P, 2, HEADS, P])
        weight, weight_b = sb("weight", [P, HEADS, P]), sb("weight_b", [P, HEADS, P])
        xw, skip, held = sb("xw", [P, 2, SSD]), sb("skip", [P, SSD]), sb("held", [P, SSD])
        y, t1, t2 = sb("y", [P, 2, SSD]), sb("t1", [P, SSD]), sb("t2", [P, SSD])
        square, total, root = sb("square", [P, SSD]), sb("total", [P, 2]), sb("root", [P, 2])
        d = sb("d", [P, HEADS])
        cb, seg, self_y, fore_y, back_y, states = (C.bank[0], C.bank[1:3], C.bank[3], C.bank[4], C.bank[5], C.bank[6:8])
        d_here, cleared, masked, weighted, expd, skipped, xw_ready, rooted, squared = (
            S(n) for n in ("d_here", "cleared", "masked", "weighted", "expd", "skipped", "xw_ready", "rooted", "squared"))
        cb_mm, seg_mm, self_mm, off_mm, states_mm, dve_steps = (
            S(n) for n in ("cb_mm", "seg_mm", "self_mm", "off_mm", "states_mm", "dve_steps"))
        rows_here, chan_here, z_here, stored = ([S(f"{n}{j}") for j in range(2)] for n in ("rows_here", "chan_here", "z_here", "stored"))
        by_head = lambda t: t.rearrange("p (h d) -> p h d", h=HEADS)
        wide = lambda t, n: t.rearrange("p a h -> p (a h)").unsqueeze(2).to_broadcast([P, HEADS, n])
        tri = lambda t: t[:].unsqueeze(1).to_broadcast([P, HEADS, P])
        fwd, bwd = slice(0, HEADS), slice(HEADS, 2 * HEADS)
        W_F, W_B, W_SUM, MIX0, MIX, T1, T2, Y1, Y2, Y3, Y4, HELD, STATE_NEXT, NORMED = range(1, 15)
        PER = NORMED
        with nc.Block() as block:
            @block.sync
            def _(sp):
                sp.dma_start(d[:], d_skip.to_broadcast([P, HEADS])).then_inc(d_here, 16)
                with sp.Fori(0, TURNS) as t:
                    for j in range(2):
                        m = t * 2 + j
                        sp.wait_ge(dve_steps, t * 2 * PER)
                        sp.nop(nofuse=True)
                        sp.wait_ge(skipped, t * 2)
                        sp.nop(nofuse=True)
                        sp.wait_ge(xw_ready, t * 2)
                        sp.nop(nofuse=True)
                        sp.wait_ge(states_mm, t * 2)
                        sp.nop(nofuse=True)
                        sp.dma_start(rows[:, j, :], xb[bass.ds(m * P, P), :]).then_inc(rows_here[j], 16)
                        sp.dma_start(chan[:, j], bc[:, :, bass.ds(m * P, P)].rearrange("c p n -> p c n")).then_inc(chan_here[j], 16)
                        sp.dma_start(z[:, j, :], zs[bass.ds(m * P, P), :]).then_inc(z_here[j], 16)
                    for j in range(2):
                        m = t * 2 + j
                        sp.wait_ge(dve_steps, (m + 1) * PER)
                        sp.nop(nofuse=True)
                        sp.dma_start(y_ssd[bass.ds(m * P, P), :], y[:, j, :]).then_inc(stored[j], 16)
                for j in range(2):
                    sp.wait_ge(stored[j], 16 * TURNS)

            @block.gpsimd
            def _(pool):
                pool.wait_ge(d_here, 16)
                with pool.Fori(0, TURNS) as t:
                    for j in range(2):
                        m = pool.snap(t * 2 + j)
                        pool.wait_ge(seg_mm, m)
                        pool.nop(nofuse=True)
                        pool.tensor_tensor(sums_f[:], tri(C.le), wide(C.adt[:, bass.ds(m, 1), fwd], P), ALU.mult).then_inc(masked, 1)
                        pool.tensor_tensor(sums_b[:], tri(C.ge), wide(C.adt[:, bass.ds(m, 1), bwd], P), ALU.mult).then_inc(masked, 1)
                        pool.wait_ge(rows_here[j], t * 16 + 16)
                        pool.nop(nofuse=True)
                        pool.wait_ge(states_mm, t * 2)
                        pool.nop(nofuse=True)
                        pool.tensor_tensor(by_head(xw[:, j, :]), by_head(rows[:, j, 0:SSD]),
                                           wide(C.dt_to_end[:, bass.ds(m, 1), fwd], HD), ALU.mult).then_inc(xw_ready, 1)
                        pool.wait_ge(dve_steps, m * PER)
                        pool.tensor_tensor(by_head(skip[:]), by_head(rows[:, j, 0:SSD]),
                                           d[:].unsqueeze(2).to_broadcast([P, HEADS, HD]), ALU.mult).then_inc(skipped, 1)
                        pool.wait_ge(squared, m + 1)
                        pool.nop(nofuse=True)
                        pool.tensor_scalar(root[:, j:j + 1], total[:, j:j + 1], 1.0 / SSD, EPS, ALU.mult, ALU.add).then_inc(rooted, 1)
                        pool.wait_ge(rooted, m * 2 + 1)
                        pool.tensor_tensor(root[:, j:j + 1], root[:, j:j + 1], C.minus_half[:], ALU.pow).then_inc(rooted, 1)

            @block.tensor
            def _(pe):
                with pe.Fori(0, TURNS) as t:
                    for j in range(2):
                        m = t * 2 + j
                        pe.wait_ge(chan_here[j], t * 16 + 16)
                        pe.wait_ge(dve_steps, m * PER)
                        for g in range(2):
                            mul = pe.matmul(cb[:, g * P:(g + 1) * P], chan[:, j, g, :], chan[:, j, 2 + g, :], start=True, stop=True)
                        mul.then_inc(cb_mm, 1)
                        pe.wait_ge(expd, m * 2)
                        pe.wait_ge(masked, m * 2 + 2)
                        for q in range(2):
                            heads = slice(q * 4, q * 4 + 4)
                            pe.matmul(seg[q][:, :], C.gt[:], sums_f[:, heads, :], start=True, stop=False)
                            mul = pe.matmul(seg[q][:, :], C.lt[:], sums_b[:, heads, :], start=False, stop=True)
                        mul.then_inc(seg_mm, 1)
                        pe.wait_ge(xw_ready, m + 1)
                        for g in range(2):
                            mul = pe.matmul(states[j][:, g * 256:(g + 1) * 256], rows[:, j, SSD + g * STATE:SSD + (g + 1) * STATE],
                                            xw[:, j, g * 256:(g + 1) * 256], start=True, stop=True)
                        mul.then_inc(states_mm, 1)
                        pe.wait_ge(cleared, 2)
                        pe.wait_ge(dve_steps, m * PER)
                        pe.nop(nofuse=True)
                        for g in range(2):
                            mul = pe.matmul(back_y[:, g * 256:(g + 1) * 256], chan[:, j, 2 + g, :],
                                            C.h_back[:, bass.ds(slot_of(m, t) + 1, 1), g * 256:(g + 1) * 256].rearrange("p a n -> p (a n)"),
                                            start=True, stop=True)
                        for g in range(2):
                            mul = pe.matmul(fore_y[:, g * 256:(g + 1) * 256], chan[:, j, 2 + g, :],
                                            h_fore[:, bass.ds(slot_of(m, t), 1), g * 256:(g + 1) * 256].rearrange("p a n -> p (a n)"),
                                            start=True, stop=True)
                        mul.then_inc(off_mm, 1)
                        pe.wait_ge(dve_steps, m * PER + MIX)
                        for h in range(HEADS):
                            mul = pe.matmul(self_y[:, h * HD:(h + 1) * HD], mix[:, j, h, :], rows[:, j, h * HD:(h + 1) * HD],
                                            start=True, stop=True)
                        mul.then_inc(self_mm, 1)

            @block.scalar
            def _(act):
                with act.Fori(0, TURNS) as t:
                    for j in range(2):
                        m = t * 2 + j
                        act.wait_ge(seg_mm, m + 1)
                        act.wait_ge(dve_steps, m * PER)
                        for q in range(2):
                            act.activation(decay[:, q * 4:q * 4 + 4, :], seg[q][:, :].rearrange("p (h n) -> p h n", h=4),
                                           ACT.Exp).then_inc(expd, 1)
                        act.wait_ge(dve_steps, m * PER + Y4)
                        act.activation(square[:], y[:, j, :], ACT.Square, accum_out=total[:, j:j + 1]).then_inc(squared, 1)

            @block.vector
            def _(dve):
                dve.memset(h_fore[:, 0, :], 0.0).then_inc(cleared, 1)
                dve.memset(h_fore[:, NT_SAMPLE + 1, :], 0.0).then_inc(cleared, 1)
                dve.wait_ge(cleared, 2)
                with dve.Fori(0, TURNS) as t:
                    steps = Steps(dve, dve_steps, t, 2 * PER)
                    for j in range(2):
                        m = dve.snap(t * 2 + j)
                        one, slot = bass.ds(m, 1), dve.snap(slot_of(m, t))
                        steps.done(dve.tensor_tensor(weight[:], tri(C.le), wide(C.dt[:, one, fwd], P), ALU.mult))
                        steps.then(dve.tensor_tensor(weight_b[:], tri(C.ge), wide(C.dt[:, one, bwd], P), ALU.mult))
                        steps.then(dve.tensor_tensor(weight[:], weight[:], weight_b[:], ALU.add))
                        dve.wait_ge(expd, t * 4 + 2 * j + 2)
                        steps.then(dve.tensor_tensor(decay[:], decay[:], weight[:], ALU.mult))
                        dve.wait_ge(cb_mm, t * 2 + j + 1)
                        steps.done(dve.tensor_tensor(
                            mix[:, j].rearrange("p (g r) n -> p g r n", g=2), decay[:].rearrange("p (g r) n -> p g r n", g=2),
                            cb[:, 0:2 * P].rearrange("p (g n) -> p g n", g=2).unsqueeze(2).to_broadcast([P, 2, HEADS // 2, P]), ALU.mult))
                        dve.wait_ge(off_mm, t * 2 + j + 1)
                        dve.nop(nofuse=True)
                        steps.done(dve.tensor_tensor(by_head(t1[:]), by_head(fore_y[:, :]), wide(C.from_start[:, one, fwd], HD), ALU.mult))
                        steps.then(dve.tensor_tensor(by_head(t2[:]), by_head(back_y[:, :]), wide(C.from_start[:, one, bwd], HD), ALU.mult))
                        dve.wait_ge(skipped, t * 2 + j + 1)
                        dve.wait_ge(stored[j], t * 16)
                        steps.then(dve.tensor_tensor(y[:, j, :], t1[:], t2[:], ALU.add))
                        steps.then(dve.tensor_tensor(y[:, j, :], y[:, j, :], skip[:], ALU.add))
                        dve.wait_ge(self_mm, t * 2 + j + 1)
                        steps.then(dve.tensor_tensor(y[:, j, :], y[:, j, :], self_y[:, :], ALU.add))
                        dve.wait_ge(z_here[j], t * 16 + 16)
                        steps.done(dve.tensor_tensor(y[:, j, :], y[:, j, :], z[:, j, :], ALU.mult))
                        steps.then(dve.tensor_tensor(by_head(held[:]), by_head(h_fore[:, bass.ds(slot, 1), :].rearrange("p a n -> p (a n)")),
                                                     wide(C.whole[:, one, fwd], HD), ALU.mult))
                        dve.wait_ge(states_mm, t * 2 + j + 1)
                        dve.nop(nofuse=True)
                        steps.done(dve.tensor_tensor(h_fore[:, bass.ds(slot + 1, 1), :].rearrange("p a n -> p (a n)"), held[:],
                                                     states[j][:, :], ALU.add))
                        dve.wait_ge(rooted, t * 4 + 2 * j + 2)
                        steps.done(dve.tensor_scalar(y[:, j, :], y[:, j, :], root[:, j:j + 1], None, ALU.mult))
                    steps.end_turn()
    S.clear()


def s5_tables(nc, C, S, lam_re, lam_im, log_step, b_re, b_im, d_skip):
    PD = PAIRS * 2
    with ExitStack() as ctx:
        sb = lambda n, s, dt=F32: ctx.enter_context(nc.sbuf_tensor("tab_" + n, s, dt))
        lr, li, ls = sb("lr", [P, PD]), sb("li", [P, PD]), sb("ls", [P, PD])
        b = [sb(f"b{n}", [P, PAIRS, CH5]) for n in range(2)]
        v = {n: sb(n, [P, PD]) for n in ("x", "k", "r", "p", "q", "step", "mag", "sin", "cos", "f", "g", "fr", "fi")}
        whole = sb("whole", [P, PD], I32)
        bit = sb("bit", [P, PD], I32)
        power = [sb(f"power{n}", [P, T5 + 1, PD]) for n in range(2)]
        t1, t2 = sb("t1", [P, 8, PD]), sb("t2", [P, 8, PD])
        u1, u2 = sb("u1", [P, PAIRS, 2, CH5]), sb("u2", [P, PAIRS, 2, CH5])
        d5 = ctx.enter_context(nc.sbuf_tensor("tab_d5", [CH5, SSD], F32))
        here, done = S("here"), S("done")
        with nc.Block() as block:
            @block.sync
            def _(sp):
                for to, a in ((lr, lam_re), (li, lam_im), (b[0], b_re), (b[1], b_im)):
                    sp.dma_start(to[:], a).then_inc(here, 16)
                for g in range(2):
                    sp.dma_start(ls[g * N5:(g + 1) * N5, :], log_step[g:g + 1, :].to_broadcast([N5, PD])).then_inc(here, 16)
                sp.dma_start(d5[:], d_skip.to_broadcast([CH5, SSD])).then_inc(here, 16)

            @block.vector
            def _(dve):
                steps = Steps(dve, done)
                ts = lambda o, a, s1, op0, s2=None, op1=ALU.bypass: steps.then(dve.tensor_scalar(o, a, s1, s2, op0, op1))
                tt = lambda o, a, c, op: steps.then(dve.tensor_tensor(o, a, c, op))
                stt = lambda o, a, s, c, op0, op1: steps.then(
                    dve.scalar_tensor_tensor(out=o, in0=a, scalar=s, in1=c, op0=op0, op1=op1))
                A = {n: t[:] for n, t in v.items()}
                ROUND = 12582912.0

                def exp(out, x):
                    ts(A["x"], x, -87.0, ALU.max, 88.0, ALU.min)
                    ts(A["k"], A["x"], 1.44269504, ALU.mult, ROUND, ALU.add)
                    ts(A["k"], A["k"], -ROUND, ALU.add)
                    stt(A["r"], A["k"], -0.693359375, A["x"], ALU.mult, ALU.add)
                    stt(A["r"], A["k"], 2.12194440e-4, A["r"], ALU.mult, ALU.add)
                    ts(A["p"], A["r"], 1.9875691500e-4, ALU.mult)
                    for c in (1.3981999507e-3, 8.3334519073e-3, 4.1665795894e-2, 1.6666665459e-1, 5.0000001201e-1):
                        stt(A["p"], A["p"], c, A["r"], ALU.add, ALU.mult)
                    tt(A["p"], A["p"], A["r"], ALU.mult)
                    tt(A["p"], A["p"], A["r"], ALU.add)
                    ts(A["p"], A["p"], 1.0, ALU.add)
                    ts(A["k"], A["k"], 127.0, ALU.add)
                    steps.then(dve.tensor_copy(whole[:], A["k"]))
                    ts(whole[:], whole[:], 23, ALU.logical_shift_left)
                    tt(out, A["p"], whole[:].bitcast(F32), ALU.mult)

                dve.wait_ge(here, 16 * 7)
                tt(C.d5_diag[:], d5[:].rearrange("p (g i) -> p g i", i=CH5),
                   C.ident[0:CH5, 0:CH5].unsqueeze(1).to_broadcast([CH5, G5, CH5]), ALU.mult)
                ts(lr[:], lr[:], -1e-4, ALU.min)
                exp(A["step"], ls[:])
                tt(A["q"], lr[:], A["step"], ALU.mult)
                exp(A["mag"], A["q"])
                tt(A["x"], li[:], A["step"], ALU.mult)
                ts(A["k"], A["x"], 0.63661977, ALU.mult, ROUND, ALU.add)
                ts(A["k"], A["k"], -ROUND, ALU.add)
                stt(A["r"], A["k"], -1.5703125, A["x"], ALU.mult, ALU.add)
                stt(A["r"], A["k"], -4.837512969970703e-4, A["r"], ALU.mult, ALU.add)
                stt(A["r"], A["k"], -7.549789948768648e-8, A["r"], ALU.mult, ALU.add)
                tt(A["q"], A["r"], A["r"], ALU.mult)
                ts(A["p"], A["q"], -1.9515295891e-4, ALU.mult, 8.3321608736e-3, ALU.add)
                tt(A["p"], A["p"], A["q"], ALU.mult)
                stt(A["p"], A["p"], -1.6666654611e-1, A["q"], ALU.add, ALU.mult)
                tt(A["p"], A["p"], A["r"], ALU.mult)
                tt(A["sin"], A["p"], A["r"], ALU.add)
                ts(A["p"], A["q"], 2.443315711809948e-5, ALU.mult, -1.388731625493765e-3, ALU.add)
                tt(A["p"], A["p"], A["q"], ALU.mult)
                stt(A["p"], A["p"], 4.166664568298827e-2, A["q"], ALU.add, ALU.mult)
                tt(A["p"], A["p"], A["q"], ALU.mult)
                stt(A["p"], A["q"], -0.5, A["p"], ALU.mult, ALU.add)
                ts(A["cos"], A["p"], 1.0, ALU.add)
                steps.then(dve.tensor_copy(whole[:], A["k"]))
                ts(bit[:], whole[:], 1, ALU.bitwise_and)
                steps.then(dve.tensor_copy(A["f"], bit[:]))
                ts(A["g"], A["f"], -1.0, ALU.mult, 1.0, ALU.add)
                tt(A["x"], A["sin"], A["g"], ALU.mult)
                tt(A["p"], A["cos"], A["f"], ALU.mult)
                tt(A["x"], A["x"], A["p"], ALU.add)
                tt(A["p"], A["cos"], A["g"], ALU.mult)
                tt(A["q"], A["sin"], A["f"], ALU.mult)
                tt(A["p"], A["p"], A["q"], ALU.add)
                for of, out, by_k in ((A["x"], A["sin"], 0.0), (A["p"], A["cos"], 1.0)):
                    ts(A["r"], A["k"], by_k, ALU.add)
                    steps.then(dve.tensor_copy(whole[:], A["r"]))
                    ts(bit[:], whole[:], 2, ALU.bitwise_and)
                    steps.then(dve.tensor_copy(A["f"], bit[:]))
                    ts(A["f"], A["f"], -1.0, ALU.mult, 1.0, ALU.add)
                    tt(A["f"], A["f"], A["mag"], ALU.mult)
                    tt(out, of, A["f"], ALU.mult)
                ts(power[0][:, 0, :], A["cos"], 0.0, ALU.mult, 1.0, ALU.add)
                ts(power[1][:, 0, :], A["cos"], 0.0, ALU.mult)
                steps.then(dve.tensor_copy(power[0][:, 1, :], A["cos"]))
                steps.then(dve.tensor_copy(power[1][:, 1, :], A["sin"]))
                n = 1
                while n < T5:
                    by = [power[c][:, n:n + 1, :].to_broadcast([P, n, PD]) for c in range(2)]
                    x = [power[c][:, 1:n + 1, :] for c in range(2)]
                    for out, op, pairs in ((0, ALU.subtract, ((0, 0), (1, 1))), (1, ALU.add, ((0, 1), (1, 0)))):
                        for t, (p, q) in zip((t1, t2), pairs):
                            tt(t[:, 0:n, :], x[p], by[q], ALU.mult)
                        tt(power[out][:, n + 1:2 * n + 1, :], t1[:, 0:n, :], t2[:, 0:n, :], op)
                    n *= 2
                for c in range(2):
                    w = power[c][:].rearrange("p q (a d) -> p a d q", d=2)
                    steps.then(dve.tensor_copy(C.power_w[c][:, :, 0, :], w[:, :, 0, 0:T5]))
                    steps.then(dve.tensor_copy(C.power_w[c][:, :, 1, :], w[:, :, 1, T5 - 1::-1]))
                    steps.then(dve.tensor_copy(C.power_y[c][:, :, 0, :], w[:, :, 0, :]))
                    steps.then(dve.tensor_copy(C.power_y[c][:, :, 1, :], w[:, :, 1, ::-1]))
                    steps.then(dve.tensor_copy(C.carry_re[:, c, :], power[0][:, T5, :]))
                ts(C.carry_im[:, 0, :], power[1][:, T5, :], -1.0, ALU.mult)
                steps.then(dve.tensor_copy(C.carry_im[:, 1, :], power[1][:, T5, :]))
                ts(A["cos"], A["cos"], -1.0, ALU.add)
                tt(A["x"], lr[:], lr[:], ALU.mult)
                tt(A["p"], li[:], li[:], ALU.mult)
                tt(A["x"], A["x"], A["p"], ALU.add)
                steps.then(dve.reciprocal(A["x"], A["x"]))
                for out, op, (p, q) in (("fr", ALU.add, (("cos", lr), ("sin", li))), ("fi", ALU.subtract, (("sin", lr), ("cos", li)))):
                    tt(A["q"], A[p[0]], p[1][:], ALU.mult)
                    tt(A["p"], A[q[0]], q[1][:], ALU.mult)
                    tt(A["q"], A["q"], A["p"], op)
                    tt(A[out], A["q"], A["x"], ALU.mult)
                f = [A[n].rearrange("p (a d) -> p a d", d=2).unsqueeze(3).to_broadcast([P, PAIRS, 2, CH5]) for n in ("fr", "fi")]
                bb = [t[:].unsqueeze(2).to_broadcast([P, PAIRS, 2, CH5]) for t in b]
                for out, op, (p, q) in ((0, ALU.subtract, ((0, 0), (1, 1))), (1, ALU.add, ((0, 1), (1, 0)))):
                    tt(u1[:], f[p[0]], bb[p[1]], ALU.mult)
                    tt(u2[:], f[q[0]], bb[q[1]], ALU.mult)
                    tt(C.b_bar[:, :, out], u1[:], u2[:], op)
    S.clear()


def s5_states_in(nc, C, S, u, turned_dram):
    TURNS = PAIRS // 2
    BOTH = 2 * T5 * CH5
    with ExitStack() as ctx:
        sb = lambda n, s: ctx.enter_context(nc.sbuf_tensor("sin_" + n, s, F32))
        us, up = sb("us", [C_S, T5, SSD]), sb("up", [C_P, T5, SSD])
        ps, pp = sb("ps", [C_S, 2, BOTH]), sb("pp", [C_P, 2, BOTH])
        ut = sb("ut", [P, 2, 2, HALF, C_ALL])
        pre = sb("pre", [P, 2, 2, 2, T5 * CH5])
        w = sb("w", [P, 2, 2, HALF, 2, P])
        t1, t2 = sb("t1", [P, 2, T5 * CH5]), sb("t2", [P, 2, T5 * CH5])
        u_here, picked_s, picked_p, made, dve_made, turned, ut_ready, turned_w, w_ready, added, read_out = (
            S(n) for n in ("u_here", "picked_s", "picked_p", "made", "dve_made", "turned", "ut_ready", "turned_w", "w_ready", "added", "read_out"))
        stored = [S(f"stored{j}") for j in range(2)]
        PRE = 6
        ub, wb, xb_ = C.bank[0:2], C.bank[2:4], C.bank[4:6]
        with nc.Block() as block:
            @block.sync
            def _(sp):
                sp.dma_start(us[:], u[0:SAMPLE, :].rearrange("(c t) n -> c t n", t=T5)).then_inc(u_here, 16)
                sp.dma_start(up[:], u[SAMPLE:TOK, :].rearrange("(c t) n -> c t n", t=T5)).then_inc(u_here, 16)
                with sp.Fori(0, TURNS) as t:
                    for j in range(2):
                        sp.wait_ge(ut_ready, t * 4 + j * 2 + 2)
                        sp.nop(nofuse=True)
                        sp.dma_start(turned_dram[bass.ds(t * 2 + j, 1)].rearrange("a p n -> p (a n)"),
                                     ut[:, j].rearrange("p g k c -> p (g k c)")).then_inc(stored[j], 16)
                for j in range(2):
                    sp.wait_ge(stored[j], 16 * TURNS)

            @block.gpsimd
            def _(pool):
                pool.wait_ge(u_here, 32)
                with pool.Fori(0, TURNS) as t:
                    for j in range(2):
                        a = pool.snap((t * 2 + j) * 2 * CH5)
                        pool.wait_ge(turned, t * 2)
                        pool.nop(nofuse=True)
                        for g in range(2):
                            put = pool.tensor_copy(pp[:, j, g * T5 * CH5:(g + 1) * T5 * CH5].rearrange("p (t i) -> p t i", i=CH5)[:, ::-1],
                                                   up[:, :, bass.ds(a + g * CH5, CH5)])
                        put.then_inc(picked_p, 1)

            @block.vector
            def _(dve):
                dve.wait_ge(u_here, 32)
                with dve.Fori(0, TURNS) as t:
                    steps = Steps(dve, dve_made, t, 2 * PRE)
                    for j in range(2):
                        n = dve.snap(t * 2 + j)
                        a = dve.snap(n * 2 * CH5)
                        dve.wait_ge(turned, t * 2)
                        dve.nop(nofuse=True)
                        for g in range(2):
                            put = dve.tensor_copy(ps[:, j, g * T5 * CH5:(g + 1) * T5 * CH5].rearrange("p (t i) -> p t i", i=CH5)[:, ::-1],
                                                  us[:, :, bass.ds(a + g * CH5, CH5)])
                        put.then_inc(picked_s, 1)
                        dve.wait_ge(turned_w, t * 2)
                        dve.nop(nofuse=True)
                        power = [C.power_w[c][:, bass.ds(n, 1)].rearrange("p a d t -> p (a d) t").unsqueeze(3).to_broadcast([P, 2, T5, CH5]) for c in range(2)]
                        b = [C.b_bar[:, bass.ds(n, 1), c].rearrange("p a d i -> p (a d) i").unsqueeze(2).to_broadcast([P, 2, T5, CH5]) for c in range(2)]
                        four = lambda x: x.rearrange("p d (t i) -> p d t i", i=CH5)
                        for out, op, (p, q) in ((0, ALU.subtract, ((0, 0), (1, 1))), (1, ALU.add, ((0, 1), (1, 0)))):
                            steps.done(dve.tensor_tensor(four(t1[:]), power[p[0]], b[p[1]], ALU.mult))
                            steps.then(dve.tensor_tensor(four(t2[:]), power[q[0]], b[q[1]], ALU.mult))
                            steps.then(dve.tensor_tensor(pre[:, j, out], t1[:], t2[:], op))
                        dve.wait_ge(added, t * 2 + j + 1)
                        dve.nop(nofuse=True)
                        for d in range(2):
                            way = slice(None, None, -1) if d else slice(None)
                            x = xb_[d][:, 0:2 * C_ALL].rearrange("p (r c) -> p c r", r=2)
                            to = C.states[:, :, :, :, bass.ds(n * 2 + d, 1)].rearrange("p k r s a -> p k r (s a)")
                            dve.tensor_copy(to[:, 0:C_S, :, 0], x[:, 0:C_S, :][:, way, :])
                            put = dve.tensor_copy(to[:, 0:C_P, :, 1], x[:, C_S:C_ALL, :][:, way, :])
                        put.then_inc(read_out, 1)
                    steps.end_turn()

            @block.tensor
            def _(pe):
                with pe.Fori(0, TURNS) as t:
                    for j in range(2):
                        m = t * 2 + j
                        pe.wait_ge(picked_s, m + 1)
                        pe.wait_ge(picked_p, m + 1)
                        pe.wait_ge(ut_ready, m * 2)
                        for g in range(2):
                            for k in range(HALF):
                                n = g * HALF + k
                                pe.transpose(ub[0][:, n * C_S:(n + 1) * C_S], ps[:, j, n * P:(n + 1) * P], C.ident[0:C_S, 0:C_S])
                                tr = pe.transpose(ub[1][:, n * C_P:(n + 1) * C_P], pp[:, j, n * P:(n + 1) * P], C.ident[0:C_P, 0:C_P])
                        tr.then_inc(turned, 1)
                        pe.wait_ge(dve_made, (m + 1) * PRE)
                        pe.wait_ge(w_ready, m * 2)
                        for r in range(2):
                            for k in range(HALF):
                                for d in range(2):
                                    n = k * 2 + d
                                    tr = pe.transpose(wb[r][:, n * P:(n + 1) * P], pre[:, j, r, d, k * P:(k + 1) * P], C.ident[:])
                        tr.then_inc(turned_w, 1)
                        pe.wait_ge(ut_ready, m * 2 + 2)
                        pe.wait_ge(w_ready, m * 2 + 2)
                        pe.wait_ge(read_out, m)
                        for d in range(2):
                            for r in range(2):
                                for g in range(2):
                                    for k in range(HALF):
                                        mul = pe.matmul(xb_[d][g * N5:(g + 1) * N5, r * C_ALL:(r + 1) * C_ALL],
                                                        w[:, j, r, k, d, g * N5:(g + 1) * N5], ut[:, j, g, k, :],
                                                        start=k == 0, stop=k == HALF - 1)
                        mul.then_inc(added, 1)

            @block.scalar
            def _(act):
                with act.Fori(0, TURNS) as t:
                    for j in range(2):
                        m = t * 2 + j
                        act.wait_ge(turned, m + 1)
                        act.wait_ge(stored[j], t * 16)
                        act.wait_ge(added, t * 2)
                        for s, (at, n) in enumerate(((0, C_S), (C_S, C_P))):
                            act.activation(ut[:, j, :, :, at:at + n].rearrange("p g k c -> p (g k) c"),
                                           ub[s][:, 0:4 * n].rearrange("p (a c) -> p a c", c=n), ACT.Copy).then_inc(ut_ready, 1)
                        act.wait_ge(turned_w, m + 1)
                        for r in range(2):
                            act.activation(w[:, j, r].rearrange("p k d n -> p (k d n)"), wb[r][:, :], ACT.Copy).then_inc(w_ready, 1)
    S.clear()


def s5_carry(nc, C, S):
    PD = PAIRS * 2
    with ExitStack() as ctx:
        sb = lambda n, s: ctx.enter_context(nc.sbuf_tensor("car_" + n, s, F32))
        t1, t2 = sb("t1", [P, 2, 2, PD]), sb("t2", [P, 2, 2, PD])
        done = S("done")
        with nc.Block() as block:
            @block.vector
            def _(dve):
                before = 0
                for lo, hi, seqs in ((1, C_P, 2), (C_P, C_S, 1)):
                    by = lambda t: t[:].unsqueeze(2).to_broadcast([P, 2, seqs, PD])
                    with dve.Fori(lo, hi) as k:
                        steps = Steps(dve, done, k - lo, 4, before)
                        at = lambda n: C.states[:, bass.ds(n, 1), :, 0:seqs, :].rearrange("p k r s n -> p (k r) s n")
                        last, here = at(k - 1), at(k)
                        steps.done(dve.tensor_tensor(t1[:, :, 0:seqs, :], by(C.carry_re), last, ALU.mult))
                        steps.then(dve.tensor_tensor(t2[:, ::-1, 0:seqs, :], by(C.carry_im)[:, ::-1], last, ALU.mult))
                        steps.then(dve.tensor_tensor(t1[:, :, 0:seqs, :], t1[:, :, 0:seqs, :], t2[:, :, 0:seqs, :], ALU.add))
                        steps.then(dve.tensor_tensor(here, here, t1[:, :, 0:seqs, :], ALU.add))
                        steps.end_turn()
                    before += 4 * (hi - lo)
    S.clear()


def s5_outputs(nc, C, S, turned_dram, kernels, c_re, c_im, yg):
    TURNS = PAIRS // 2
    Q = T5 + 1
    TC = T5 * CH5
    LAGS = 2 * T5 - 1
    with ExitStack() as ctx:
        sb = lambda n, s: ctx.enter_context(nc.sbuf_tensor("out5_" + n, s, F32))
        c = [sb(f"c{n}", [P, PAIRS, 2, CH5]) for n in range(2)]
        e = sb("e", [P, 2, 2, 2, 2, Q * CH5])
        t1, t2 = sb("t1", [P, 2, Q * CH5]), sb("t2", [P, 2, Q * CH5])
        bs = sb("bs", [P, 2, 2, 2, CH5])
        lags = sb("lags", [CH5, 2, 2, LAGS * CH5])
        toe = sb("toe", [P, 2, 2, HALF, TC])
        ut = sb("ut", [P, 2, 2, HALF, C_ALL])
        st = sb("st", [P, 2, 2, 2, C_ALL])
        ys, yp = sb("ys", [C_S, T5, SSD]), sb("yp", [C_P, T5, SSD])
        c_here, dve_made, b_picked, zeroed, entered, kernel_mm, lag_steps, y_mm, gelued, out = (
            S(n) for n in ("c_here", "dve_made", "b_picked", "zeroed", "entered", "kernel_mm", "lag_steps", "y_mm", "gelued", "out"))
        lags_stored, toe_here, ut_here = ([S(f"{n}{j}") for j in range(2)] for n in ("lags_stored", "toe_here", "ut_here"))
        kf, kb = C.bank[0:2]
        yb = C.bank[2:6]
        PRE, LAG = 8, 4
        with nc.Block() as block:
            @block.sync
            def _(sp):
                sp.dma_start(c[0][:], c_re).then_inc(c_here, 16)
                sp.dma_start(c[1][:], c_im).then_inc(c_here, 16)
                with sp.Fori(0, TURNS) as t:
                    for j in range(2):
                        n = sp.snap(t * 2 + j)
                        sp.wait_ge(y_mm, t * 4)
                        sp.nop(nofuse=True)
                        sp.dma_start(ut[:, j].rearrange("p g k c -> p (g k c)"),
                                     turned_dram[bass.ds(n, 1)].rearrange("a p n -> p (a n)")).then_inc(ut_here[j], 16)
                    for j in range(2):
                        sp.wait_ge(lag_steps, (t * 2 + j + 1) * LAG)
                        sp.nop(nofuse=True)
                        sp.dma_start(kernels[j].rearrange("g i n -> i g n"), lags[:, j]).then_inc(lags_stored[j], 16)
                        sp.wait_ge(lags_stored[j], t * 16 + 16)
                        sp.nop(nofuse=True)
                        for g in range(2):
                            for k in range(HALF):
                                rows = bass.AP(tensor=kernels.tensor, offset=((j * 2 + g) * CH5 * LAGS * CH5) + k * SPK * CH5,
                                               ap=[[CH5, SPK], [LAGS * CH5, CH5], [1, TC]])
                                sp.dma_start(toe[:, j, g, k, :], rows).then_inc(toe_here[j], 16)
                sp.wait_ge(gelued, 2 * PAIRS)
                sp.dma_start(yg[0:SAMPLE, :].rearrange("(c t) n -> c t n", t=T5), ys[:]).then_inc(out, 16)
                sp.dma_start(yg[SAMPLE:TOK, :].rearrange("(c t) n -> c t n", t=T5), yp[:]).then_inc(out, 16)
                sp.wait_ge(out, 32)

            @block.gpsimd
            def _(pool):
                pool.memset(e[:], 0.0).then_inc(zeroed, 1)
                pool.memset(st[:], 0.0).then_inc(zeroed, 1)
                pool.wait_ge(zeroed, 2)
                with pool.Fori(0, TURNS) as t:
                    for j in range(2):
                        n = pool.snap(t * 2 + j)
                        pool.wait_ge(kernel_mm, t * 2)
                        pool.nop(nofuse=True)
                        pool.tensor_copy(bs[:, j], C.b_bar[:, bass.ds(n, 1)].rearrange("p a r d i -> p (a r) d i")).then_inc(b_picked, 1)
                        pool.wait_ge(y_mm, t * 4)
                        pool.nop(nofuse=True)
                        for d in range(2):
                            x = C.states[:, :, :, :, bass.ds(n * 2 + d, 1)].rearrange("p k r s a -> p r k (s a)")
                            for s, (at, m) in enumerate(((0, C_S), (C_S, C_P))):
                                if d == 0:
                                    put = pool.tensor_copy(st[:, j, :, d, at + 1:at + m], x[:, :, 0:m - 1, s])
                                else:
                                    put = pool.tensor_copy(st[:, j, :, d, at:at + m - 1][:, :, ::-1], x[:, :, 0:m - 1, s])
                        put.then_inc(entered, 1)

            @block.vector
            def _(dve):
                dve.wait_ge(c_here, 32)
                dve.wait_ge(zeroed, 1)
                with dve.Fori(0, TURNS) as t:
                    steps = Steps(dve, dve_made, t, 2 * PRE)
                    lag = Steps(dve, lag_steps, t, 2 * LAG)
                    for j in range(2):
                        n = dve.snap(t * 2 + j)
                        dve.wait_ge(y_mm, t * 4)
                        dve.nop(nofuse=True)
                        four = lambda x: x.rearrange("p d (q i) -> p d q i", i=CH5)
                        power = [C.power_y[r][:, bass.ds(n, 1)].rearrange("p a d q -> p (a d) q").unsqueeze(3).to_broadcast([P, 2, Q, CH5]) for r in range(2)]
                        cc = [c[r][:, bass.ds(n, 1)].rearrange("p a d i -> p (a d) i").unsqueeze(2).to_broadcast([P, 2, Q, CH5]) for r in range(2)]
                        steps.done(dve.tensor_tensor(four(t1[:]), cc[0], power[0], ALU.mult))
                        steps.then(dve.tensor_tensor(four(t2[:]), cc[1], power[1], ALU.mult))
                        for g in range(2):
                            own = slice(g * N5, (g + 1) * N5)
                            steps.done(dve.tensor_tensor(e[own, j, 0, :, g], t1[own], t2[own], ALU.subtract))
                        steps.wait()
                        steps.done(dve.tensor_tensor(four(t1[:]), cc[0], power[1], ALU.mult))
                        steps.then(dve.tensor_tensor(four(t2[:]), cc[1], power[0], ALU.mult))
                        for g in range(2):
                            own = slice(g * N5, (g + 1) * N5)
                            steps.done(dve.scalar_tensor_tensor(out=e[own, j, 1, :, g], in0=t1[own], scalar=-1.0, in1=t2[own],
                                                                op0=ALU.mult, op1=ALU.subtract))
                        steps.wait()
                        dve.wait_ge(kernel_mm, t * 2 + j + 1)
                        dve.wait_ge(lags_stored[j], t * 16)
                        dve.nop(nofuse=True)
                        to = lags[:, j]
                        f, b = (x[0:CH5, :].rearrange("p (g n) -> p g n", g=2) for x in (kf, kb))
                        L0 = (T5 - 1) * CH5
                        lag.done(dve.tensor_copy(to[:, :, 0:L0], b[:, :, 0:L0]))
                        lag.done(dve.tensor_copy(to[:, :, L0 + CH5:], f[:, :, CH5:TC]))
                        lag.then(dve.tensor_tensor(to[:, :, L0:L0 + CH5], f[:, :, 0:CH5], C.d5_diag[:, bass.ds(n * 2, 2), :], ALU.add))
                        lag.then(dve.tensor_tensor(to[:, :, L0:L0 + CH5], b[:, :, L0:TC], to[:, :, L0:L0 + CH5], ALU.add))
                    steps.end_turn()
                    lag.end_turn()

            @block.tensor
            def _(pe):
                with pe.Fori(0, TURNS) as t:
                    for j in range(2):
                        m = t * 2 + j
                        pe.wait_ge(dve_made, (m + 1) * PRE)
                        pe.wait_ge(b_picked, m + 1)
                        pe.wait_ge(lag_steps, m * LAG)
                        for d, bank in enumerate((kf, kb)):
                            for r in range(2):
                                mul = pe.matmul(bank[0:CH5, :].rearrange("p (g n) -> p g n", g=2), bs[:, j, r, d, :],
                                                e[:, j, r, d, :, d * CH5:d * CH5 + TC], start=r == 0, stop=r == 1)
                        mul.then_inc(kernel_mm, 1)
                    for j in range(2):
                        m = t * 2 + j
                        pe.wait_ge(entered, m + 1)
                        pe.wait_ge(ut_here[j], t * 16 + 16)
                        pe.wait_ge(gelued, t * 4)
                        for s, (at, n) in enumerate(((0, C_S), (C_S, C_P))):
                            bank = yb[j * 2 + s][0:n, :]
                            for d in range(2):
                                for r in range(2):
                                    pe.matmul(bank.rearrange("p (g n) -> p g n", g=2), st[:, j, r, d, at:at + n],
                                              e[:, j, r, d, :, (1 - d) * CH5:(1 - d) * CH5 + TC], start=d == 0 and r == 0, stop=False)
                            if s == 0:
                                pe.wait_ge(toe_here[j], (t + 1) * 16 * 2 * HALF)
                            for g in range(2):
                                for k in range(HALF):
                                    mul = pe.matmul(bank[:, g * TC:(g + 1) * TC], ut[:, j, g, k, at:at + n], toe[:, j, g, k, :],
                                                    start=False, stop=g == 1 and k == HALF - 1)
                            mul.then_inc(y_mm, 1)

            @block.scalar
            def _(act):
                with act.Fori(0, TURNS) as t:
                    for j in range(2):
                        m = t * 2 + j
                        cols = act.snap(m * 2 * CH5)
                        for s, (y, n) in enumerate(((ys, C_S), (yp, C_P))):
                            act.wait_ge(y_mm, m * 2 + s + 1)
                            act.nop(nofuse=True)
                            act.activation(y[:, :, bass.ds(cols, 2 * CH5)].rearrange("p t (g i) -> p g t i", g=2),
                                           yb[j * 2 + s][0:n, :].rearrange("p (g t i) -> p g t i", g=2, t=T5), ACT.Gelu_apprx_tanh).then_inc(gelued, 1)
    S.clear()


def load_across(eng, to, row, sem):
    eng.dma_start(to, row.to_broadcast([P, row.shape[-1]])).then_inc(sem, 16)


def mix_out(nc, C, S, y_ssd, yg, x, mod, W, x1_dram, h_dram):
    TURNS = NWIDE // 2
    KY = SSD // P
    EVENTS = 3 * KY
    with ExitStack() as ctx:
        sb = lambda n, s: ctx.enter_context(nc.sbuf_tensor("mix_" + n, s, F32))
        wg, wo, wr = sb("wg", [P, KY, SSD]), sb("wo", [P, KT, D]), sb("wr", [P, KT, NE])
        norm_w, b_glu = sb("norm_w", [P, KY]), sb("b_glu", [P, KY])
        g1, scale, shift = sb("g1", [P, 2, D]), sb("scale", [P, 2, D]), sb("shift", [P, 2, D])
        ln_g, ln_b = sb("ln_g", [P, D]), sb("ln_b", [P, D])
        ya, yb = sb("ya", [P, TPW, SSD]), sb("yb", [P, TPW, SSD])
        xt = sb("xt", [P, 2, TPW, D])
        yt, gt, sg = sb("yt", [P, 2, KT, WIDE]), sb("gt", [P, KY, WIDE]), sb("sg", [P, KY, WIDE])
        v, h, ht = sb("v", [P, 2, D]), sb("h", [P, 2, D]), sb("ht", [P, KT, P])
        stats, mean = sb("stats", [P, 2, 6]), sb("mean", [P, 2, 2])
        flat = lambda a: a.rearrange("p a n -> p (a n)")
        w_here, y_here, one_added, turned, taken, gated, mixed, mix_read, ln, rooted, h_made = (
            S(n) for n in ("w_here", "y_here", "one_added", "turned", "taken", "gated", "mixed", "mix_read", "ln", "rooted", "h_made"))
        h_turned, h_taken, routed, kept = (S(n) for n in ("h_turned", "h_taken", "routed", "kept"))
        x_here, x1_stored, h_stored = ([S(f"{n}{j}") for j in range(2)] for n in ("x_here", "x1_stored", "h_stored"))
        LN = 8
        with nc.Block() as block:
            @block.sync
            def _(sp):
                loads = 0

                def load(to, src):
                    nonlocal loads
                    sp.dma_start(to, src).then_inc(w_here, 16)
                    loads += 16

                load(norm_w[:], W["ssd_norm_w"])
                load(b_glu[:], W["s5_b_glu"])
                load(wg[:], W["s5_w_glu"][0].rearrange("(k p) n -> p k n", p=P))
                load(wr[:], W["w_router"].rearrange("(k p) n -> p k n", p=P))
                load(wo[:], W["w_out"][0].rearrange("(k p) n -> p k n", p=P))
                for s in range(2):
                    for kind, to in ((2, g1), (4, scale), (3, shift)):
                        load(to[:, s, :], mod[s:s + 1, kind * D:(kind + 1) * D].to_broadcast([P, D]))
                load(ln_g[:], W["ln1_g"].to_broadcast([P, D]))
                load(ln_b[:], W["ln1_b"].to_broadcast([P, D]))
                assert loads == C.mix_loads
                with sp.Fori(0, TURNS) as t:
                    for j in range(2):
                        m = t * 2 + j
                        sp.wait_ge(turned, m * EVENTS)
                        sp.nop(nofuse=True)
                        sp.wait_ge(ln, t * 2 * TPW * LN)
                        sp.nop(nofuse=True)
                        wide = bass.ds(m * WIDE, WIDE)
                        sp.dma_start(yb[:], yg[wide, :].rearrange("(a p) n -> p a n", p=P)).then_inc(y_here, 16)
                        sp.dma_start(ya[:], y_ssd[wide, :].rearrange("(a p) n -> p a n", p=P)).then_inc(y_here, 16)
                        sp.dma_start(xt[:, j], x[wide, :].rearrange("(a p) n -> p a n", p=P)).then_inc(x_here[j], 16)

            @block.gpsimd
            def _(pool):
                pool.wait_ge(w_here, C.mix_loads)
                pool.tensor_scalar(scale[:], scale[:], 1.0, None, ALU.add).then_inc(one_added, 1)
                pool.wait_ge(one_added, 1)
                with pool.Fori(0, TURNS) as t:
                    for j in range(2):
                        s = pool.snap(seq_of(t, WIDE_SAMPLE // 2))
                        for a in range(TPW):
                            r = a % 2
                            n = (t * 2 + j) * TPW + a
                            pool.wait_ge(ln, n * LN + 5)
                            pool.nop(nofuse=True)
                            pool.tensor_scalar(mean[:, r, 1:2], mean[:, r, 1:2], EPS, None, ALU.add).then_inc(rooted, 1)
                            pool.wait_ge(rooted, n * 2 + 1)
                            pool.tensor_tensor(mean[:, r, 1:2], mean[:, r, 1:2], C.minus_half[:], ALU.pow).then_inc(rooted, 1)
                            pool.wait_ge(h_turned, (n - r) * 2)
                            pool.nop(nofuse=True)
                            pool.wait_ge(h_stored[r], (t * 2 + j) * 32 + a // 2 * 16)
                            pool.nop(nofuse=True)
                            pool.wait_ge(ln, (n + 1) * LN)
                            pool.nop(nofuse=True)
                            pool.tensor_tensor(h[:, r, :], v[:, r, :], flat(scale[:, bass.ds(s, 1), :]), ALU.mult).then_inc(h_made, 1)
                            pool.wait_ge(h_made, n * 2 + 1)
                            pool.nop(nofuse=True)
                            pool.tensor_tensor(h[:, r, :], h[:, r, :], flat(shift[:, bass.ds(s, 1), :]), ALU.add).then_inc(h_made, 1)

            @block.vector
            def _(dve):
                dve.wait_ge(w_here, C.mix_loads)
                with dve.Fori(0, TURNS) as t:
                    steps = Steps(dve, ln, t, 2 * TPW * LN)
                    for j in range(2):
                        m = dve.snap(t * 2 + j)
                        s = dve.snap(seq_of(t, WIDE_SAMPLE // 2))
                        for k in range(KY):
                            dve.wait_ge(taken, m * EVENTS + 2 * KY + k + 1)
                            dve.tensor_tensor(yt[:, j, KY + k, :], sg[:, k, :], gt[:, k, :], ALU.mult).then_inc(gated, 1)
                        dve.wait_ge(x_here[j], t * 16 + 16)
                        for a in range(TPW):
                            r = a % 2
                            dve.wait_ge(mixed, m * TPW + a + 1)
                            dve.wait_ge(x1_stored[r], m * 32 + a // 2 * 16)
                            dve.wait_ge(h_made, m * 2 * TPW + (a - r) * 2)
                            dve.nop(nofuse=True)
                            banks = C.bank[2 + 2 * r:4 + 2 * r]
                            steps.done(dve.tensor_tensor(v[:, r, 0:WIDE], banks[0][:, :], flat(g1[:, bass.ds(s, 1), 0:WIDE]), ALU.mult))
                            dve.tensor_tensor(v[:, r, WIDE:D], banks[1][:, :], flat(g1[:, bass.ds(s, 1), WIDE:D]), ALU.mult).then_inc(mix_read, 1)
                            dve.wait_ge(mix_read, m * TPW + a + 1)
                            steps.then(dve.scalar_tensor_tensor(out=v[:, r, :], in0=xt[:, j, a, :], scalar=ALPHA, in1=v[:, r, :],
                                                                op0=ALU.mult, op1=ALU.add))
                            for q in range(2):
                                steps.done(dve.bn_stats(stats[:, q, :], v[:, r, q * WIDE:(q + 1) * WIDE]))
                            steps.wait()
                            dve.nop(nofuse=True)
                            steps.done(dve.bn_aggr(mean[:, r, :], flat(stats[:])))
                            dve.wait_ge(rooted, (m * TPW + a + 1) * 2)
                            steps.then(dve.tensor_scalar(v[:, r, :], v[:, r, :], mean[:, r, 0:1], mean[:, r, 1:2], ALU.subtract, ALU.mult))
                            steps.then(dve.tensor_tensor(v[:, r, :], v[:, r, :], ln_g[:], ALU.mult))
                            steps.done(dve.tensor_tensor(v[:, r, :], v[:, r, :], ln_b[:], ALU.add))
                    steps.end_turn()

            def in_order(turn_gate, products, logits):
                def last_turn_or_not(m, j, more):
                    for a in range(TPW):
                        products(m, j, a)
                        if a:
                            logits(m, a - 1)
                    if more:
                        turn_gate(m + 1, 1 - j)
                    logits(m, TPW - 1)
                return last_turn_or_not

            @block.tensor
            def _(pe):
                def turn_gate(m, j):
                    pe.wait_ge(y_here, (m + 1) * 32)
                    for e in range(2 * KY):
                        pe.wait_ge(taken, m * EVENTS + max(e - 1, 0))
                        k, src = e % KY, yb if e < KY else ya
                        for a in range(TPW):
                            tr = pe.transpose(C.bank[e % 2][:, a * P:(a + 1) * P], src[:, a, k * P:(k + 1) * P], C.ident[:])
                        tr.then_inc(turned, 1)
                    for c in range(KY):
                        pe.wait_ge(taken, m * EVENTS + 2 * KY + c - 1)
                        for k in range(KY):
                            mul = pe.matmul(C.bank[c % 2][:, :], wg[:, k, c * P:(c + 1) * P], gt[:, k, :], start=k == 0, stop=k == KY - 1)
                        mul.then_inc(turned, 1)

                def products(m, j, a):
                    if a == 0:
                        pe.wait_ge(gated, (m + 1) * KY)
                    pe.wait_ge(mix_read, m * TPW + max(a - 1, 0))
                    for q in range(2):
                        for k in range(KT):
                            mul = pe.matmul(C.bank[2 + 2 * (a % 2) + q][:, :], yt[:, j, k, a * P:(a + 1) * P], wo[:, k, q * WIDE:(q + 1) * WIDE],
                                            start=k == 0, stop=k == KT - 1)
                    mul.then_inc(mixed, 1)

                def logits(m, a):
                    n = m * TPW + a
                    pe.wait_ge(h_made, n * 2 + 2)
                    for q in range(2):
                        pe.wait_ge(h_taken, n * 2 + q)
                        for k in range(4):
                            tr = pe.transpose(C.bank[6][:, k * P:(k + 1) * P], h[:, a % 2, (q * 4 + k) * P:(q * 4 + k + 1) * P], C.ident[:])
                        tr.then_inc(h_turned, 1)
                    pe.wait_ge(h_taken, n * 2 + 2)
                    pe.wait_ge(kept, n)
                    for k in range(KT):
                        mul = pe.matmul(C.bank[7][:, 0:NE], ht[:, k, :], wr[:, k, :], start=k == 0, stop=k == KT - 1)
                    mul.then_inc(routed, 1)

                pe.wait_ge(w_here, C.mix_loads)
                wide = in_order(turn_gate, products, logits)
                turn_gate(0, 0)
                with pe.Fori(0, TURNS - 1) as t:
                    for j in range(2):
                        wide(t * 2 + j, j, True)
                wide(NWIDE - 2, 0, True)
                wide(NWIDE - 1, 1, False)

            @block.scalar
            def _(act):
                def turn_gate(m, j):
                    act.wait_ge(gated, m * KY)
                    for e in range(EVENTS):
                        act.wait_ge(turned, m * EVENTS + e + 1)
                        k, bank = e % KY, C.bank[e % 2][:, :]
                        if e < KY:
                            take = act.activation(gt[:, k, :], bank, ACT.Copy)
                        elif e < 2 * KY:
                            take = act.activation(yt[:, j, k, :], bank, ACT.Copy, scale=norm_w[:, k:k + 1])
                        else:
                            take = act.activation(sg[:, k, :], bank, ACT.Sigmoid, bias=b_glu[:, k:k + 1])
                        take.then_inc(taken, 1)

                def products(m, j, a):
                    pass

                def logits(m, a):
                    n, r = m * TPW + a, a % 2
                    rows = bass.ds(n * P, P) if not isinstance(n, int) else slice(n * P, (n + 1) * P)
                    act.wait_ge(ln, (n + 1) * LN)
                    act.nop(nofuse=True)
                    act.dma_start(x1_dram[rows, :], v[:, r, :]).then_inc(x1_stored[r], 16)
                    act.wait_ge(h_made, n * 2 + 2)
                    act.nop(nofuse=True)
                    act.dma_start(h_dram[rows, :], h[:, r, :]).then_inc(h_stored[r], 16)
                    act.wait_ge(routed, n)
                    for q in range(2):
                        act.wait_ge(h_turned, n * 2 + q + 1)
                        act.activation(ht[:, q * 4:q * 4 + 4, :].rearrange("p k n -> p (k n)"), C.bank[6][:, :], ACT.Copy).then_inc(h_taken, 1)
                    act.wait_ge(routed, n + 1)
                    act.nop(nofuse=True)
                    where = bass.ds(n, 1) if not isinstance(n, int) else slice(n, n + 1)
                    act.activation(flat(C.logits[:, where, :]), C.bank[7][:, 0:NE], ACT.Copy).then_inc(kept, 1)

                act.wait_ge(w_here, C.mix_loads)
                wide = in_order(turn_gate, products, logits)
                turn_gate(0, 0)
                with act.Fori(0, TURNS - 1) as t:
                    for j in range(2):
                        wide(t * 2 + j, j, True)
                wide(NWIDE - 2, 0, True)
                wide(NWIDE - 1, 1, False)
                for r in range(2):
                    act.wait_ge(x1_stored[r], NT // 2 * 16)
                    act.wait_ge(h_stored[r], NT // 2 * 16)
    S.clear()


def route(nc, C, S, b_router, row_token):
    with ExitStack() as ctx:
        sb = lambda n, s, dt=F32: ctx.enter_context(nc.sbuf_tensor("rou_" + n, s, dt))
        b = sb("b", [P, NE])
        prob, masked, tie, both = (sb(n, [P, NT, NE]) for n in ("prob", "masked", "tie", "both"))
        first, second = sb("first", [P, NT, NE]), sb("second", [P, NT, NE])
        top, top2, one = sb("top", [P, NT]), sb("top2", [P, NT]), sb("one", [P, NT])
        group, group_tie = sb("group", [P, NT, NG]), sb("group_tie", [P, NT, NG])
        down_i, down = sb("down_i", [P, NE], I32), sb("down", [P, NE])
        base = sb("base", [P, NT + 1, NE])
        filled, filled_i, ends = sb("filled", [P, NE]), sb("filled_i", [P, NE], I32), sb("ends", [P, NE])
        place = sb("place", [P, NT, 2])
        starts_i, starts = sb("starts_i", [P, NBLK], I32), sb("starts", [P, NBLK])
        behind, owner = sb("behind", [P, NBLK, NE]), sb("owner", [P, NBLK])
        token, zero = sb("token", [P, NT], I32), sb("zero", [P, ROWS // P], I32)
        index, value = sb("index", [P, 8], I32), sb("value", [P, 8], I32)
        rows_i, rows_f = sb("rows_i", [NBLK, BLK], I32), sb("rows_f", [NBLK, BLK])
        b_here, made, steps_done, expd, counted, cleared, read_back, rows_turned, picked = (
            S(n) for n in ("b_here", "made", "steps_done", "expd", "counted", "cleared", "read_back", "rows_turned", "picked"))
        scattered = S("scattered", pool_dma=True)
        with nc.Block() as block:
            @block.sync
            def _(sp):
                sp.dma_start(b[:], b_router.to_broadcast([P, NE])).then_inc(b_here, 16)
                sp.wait_ge(made, 4)
                sp.dma_start(row_token.rearrange("(p n) a -> p (n a)", p=P), zero[:]).then_inc(cleared, 16)
                sp.wait_ge(scattered, 16 * 2 * NT)
                sp.dma_start(rows_i[:], row_token.rearrange("(b p) a -> b (p a)", p=BLK)).then_inc(read_back, 16)

            @block.gpsimd
            def _(pool):
                pool.iota(down_i[:], pattern=[[-1, NE]], base=NE, channel_multiplier=0).then_inc(made, 1)
                pool.iota(starts_i[:], pattern=[[BLK, NBLK]], base=0, channel_multiplier=0).then_inc(made, 1)
                pool.iota(token[:], pattern=[[P, NT]], base=0, channel_multiplier=1).then_inc(made, 1)
                pool.memset(zero[:], 0).then_inc(made, 1)
                pool.wait_ge(cleared, 16)
                pool.wait_ge(made, 4)
                pool.wait_ge(steps_done, C.route_placed)
                with pool.Fori(0, NT // 4) as t:
                    pool.wait_ge(scattered, t * 8 * 16)
                    pool.nop(nofuse=True)
                    dest = C.dest[:, bass.ds(t * 4, 4), :].rearrange("p t k -> p (t k)")
                    pool.tensor_copy(index[:], dest).then_inc(picked, 1)
                    pool.tensor_copy(value[:].rearrange("p (t k) -> p t k", k=2),
                                     token[:, bass.ds(t * 4, 4)].unsqueeze(2).to_broadcast([P, 4, 2])).then_inc(picked, 1)
                    pool.wait_ge(picked, t * 2 + 2)
                    pool.nop(nofuse=True)
                    for n in range(8):
                        pool.indirect_dma_start(out=row_token, out_offset=bass.IndirectOffsetOnAxis(ap=index[:, n:n + 1], axis=0),
                                                in_=value[:, n:n + 1], in_offset=None).then_inc(scattered, 16)

            @block.vector
            def _(dve):
                steps = Steps(dve, steps_done)
                tt = lambda o, a, c, op: steps.then(dve.tensor_tensor(o, a, c, op))
                ts = lambda o, a, s1, op0, s2=None, op1=ALU.bypass: steps.then(dve.tensor_scalar(o, a, s1, s2, op0, op1))
                red = lambda o, a, op: steps.then(dve.tensor_reduce(o, a, AX.X, op))
                per = lambda a, n: a.unsqueeze(2).to_broadcast([P, NT, n])
                row = lambda a: a.unsqueeze(1).to_broadcast([P, NT, NE])
                dve.wait_ge(b_here, 16)
                dve.wait_ge(made, 4)
                steps.then(dve.tensor_copy(down[:], down_i[:]))
                steps.then(dve.tensor_copy(starts[:], starts_i[:]))
                tt(prob[:], C.logits[:], row(b[:]), ALU.add)
                red(top[:], prob[:], ALU.max)
                tt(prob[:], prob[:], per(top[:], NE), ALU.subtract)
                C.route_shifted = steps.n
                dve.wait_ge(expd, 1)
                red(one[:], prob[:], ALU.add)
                steps.then(dve.reciprocal(one[:], one[:]))
                tt(prob[:], prob[:], per(one[:], NE), ALU.mult)
                red(group[:], prob[:].rearrange("p t (g e) -> p t g e", g=NG), ALU.max)
                red(top[:], group[:], ALU.max)
                tt(group_tie[:], group[:], per(top[:], NG), ALU.is_equal)
                tt(group_tie[:], group_tie[:], down[:, NE - NG:NE].unsqueeze(1).to_broadcast([P, NT, NG]), ALU.mult)
                red(one[:], group_tie[:], ALU.max)
                tt(group[:], group_tie[:], per(one[:], NG), ALU.is_equal)
                inside = group[:].unsqueeze(3).to_broadcast([P, NT, NG, EPG])
                four = lambda a: a.rearrange("p t (g e) -> p t g e", g=NG)
                tt(four(masked[:]), four(prob[:]), inside, ALU.mult)
                steps.then(dve.tensor_copy(four(tie[:]), inside))
                steps.then(dve.scalar_tensor_tensor(out=masked[:], in0=tie[:], scalar=-1.0, in1=masked[:], op0=ALU.add, op1=ALU.add))
                for best, pick in ((top, first), (top2, second)):
                    red(best[:], masked[:], ALU.max)
                    tt(tie[:], masked[:], per(best[:], NE), ALU.is_equal)
                    tt(tie[:], tie[:], row(down[:]), ALU.mult)
                    red(one[:], tie[:], ALU.max)
                    tt(pick[:], tie[:], per(one[:], NE), ALU.is_equal)
                    if pick is first:
                        steps.then(dve.scalar_tensor_tensor(out=masked[:], in0=first[:], scalar=-4.0, in1=masked[:], op0=ALU.mult, op1=ALU.add))
                tt(one[:], top[:], top2[:], ALU.add)
                steps.then(dve.reciprocal(one[:], one[:]))
                tt(C.gate[:, :, 0], top[:], one[:], ALU.mult)
                tt(C.gate[:, :, 1], top2[:], one[:], ALU.mult)
                tt(both[:], first[:], second[:], ALU.add)
                C.route_chosen = steps.n
                steps.then(dve.memset(base[:, 0, :], 0.0))
                dve.wait_ge(counted, 2)
                total = C.bank[1][:, 0:NT * NE].rearrange("p (t e) -> p t e", e=NE)
                with dve.Fori(0, NT) as t:
                    loop = Steps(dve, steps_done, t, 1, steps.n)
                    loop.then(dve.tensor_tensor(base[:, bass.ds(t + 1, 1), :], base[:, bass.ds(t, 1), :], total[:, bass.ds(t, 1), :], ALU.add))
                steps.n += NT
                ts(filled[:], base[:, NT, :], float(BLK - 1), ALU.add)
                steps.then(dve.tensor_copy(filled_i[:], filled[:]))
                ts(filled_i[:], filled_i[:], 7, ALU.logical_shift_right, 7, ALU.logical_shift_left)
                steps.then(dve.tensor_copy(filled[:], filled_i[:]))
                steps.then(dve.tensor_copy(ends[:], filled[:]))
                with dve.Fori(1, NE) as e:
                    loop = Steps(dve, steps_done, e - 1, 1, steps.n)
                    loop.then(dve.tensor_tensor(ends[:, bass.ds(e, 1)], ends[:, bass.ds(e, 1)], ends[:, bass.ds(e - 1, 1)], ALU.add))
                steps.n += NE - 1
                tt(filled[:], ends[:], filled[:], ALU.subtract)
                before = C.bank[0][:, 0:NT * NE].rearrange("p (t e) -> p t e", e=NE)
                tt(base[:, 0:NT, :], base[:, 0:NT, :], row(filled[:]), ALU.add)
                tt(base[:, 0:NT, :], base[:, 0:NT, :], before, ALU.add)
                for k, pick in enumerate((first, second)):
                    tt(tie[:], pick[:], base[:, 0:NT, :], ALU.mult)
                    red(place[:, :, k], tie[:], ALU.add)
                steps.then(dve.tensor_copy(C.dest[:], place[:]))
                assert steps.n == C.route_placed, steps.n
                tt(behind[:], ends[:].unsqueeze(1).to_broadcast([P, NBLK, NE]), starts[:].unsqueeze(2).to_broadcast([P, NBLK, NE]), ALU.is_le)
                red(owner[:], behind[:], ALU.add)
                ts(owner[:], owner[:], float(NE - 1), ALU.min)
                steps.then(dve.tensor_copy(C.expert[:], owner[:]))
                dve.wait_ge(read_back, 16)
                steps.then(dve.tensor_copy(rows_f[:], rows_i[:]))
                C.route_read = steps.n
                dve.wait_ge(rows_turned, 1)
                steps.then(dve.tensor_copy(C.source[:], C.bank[2][:, 0:NBLK]))

            @block.scalar
            def _(act):
                act.wait_ge(steps_done, C.route_shifted)
                act.activation(prob[:], prob[:], ACT.Exp).then_inc(expd, 1)

            @block.tensor
            def _(pe):
                pe.wait_ge(steps_done, C.route_chosen)
                for n, mask in enumerate((C.lt, C.ones)):
                    pe.matmul(C.bank[n][:, 0:NT * NE].rearrange("p (t e) -> p t e", e=NE), mask[:], both[:], start=True, stop=True).then_inc(counted, 1)
                pe.wait_ge(steps_done, C.route_read)
                pe.transpose(C.bank[2][:, 0:NBLK], rows_f[:], C.ident[0:NBLK, 0:NBLK]).then_inc(rows_turned, 1)
    S.clear()


def experts(nc, C, S, h_dram, w_gate, w_up, w_down, rows_out):
    TURNS = NBLK // 2 - 1
    KD = DE // P
    with ExitStack() as ctx:
        sb = lambda n, s, dt=F32: ctx.enter_context(nc.sbuf_tensor("exp_" + n, s, dt))
        wg, wu, wd = sb("wg", [P, 2, KT * DE]), sb("wu", [P, 2, KT * DE]), sb("wd", [P, 2, KD * D])
        index = sb("index", [P, 2], I32)
        h, ht = sb("h", [P, 2, D]), sb("ht", [P, 2, KT, P])
        silu, hid, hid_t = sb("silu", [P, DE]), sb("hid", [P, DE]), sb("hid_t", [P, 2, KD, P])
        out = sb("out", [P, 2, D])
        x0, x1, gate_b, up_b, hid_b, out0, out1 = (C.bank[n] for n in range(7))
        picked, turned, taken0, taken1, gate_mm, up_mm, down_mm, silu_done, hid_done, hid_turned, hid_taken, out0_read, out1_read = (
            S(n) for n in ("picked", "turned", "taken0", "taken1", "gate_mm", "up_mm", "down_mm", "silu_done", "hid_done",
                           "hid_turned", "hid_taken", "out0_read", "out1_read"))
        wg_here, wu_here, wd_here, h_here, stored = (
            [S(f"{n}{j}", pool_dma=n in ("h_here", "stored")) for j in range(2)] for n in ("wg_here", "wu_here", "wd_here", "h_here", "stored"))
        gv = w_gate.rearrange("e (p k) n -> e p (k n)", p=P)
        uv = w_up.rearrange("e (p k) n -> e p (k n)", p=P)
        dv = w_down.rearrange("e (p k) n -> e p (k n)", p=P)

        def blocks(eng, body, first, last):
            first()
            with eng.Fori(0, TURNS) as t:
                for i in range(2):
                    body(t * 2 + 1 + i, 1 - i)
            last()

        with nc.Block() as block:
            @block.sync
            def _(sp):
                def load(b, j, to, of, here):
                    one = bass.ds(b, 1) if not isinstance(b, int) else slice(b, b + 1)
                    e = sp.value_load(C.expert[0:1, one], min_val=0, max_val=NE - 1)
                    sp.dma_start(to[:, j, :], of[bass.ds(e, 1)].rearrange("a p n -> p (a n)")).then_inc(here[j], 16)

                for b in range(2):
                    load(b, b, wg, gv, wg_here)
                    load(b, b, wu, uv, wu_here)
                    load(b, b, wd, dv, wd_here)
                with sp.Fori(1, NBLK // 2) as t:
                    for j in range(2):
                        b = t * 2 + j
                        for to, of, here, free in ((wg, gv, wg_here, gate_mm), (wu, uv, wu_here, up_mm), (wd, dv, wd_here, down_mm)):
                            sp.wait_ge(free, b - 1)
                            sp.nop(nofuse=True)
                            load(b, j, to, of, here)

            @block.gpsimd
            def _(pool):
                def gather(b, j, wait=True):
                    if wait:
                        pool.wait_ge(turned, (b - 1) * 2)
                        pool.nop(nofuse=True)
                    one = bass.ds(b, 1) if not isinstance(b, int) else slice(b, b + 1)
                    pool.tensor_copy(index[:, j:j + 1], C.source[:, one]).then_inc(picked, 1)
                    pool.wait_ge(picked, b + 1)
                    pool.nop(nofuse=True)
                    pool.indirect_dma_start(out=h[:, j, :], out_offset=None, in_=h_dram,
                                            in_offset=bass.IndirectOffsetOnAxis(ap=index[:, j:j + 1], axis=0)).then_inc(h_here[j], 16)

                def store(b, j):
                    pool.wait_ge(out0_read, b + 1)
                    pool.nop(nofuse=True)
                    pool.wait_ge(out1_read, b + 1)
                    pool.nop(nofuse=True)
                    rows = bass.ds(b * BLK, BLK) if not isinstance(b, int) else slice(b * BLK, (b + 1) * BLK)
                    pool.dma_start(rows_out[rows, :], out[:, j, :]).then_inc(stored[j], 16)

                gather(0, 0, wait=False)
                gather(1, 1, wait=False)
                with pool.Fori(1, NBLK // 2) as t:
                    for j in range(2):
                        b = t * 2 + j
                        gather(b, j)
                        store(b - 2, j)
                store(NBLK - 2, 0)
                store(NBLK - 1, 1)
                for j in range(2):
                    pool.wait_ge(stored[j], NBLK // 2 * 16)

            @block.tensor
            def _(pe):
                def turn(b, j):
                    pe.wait_ge(h_here[j], b // 2 * 16 + 16)
                    pe.wait_ge(taken0, b)
                    for k in range(4):
                        tr = pe.transpose(x0[:, k * P:(k + 1) * P], h[:, j, k::KT], C.ident[:])
                    tr.then_inc(turned, 1)
                    pe.wait_ge(taken1, b)
                    for k in range(4, KT):
                        tr = pe.transpose(x1[:, (k - 4) * P:(k - 3) * P], h[:, j, k::KT], C.ident[:])
                    tr.then_inc(turned, 1)

                def hidden(b, j, of, bank, here, done, read):
                    pe.wait_ge(here[j], b // 2 * 16 + 16)
                    pe.wait_ge(read, b)
                    pe.wait_ge(taken0, b + 1)
                    pe.wait_ge(taken1, b + 1)
                    for k in range(KT):
                        mul = pe.matmul(bank[:, :], ht[:, j, k, :], of[:, j, k * DE:(k + 1) * DE], start=k == 0, stop=k == KT - 1)
                    mul.then_inc(done, 1)

                def turn_hidden(b, j):
                    pe.wait_ge(hid_done, b + 1)
                    pe.wait_ge(hid_taken, b)
                    for k in range(KD):
                        tr = pe.transpose(hid_b[:, k * P:(k + 1) * P], hid[:, k::KD], C.ident[:])
                    tr.then_inc(hid_turned, 1)

                def down(b, j):
                    pe.wait_ge(wd_here[j], b // 2 * 16 + 16)
                    pe.wait_ge(hid_taken, b + 1)
                    for bank, read, q in ((out0, out0_read, 0), (out1, out1_read, 1)):
                        pe.wait_ge(read, b)
                        for k in range(KD):
                            mul = pe.matmul(bank[:, :], hid_t[:, j, k, :], wd[:, j, k * D + q * WIDE:k * D + (q + 1) * WIDE],
                                            start=k == 0, stop=k == KD - 1)
                    mul.then_inc(down_mm, 1)

                def first():
                    turn(0, 0)
                    hidden(0, 0, wg, gate_b, wg_here, gate_mm, silu_done)
                    hidden(0, 0, wu, up_b, wu_here, up_mm, hid_done)
                    turn(1, 1)
                    turn_hidden(0, 0)

                def body(b, j, more=True):
                    hidden(b, j, wg, gate_b, wg_here, gate_mm, silu_done)
                    down(b - 1, 1 - j)
                    hidden(b, j, wu, up_b, wu_here, up_mm, hid_done)
                    if more:
                        turn(b + 1, 1 - j)
                    turn_hidden(b, j)

                def last():
                    body(NBLK - 1, 1, more=False)
                    down(NBLK - 1, 1)
                blocks(pe, body, first, last)

            @block.scalar
            def _(act):
                def take(b, j):
                    act.wait_ge(turned, b * 2 + 1)
                    act.activation(ht[:, j, 0:4, :].rearrange("p k n -> p (k n)"), x0[:, :], ACT.Copy).then_inc(taken0, 1)

                def gate(b):
                    act.wait_ge(gate_mm, b + 1)
                    act.wait_ge(hid_done, b)
                    act.activation(silu[:], gate_b[:, :], ACT.Silu).then_inc(silu_done, 1)

                def hidden(b, j):
                    act.wait_ge(hid_turned, b + 1)
                    act.activation(hid_t[:, j].rearrange("p k n -> p (k n)"), hid_b[:, :], ACT.Copy).then_inc(hid_taken, 1)

                def result(b, j):
                    act.wait_ge(down_mm, b + 1)
                    act.wait_ge(stored[j], b // 2 * 16)
                    act.activation(out[:, j, 0:WIDE], out0[:, :], ACT.Copy).then_inc(out0_read, 1)

                def first():
                    take(0, 0)
                    gate(0)
                    take(1, 1)
                    hidden(0, 0)

                def body(b, j, more=True):
                    gate(b)
                    result(b - 1, 1 - j)
                    if more:
                        take(b + 1, 1 - j)
                    hidden(b, j)

                def last():
                    body(NBLK - 1, 1, more=False)
                    result(NBLK - 1, 1)
                blocks(act, body, first, last)

            @block.vector
            def _(dve):
                def take(b, j):
                    dve.wait_ge(turned, b * 2 + 2)
                    dve.tensor_copy(ht[:, j, 4:KT, :].rearrange("p k n -> p (k n)"), x1[:, :]).then_inc(taken1, 1)

                def hidden(b):
                    dve.wait_ge(up_mm, b + 1)
                    dve.wait_ge(silu_done, b + 1)
                    dve.wait_ge(hid_turned, b)
                    dve.tensor_tensor(hid[:], silu[:], up_b[:, :], ALU.mult).then_inc(hid_done, 1)

                def result(b, j):
                    dve.wait_ge(down_mm, b + 1)
                    dve.wait_ge(stored[j], b // 2 * 16)
                    dve.tensor_copy(out[:, j, WIDE:D], out1[:, :]).then_inc(out1_read, 1)

                def first():
                    take(0, 0)
                    hidden(0)
                    take(1, 1)

                def body(b, j, more=True):
                    result(b - 1, 1 - j)
                    hidden(b)
                    if more:
                        take(b + 1, 1 - j)

                def last():
                    body(NBLK - 1, 1, more=False)
                    result(NBLK - 1, 1)
                blocks(dve, body, first, last)
    S.clear()


def combine(nc, C, S, rows_out, x1_dram, mod, ln_g_row, ln_b_row, out_sample, out_prompt):
    TURNS = NT // 2
    with ExitStack() as ctx:
        sb = lambda n, s, dt=F32: ctx.enter_context(nc.sbuf_tensor("com_" + n, s, dt))
        g2, ln_g, ln_b = sb("g2", [P, 2, D]), sb("ln_g", [P, D]), sb("ln_b", [P, D])
        index = sb("index", [P, 2, 2], I32)
        r, x1, v = sb("r", [P, 2, 2, D]), sb("x1", [P, 2, D]), sb("v", [P, 2, D])
        stats, mean, y = sb("stats", [P, 2, 6]), sb("mean", [P, 2, 2]), sb("y", [P, 2, D])
        flat = lambda a: a.rearrange("p a n -> p (a n)")
        w_here, picked, ln, rooted, shifted = (S(n) for n in ("w_here", "picked", "ln", "rooted", "shifted"))
        x1_here, stored = ([S(f"{n}{j}") for j in range(2)] for n in ("x1_here", "stored"))
        r_here = [S(f"r_here{j}", pool_dma=True) for j in range(2)]
        LN = 9
        with nc.Block() as block:
            @block.sync
            def _(sp):
                for s in range(2):
                    sp.dma_start(g2[:, s, :], mod[s:s + 1, 5 * D:6 * D].to_broadcast([P, D])).then_inc(w_here, 16)
                sp.dma_start(ln_g[:], ln_g_row.to_broadcast([P, D])).then_inc(w_here, 16)
                sp.dma_start(ln_b[:], ln_b_row.to_broadcast([P, D])).then_inc(w_here, 16)
                for lo, hi, out in ((0, NT_SAMPLE // 2, out_sample), (NT_SAMPLE // 2, TURNS, out_prompt)):
                    with sp.Fori(lo, hi) as t:
                        sp.wait_ge(ln, t * 2 * LN)
                        sp.nop(nofuse=True)
                        for j in range(2):
                            sp.dma_start(x1[:, j, :], x1_dram[bass.ds((t * 2 + j) * P, P), :]).then_inc(x1_here[j], 16)
                        for j in range(2):
                            sp.wait_ge(shifted, t * 2 + j + 1)
                            sp.nop(nofuse=True)
                            sp.dma_start(out[0, bass.ds(((t - lo) * 2 + j) * P, P), :], y[:, j, :]).then_inc(stored[j], 16)
                for j in range(2):
                    sp.wait_ge(stored[j], TURNS * 16)
                    sp.wait_ge(x1_here[j], TURNS * 16)

            @block.gpsimd
            def _(pool):
                def gather(t, j, first=False):
                    n = t * 2 + j
                    if not first:
                        pool.wait_ge(ln, (n - 1) * LN)
                        pool.nop(nofuse=True)
                    one = slice(n, n + 1) if isinstance(n, int) else bass.ds(n, 1)
                    pool.tensor_copy(index[:, j, :], flat(C.dest[:, one, :])).then_inc(picked, 1)
                    pool.wait_ge(picked, n + 1)
                    pool.nop(nofuse=True)
                    for k in range(2):
                        pool.indirect_dma_start(out=r[:, j, k, :], out_offset=None, in_=rows_out,
                                                in_offset=bass.IndirectOffsetOnAxis(ap=index[:, j, k:k + 1], axis=0)).then_inc(r_here[j], 16)

                def finish(n, j):
                    pool.wait_ge(ln, n * LN + 7)
                    pool.nop(nofuse=True)
                    pool.tensor_scalar(mean[:, j, 1:2], mean[:, j, 1:2], EPS, None, ALU.add).then_inc(rooted, 1)
                    pool.wait_ge(rooted, n * 2 + 1)
                    pool.tensor_tensor(mean[:, j, 1:2], mean[:, j, 1:2], C.minus_half[:], ALU.pow).then_inc(rooted, 1)
                    pool.wait_ge(ln, (n + 1) * LN)
                    pool.nop(nofuse=True)
                    pool.wait_ge(stored[j], n // 2 * 16)
                    pool.tensor_tensor(y[:, j, :], v[:, j, :], ln_b[:], ALU.add).then_inc(shifted, 1)

                pool.wait_ge(w_here, 64)
                gather(0, 0, first=True)
                gather(0, 1, first=True)
                with pool.Fori(1, TURNS) as t:
                    for j in range(2):
                        finish(t * 2 + j - 2, j)
                        gather(t, j)
                finish(NT - 2, 0)
                finish(NT - 1, 1)

            @block.vector
            def _(dve):
                dve.wait_ge(w_here, 64)
                with dve.Fori(0, TURNS) as t:
                    steps = Steps(dve, ln, t, 2 * LN)
                    s = dve.snap(seq_of(t, NT_SAMPLE // 2))
                    for j in range(2):
                        n = dve.snap(t * 2 + j)
                        dve.wait_ge(r_here[j], t * 32 + 32)
                        dve.wait_ge(shifted, t * 2)
                        dve.nop(nofuse=True)
                        steps.then(dve.tensor_scalar(v[:, j, :], r[:, j, 0, :], flat(C.gate[:, bass.ds(n, 1), 0:1]), None, ALU.mult))
                        steps.then(dve.scalar_tensor_tensor(out=v[:, j, :], in0=r[:, j, 1, :], scalar=flat(C.gate[:, bass.ds(n, 1), 1:2]),
                                                            in1=v[:, j, :], op0=ALU.mult, op1=ALU.add))
                        steps.then(dve.tensor_tensor(v[:, j, :], v[:, j, :], flat(g2[:, bass.ds(s, 1), :]), ALU.mult))
                        dve.wait_ge(x1_here[j], t * 16 + 16)
                        steps.then(dve.scalar_tensor_tensor(out=v[:, j, :], in0=x1[:, j, :], scalar=ALPHA, in1=v[:, j, :], op0=ALU.mult, op1=ALU.add))
                        for q in range(2):
                            steps.done(dve.bn_stats(stats[:, q, :], v[:, j, q * WIDE:(q + 1) * WIDE]))
                        steps.wait()
                        dve.nop(nofuse=True)
                        steps.done(dve.bn_aggr(mean[:, j, :], flat(stats[:])))
                        dve.wait_ge(rooted, (t * 2 + j + 1) * 2)
                        steps.then(dve.tensor_scalar(v[:, j, :], v[:, j, :], mean[:, j, 0:1], mean[:, j, 1:2], ALU.subtract, ALU.mult))
                        steps.done(dve.tensor_tensor(v[:, j, :], v[:, j, :], ln_g[:], ALU.mult))
                    steps.end_turn()
    S.clear()


class Kept:
    pass


def encoder(nc, A, out_sample, out_prompt, upto=99, debug=()):
    def scratch(name, shape, dt=F32):
        kind = "ExternalOutput" if name in debug else "Internal"
        return nc.dram_tensor(name, shape, dt, kind=kind).ap()

    with ExitStack() as ctx:
        C = Kept()
        S = Semaphores(nc, ctx)
        kept = lambda name, shape, dt=F32: ctx.enter_context(nc.sbuf_tensor(name, shape, dt))
        C.ident, C.le, C.ge, C.gt, C.lt, C.ones = (kept(n, [P, P]) for n in ("ident", "le", "ge", "gt", "lt", "ones"))
        C.minus_half = kept("minus_half", [P, 1])
        C.dt_raw = kept("dt_raw", [P, NT, 2 * HEADS])
        C.bank = [ctx.enter_context(nc.psum_tensor(f"bank{b}", [P, WIDE], F32)) for b in range(8)]
        C.dt, C.adt, C.dt_to_end, C.from_start, C.whole = (
            kept(n, [P, NT, 2 * HEADS]) for n in ("dt", "adt", "dt_to_end", "from_start", "whole"))
        mod = scratch("mod", [2, 6 * D])
        zs, u = scratch("zs", [TOK, SSD]), scratch("u", [TOK, SSD])
        raw, bc = scratch("raw", [CONV_CH, RAW_COLS]), scratch("bc", [CT - SSD // P, P, TOK])
        xb, y_ssd = scratch("xb", [TOK, SSD + 2 * STATE]), scratch("y_ssd", [TOK, SSD])
        constants(nc, C, S)
        adapt(nc, C, S, A["c"], A["w_ada"][0], A["b_ada"], mod)
        if upto < 1: return
        project(nc, C, S, A["x"], mod, A["w_in"][0], zs, raw, u)
        if upto < 2: return
        convolve(nc, C, S, raw, A["conv_w"], A["conv_b"], xb, bc)
        decays(nc, C, S, A["ssd_dt_bias"], A["ssd_a_log"])
        with ExitStack() as of_ssd:
            C.h_back = of_ssd.enter_context(nc.sbuf_tensor("h_back", [P, NT + 2, SSD], F32))
            scan_back(nc, C, S, xb)
            scan_forward(nc, C, S, xb, bc, zs, A["ssd_d"], y_ssd)
        if upto < 3: return
        yg = scratch("yg", [TOK, SSD])
        with ExitStack() as of_s5:
            sb = lambda n, s: of_s5.enter_context(nc.sbuf_tensor(n, s, F32))
            C.states = sb("states", [P, C_S, 2, 2, 2 * PAIRS])
            C.power_y = [sb(f"power_y{c}", [P, PAIRS, 2, T5 + 1]) for c in range(2)]
            C.b_bar = sb("b_bar", [P, PAIRS, 2, 2, CH5])
            C.d5_diag = sb("d5_diag", [CH5, G5, CH5])
            turned = scratch("turned", [PAIRS, P, 2 * HALF * C_ALL])
            kernels = scratch("kernels", [2, 2, CH5, (2 * T5 - 1) * CH5])
            with ExitStack() as of_states:
                sb = lambda n, s: of_states.enter_context(nc.sbuf_tensor(n, s, F32))
                C.power_w = [sb(f"power_w{c}", [P, PAIRS, 2, T5]) for c in range(2)]
                C.carry_re, C.carry_im = sb("carry_re", [P, 2, 2 * PAIRS]), sb("carry_im", [P, 2, 2 * PAIRS])
                s5_tables(nc, C, S, A["s5_lam_re"], A["s5_lam_im"], A["s5_log_step"], A["s5_b_re"], A["s5_b_im"], A["s5_d"])
                s5_states_in(nc, C, S, u, turned)
                s5_carry(nc, C, S)
            s5_outputs(nc, C, S, turned, kernels, A["s5_c_re"], A["s5_c_im"], yg)
        if upto < 4: return
        C.logits, C.gate = kept("logits", [P, NT, NE]), kept("gate", [P, NT, 2])
        C.dest, C.expert, C.source = kept("dest", [P, NT, 2], I32), kept("expert", [P, NBLK], I32), kept("source", [P, NBLK], I32)
        C.mix_loads = 16 * 13
        x1, h = scratch("x1", [TOK, D]), scratch("h", [TOK, D])
        mix_out(nc, C, S, y_ssd, yg, A["x"], mod, A, x1, h)
        if upto < 5: return
        C.route_placed = 86
        row_token = scratch("row_token", [ROWS, 1], I32)
        route(nc, C, S, A["b_router"], row_token)
        if upto < 6: return
        rows_out = scratch("rows_out", [ROWS, D])
        experts(nc, C, S, h, A["w_gate"][0], A["w_up"][0], A["w_down"][0], rows_out)
        combine(nc, C, S, rows_out, x1, mod, A["ln2_g"], A["ln2_b"], out_sample, out_prompt)


def layout(a):
    a = dict(a)
    t = np.ascontiguousarray
    for n in ("x", "c"):
        if n not in a:
            a[n] = np.concatenate([a[n + "_sample"].reshape(-1, D), a[n + "_prompt"].reshape(-1, D)])
            del a[n + "_sample"], a[n + "_prompt"]
    a["conv_w"] = t(a["conv_w"][0].T.reshape(CT, P, TAPS).transpose(1, 0, 2))
    a["conv_b"] = t(a["conv_b"][0].reshape(CT, P).T)
    for n in ("ssd_dt_bias", "ssd_a_log"):
        a[n] = a[n].reshape(1, 2 * HEADS)
    for n in ("ssd_norm_w", "s5_b_glu"):
        a[n] = t(a[n][0].reshape(-1, P).T)
    a["b_router"] = a["b_router"].reshape(1, NE)
    by_state = lambda x: t(x.reshape(2, PAIRS, 2, N5).transpose(2, 3, 1, 0).reshape(P, 2 * PAIRS))
    a["s5_lam_re"], a["s5_lam_im"] = by_state(a["s5_lam_re"][0]), by_state(a["s5_lam_im"][0])
    a["s5_log_step"] = t(a["s5_log_step"][0].reshape(2, PAIRS, 2).transpose(2, 1, 0).reshape(2, 2 * PAIRS))
    for n in ("s5_b_re", "s5_b_im"):
        a[n] = t(a[n][0].reshape(PAIRS, 2, N5, CH5).transpose(1, 2, 0, 3).reshape(P, PAIRS, CH5))
    for n in ("s5_c_re", "s5_c_im"):
        a[n] = t(a[n][0].reshape(2, PAIRS, 2, CH5, N5).transpose(2, 4, 1, 0, 3).reshape(P, PAIRS, 2, CH5))
    return a


OUTPUTS = ((1, PROMPT, D), (1, SAMPLE, D))


def kernel(**inputs):
    import concourse.bacc as bacc
    from concourse.bass_utils import run_bass_kernel_spmd

    nc = bacc.Bacc("TRN2", target_bir_lowering=False, num_devices=1)
    arrays, aps = {}, {}
    for name, a in layout({n: np.asarray(v) for n, v in inputs.items()}).items():
        arrays[f"in_{name}"] = np.ascontiguousarray(a)
        aps[name] = nc.dram_tensor(f"in_{name}", a.shape, mybir.dt.from_np(a.dtype), kind="ExternalInput").ap()
    outs = [nc.dram_tensor(f"out_{i}", s, F32, kind="ExternalOutput").ap() for i, s in enumerate(OUTPUTS)]
    encoder(nc, aps, outs[1], outs[0])
    r = run_bass_kernel_spmd(nc, [arrays], core_ids=[0]).results[0]
    return r["out_0"], r["out_1"]
```

```python
from contextlib import ExitStack

import numpy as np

import concourse.bass as bass
from concourse import mybir

F32 = mybir.dt.float32
I32 = mybir.dt.int32
ALU = mybir.AluOpType
ACT = mybir.ActivationFunctionType
AX = mybir.AxisListType

P = 128
D = 1024
SAMPLE, PROMPT = 2048, 1024
TOK = SAMPLE + PROMPT
KT = D // P
WIDE = 512
NWIDE = TOK // WIDE
WIDE_SAMPLE = SAMPLE // WIDE
TPW = WIDE // P
NT = TOK // P
NT_SAMPLE = SAMPLE // P
EPS = 1e-5
ALPHA = 2.0 ** 0.25

SSD = 512
HEADS, HD = 8, 64
STATE = 128
CONV_CH, TAPS = 1024, 5
CT = CONV_CH // P
HALO = TAPS // 2
Z0, XBC0, DT0, U0 = 0, SSD, SSD + CONV_CH, SSD + CONV_CH + 2 * HEADS
IN_COLS = U0 + SSD
RAW_COLS = TOK + 4 * HALO

G5, CH5, N5 = 32, 16, 64
PAIRS = G5 // 2
T5 = 16
C_S, C_P = SAMPLE // T5, PROMPT // T5
C_ALL = C_S + C_P
HALF = T5 * CH5 // P
SPK = T5 // HALF

NE, NG, EPG, DE = 16, 4, 4, 512
BLK = 128
NBLK = 2 * TOK // BLK + NE - 1
ROWS = NBLK * BLK


class Semaphores:

    def __init__(self, nc, ctx):
        self.nc, self.ctx, self.made = nc, ctx, 0
        self.free, self.used = [], []

    def __call__(self, name, pool_dma=False):
        if self.free and not pool_dma:
            s = self.free.pop()
        else:
            s = self.ctx.enter_context(self.nc.semaphore(f"count{self.made}_{name}"))
            self.made += 1
        if not pool_dma:
            self.used.append(s)
        return s

    def clear(self):
        with self.nc.Block() as block:
            @block.gpsimd
            def _(pool):
                for s in self.used:
                    pool.sem_clear(s)
        self.free += self.used[::-1]
        self.used = []


class Steps:

    def __init__(self, eng, sem, turn=None, per_turn=0, before=0):
        self.eng, self.sem, self.turn, self.per_turn, self.n, self.before = eng, sem, turn, per_turn, 0, before

    def done(self, ins):
        ins.then_inc(self.sem, 1)
        self.n += 1

    def wait(self, back=0):
        at = self.before + self.n - back
        self.eng.wait_ge(self.sem, at if self.turn is None else self.turn * self.per_turn + at)

    def then(self, ins):
        self.done(ins)
        self.wait()

    def end_turn(self):
        assert self.n == self.per_turn, (self.n, self.per_turn)


def seq_of(turn, turns_of_sample):
    return turn // turns_of_sample


def constants(nc, C, S):
    made = S("made")
    with nc.Block() as block:
        @block.gpsimd
        def _(pool):
            steps = Steps(pool, made)
            steps.done(pool.memset(C.ident[:], 0.0))
            for t in (C.le, C.ge, C.gt, C.lt, C.ones):
                steps.done(pool.memset(t[:], 1.0))
            steps.done(pool.memset(C.minus_half[:], -0.5))
            steps.wait()
            for t, sign, op, fill in ((C.ident, 1, ALU.not_equal, 1.0), (C.le, 1, ALU.is_ge, 0.0), (C.ge, -1, ALU.is_ge, 0.0),
                                      (C.gt, -1, ALU.is_gt, 0.0), (C.lt, 1, ALU.is_gt, 0.0)):
                steps.done(pool.affine_select(out=t[:], in_=t[:], compare_op=op, fill=fill, base=0, pattern=[[sign, P]],
                                              channel_multiplier=-sign))
            steps.wait()
    S.clear()


def adapt(nc, C, S, c_all, w_ada, b_ada, mod, kinds, ahead=None, beside=None):
    PIECE = 512
    lo, hi = kinds.start * D, kinds.stop * D
    TURNS = (hi - lo) // PIECE // 2
    w = w_ada.rearrange("(p k) n -> p k n", p=P)
    with ExitStack() as ctx:
        sb = lambda n, s: ctx.enter_context(nc.sbuf_tensor(f"ada{lo}_{n}", s, F32))
        ct, cs = sb("ct", [P, 2, KT]), sb("cs", [P, KT, 2])
        wt = sb("wt", [P, 2, KT, PIECE])
        rows, bias = sb("rows", [2, hi - lo]), sb("bias", [2, hi - lo])
        acc = C.bank[0:2]
        c_in, b_in, act_c, mm, kept, added, out = (S(n) for n in ("c_in", "b_in", "act_c", "mm", "kept", "added", "out"))
        w_in = [S(f"w_in{j}") for j in range(2)]
        with nc.Block() as block:
            @block.sync
            def _(sp):
                sp.dma_start(ct[:], c_all.rearrange("s (p k) -> p s k", p=P)).then_inc(c_in, 16)
                for j in range(2):
                    sp.dma_start(wt[:, j], w[:, :, lo + j * PIECE:lo + (j + 1) * PIECE]).then_inc(w_in[j], 16)
                for s in range(2):
                    sp.dma_start(bias[s:s + 1, :], b_ada[:, lo:hi]).then_inc(b_in, 16)
                with sp.Fori(0, TURNS - 1) as t:
                    for j in range(2):
                        sp.wait_ge(mm, t * 2 + j + 1)
                        sp.dma_start(wt[:, j], w[:, :, bass.ds((t * 2 + j + 2) * PIECE + lo, PIECE)]).then_inc(w_in[j], 16)
                if ahead:
                    ahead(sp)
                sp.wait_ge(added, 1)
                sp.dma_start(mod[:, lo:hi], rows[:]).then_inc(out, 16)
                sp.wait_ge(out, 16)

            @block.gpsimd
            def _(pool):
                pool.wait_ge(b_in, 32)
                pool.wait_ge(kept, 2 * TURNS)
                pool.tensor_tensor(rows[:], rows[:], bias[:], ALU.add).then_inc(added, 1)

            @block.scalar
            def _(act):
                act.wait_ge(c_in, 16)
                act.activation(cs[:], ct[:].rearrange("p s k -> p k s"), ACT.Silu).then_inc(act_c, 1)
                with act.Fori(0, TURNS) as t:
                    for j in range(2):
                        act.wait_ge(mm, t * 2 + j + 1)
                        act.nop(nofuse=True)
                        act.activation(rows[:, bass.ds((t * 2 + j) * PIECE, PIECE)], acc[j][0:2, :], ACT.Copy).then_inc(kept, 1)

            @block.tensor
            def _(pe):
                pe.wait_ge(act_c, 1)
                with pe.Fori(0, TURNS) as t:
                    for j in range(2):
                        pe.wait_ge(w_in[j], t * 16 + 16)
                        pe.wait_ge(kept, t * 2)
                        for k in range(KT):
                            mul = pe.matmul(acc[j][0:2, :], cs[:, k, :], wt[:, j, k, :], start=k == 0, stop=k == KT - 1)
                        mul.then_inc(mm, 1)

            @block.vector
            def _(dve):
                if beside:
                    beside(dve)
    S.clear()


def project(nc, C, S, x, mod, zs, raw, u):
    TURNS = NWIDE // 2
    SAMPLE_TURNS = WIDE_SAMPLE // 2
    RING = 4
    OUTS = CT + 2 * TPW
    with ExitStack() as ctx:
        sb = lambda n, s: ctx.enter_context(nc.sbuf_tensor("pro_" + n, s, F32))
        w = C.w_in
        xt = sb("xt", [P, 2, TPW, D])
        ht = sb("ht", [P, 2, KT, WIDE])
        scale, shift = sb("scale", [P, 2, KT]), sb("shift", [P, 2, KT])
        zero = sb("zero", [P, CT, 2 * HALO])
        stage = sb("stage", [P, RING, WIDE])
        turned, acc, dt_acc = C.bank[0:2], C.bank[2:2 + RING], C.bank[6]
        mod_here, one_added, zeroed, padded = (S(n) for n in ("mod_here", "one_added", "zeroed", "padded"))
        x_here = [S(f"x_here{j}", pool_dma=True) for j in range(2)]
        transposed, h_ready, product, staged, dt_mm, dt_kept = (
            S(n) for n in ("transposed", "h_ready", "product", "staged", "dt_mm", "dt_kept"))
        stored = [S(f"stored{r}") for r in range(RING)]
        with nc.Block() as block:
            @block.gpsimd
            def _(pool):
                with pool.Fori(0, TURNS) as t:
                    for j in range(2):
                        pool.wait_ge(transposed, t * 2 * KT)
                        pool.dma_start(xt[:, j], x[bass.ds((t * 2 + j) * WIDE, WIDE), :].rearrange(
                            "(a p) n -> p a n", p=P)).then_inc(x_here[j], 16)

            @block.sync
            def _(sp):
                for kind, sc in ((1, scale), (0, shift)):
                    sp.dma_start(sc[:], mod[:, kind * D:(kind + 1) * D].rearrange("s (p k) -> p s k", p=P)).then_inc(mod_here, 16)
                sp.wait_ge(zeroed, 1)
                rows = raw.rearrange("(c p) n -> p c n", p=P)
                for at, n in ((0, HALO), (HALO + SAMPLE, 2 * HALO), (RAW_COLS - HALO, HALO)):
                    sp.dma_start(rows[:, :, at:at + n], zero[:, :, 0:n]).then_inc(padded, 16)
                with sp.Fori(0, TURNS) as t:
                    for j in range(2):
                        m = t * 2 + j
                        col = m * WIDE + HALO + seq_of(t, SAMPLE_TURNS) * (2 * HALO)
                        for o in range(OUTS):
                            sp.wait_ge(staged, m * OUTS + o + 1)
                            r = o % RING
                            if o < CT:
                                to = raw[o * P:(o + 1) * P, bass.ds(col, WIDE)]
                            else:
                                to = (zs if o < CT + TPW else u)[bass.ds(m * WIDE + (o - CT) % TPW * P, P), :]
                            sp.dma_start(to, stage[:, r, :]).then_inc(stored[r], 16)
                sp.wait_ge(padded, 48)
                for r in range(RING):
                    sp.wait_ge(stored[r], 16 * NWIDE * OUTS // RING)

            @block.vector
            def _(dve):
                dve.memset(zero[:], 0.0).then_inc(zeroed, 1)
                dve.wait_ge(mod_here, 32)
                dve.tensor_scalar(scale[:], scale[:], 1.0, None, ALU.add).then_inc(one_added, 1)
                dve.wait_ge(one_added, 1)
                with dve.Fori(0, TURNS) as t:
                    s = seq_of(t, SAMPLE_TURNS)
                    for j in range(2):
                        m = t * 2 + j
                        dve.wait_ge(product, t * 2 * OUTS)
                        for k in range(KT):
                            dve.wait_ge(transposed, m * KT + k + 1)
                            dve.tensor_scalar(ht[:, j, k, :], turned[k % 2][:, :], scale[:, bass.ds(s, 1), k:k + 1].rearrange("p a b -> p (a b)"),
                                              shift[:, bass.ds(s, 1), k:k + 1].rearrange("p a b -> p (a b)"),
                                              ALU.mult, ALU.add).then_inc(h_ready, 1)
                        dve.wait_ge(dt_mm, m + 1)
                        dve.tensor_copy(C.dt_raw[:, bass.ds(m * TPW, TPW), :],
                                        dt_acc[:, 0:TPW * 2 * HEADS].rearrange("p (a c) -> p a c", a=TPW)).then_inc(dt_kept, 1)

            @block.tensor
            def _(pe):
                with pe.Fori(0, TURNS) as t:
                    for j in range(2):
                        m = t * 2 + j
                        pe.wait_ge(x_here[j], t * 16 + 16)
                        for k in range(KT):
                            if k >= 2:
                                pe.wait_ge(h_ready, m * KT + k - 1)
                            else:
                                pe.wait_ge(h_ready, m * KT)
                            for a in range(TPW):
                                tr = pe.transpose(turned[k % 2][:, a * P:(a + 1) * P], xt[:, j, a, k::KT], C.ident[:])
                            tr.then_inc(transposed, 1)
                        if j == 0:
                            pe.wait_ge(C.w_in_here, 16)
                        pe.wait_ge(h_ready, (m + 1) * KT)
                        pe.wait_ge(dt_kept, m)
                        for a in range(TPW):
                            for k in range(KT):
                                mul = pe.matmul(dt_acc[:, a * 2 * HEADS:(a + 1) * 2 * HEADS], ht[:, j, k, a * P:(a + 1) * P],
                                                w[:, k, DT0:DT0 + 2 * HEADS], start=k == 0, stop=k == KT - 1)
                        mul.then_inc(dt_mm, 1)
                        for o in range(OUTS):
                            if o >= RING:
                                pe.wait_ge(staged, m * OUTS + o - RING + 1)
                            else:
                                pe.wait_ge(staged, m * OUTS)
                            for k in range(KT):
                                if o < CT:
                                    left, right = w[:, k, XBC0 + o * P:XBC0 + (o + 1) * P], ht[:, j, k, :]
                                else:
                                    a = (o - CT) % TPW
                                    at = Z0 if o < CT + TPW else U0
                                    left, right = ht[:, j, k, a * P:(a + 1) * P], w[:, k, at:at + SSD]
                                mul = pe.matmul(acc[o % RING][:, :], left, right, start=k == 0, stop=k == KT - 1)
                            mul.then_inc(product, 1)

            @block.scalar
            def _(act):
                with act.Fori(0, TURNS) as t:
                    for j in range(2):
                        m = t * 2 + j
                        for o in range(OUTS):
                            r = o % RING
                            act.wait_ge(product, m * OUTS + o + 1)
                            act.wait_ge(stored[r], (m * (OUTS // RING) + o // RING) * 16)
                            act.activation(stage[:, r, :], acc[r][:, :],
                                           ACT.Silu if CT <= o < CT + TPW else ACT.Copy).then_inc(staged, 1)
    S.clear()


def convolve(nc, C, S, raw, conv_w, conv_b, xb, bc):
    TURNS = NWIDE // 2
    BY_DVE = 5
    BY_PE = CT - BY_DVE
    XB = SSD // P + 2
    with ExitStack() as ctx:
        sb = lambda n, s: ctx.enter_context(nc.sbuf_tensor("con_" + n, s, F32))
        cw, cb = sb("cw", [P, CT, TAPS]), sb("cb", [P, CT])
        diag = sb("diag", [P, BY_PE, TAPS, P])
        src = sb("src", [P, 2, CT, WIDE + 2 * HALO])
        acc = sb("acc", [P, 2, BY_DVE, WIDE])
        out = sb("out", [P, 2, CT, WIDE])
        rows = sb("rows", [P, 2, XB * P])
        sums, turned = C.bank[0:BY_PE], C.bank[4:8]
        w_here, diag_made, taps, summed, activated, transposed, rows_ready = (
            S(n) for n in ("w_here", "diag_made", "taps", "summed", "activated", "transposed", "rows_ready"))
        src_here, bc_stored, rows_stored = ([S(f"{n}{j}") for j in range(2)] for n in ("src_here", "bc_stored", "rows_stored"))
        order = [*range(BY_DVE, CT), *range(BY_DVE)]
        with nc.Block() as block:
            @block.sync
            def _(sp):
                sp.dma_start(cw[:], conv_w).then_inc(w_here, 16)
                sp.dma_start(cb[:], conv_b).then_inc(w_here, 16)
                with sp.Fori(0, TURNS) as t:
                    for j in range(2):
                        col = sp.snap((t * 2 + j) * WIDE + seq_of(t, WIDE_SAMPLE // 2) * (2 * HALO))
                        sp.wait_ge(taps, t * 2 * BY_DVE * TAPS)
                        sp.nop(nofuse=True)
                        sp.wait_ge(summed, t * 2 * BY_PE)
                        sp.nop(nofuse=True)
                        sp.dma_start(src[:, j], raw[:, bass.ds(col, WIDE + 2 * HALO)].rearrange(
                            "(c p) n -> p c n", p=P)).then_inc(src_here[j], 16)
                    for j in range(2):
                        m = t * 2 + j
                        sp.wait_ge(activated, (m + 1) * CT)
                        sp.nop(nofuse=True)
                        sp.dma_start(bc[:, :, bass.ds(m * WIDE, WIDE)].rearrange("c p n -> p c n"),
                                     out[:, j, SSD // P:CT, :]).then_inc(bc_stored[j], 16)
                        for a in range(TPW):
                            sp.wait_ge(rows_ready, m * TPW + a + 1)
                            sp.nop(nofuse=True)
                            sp.dma_start(xb[bass.ds(m * WIDE + a * P, P), :], rows[:, a % 2, :]).then_inc(rows_stored[a % 2], 16)
                for j in range(2):
                    sp.wait_ge(bc_stored[j], 16 * TURNS)
                    sp.wait_ge(rows_stored[j], 16 * NT // 2)

            @block.gpsimd
            def _(pool):
                pool.wait_ge(w_here, 32)
                for c in range(BY_PE):
                    for k in range(TAPS):
                        pool.tensor_scalar(diag[:, c, k, :], C.ident[:], cw[:, BY_DVE + c, k:k + 1], None, ALU.mult).then_inc(diag_made, 1)

            @block.vector
            def _(dve):
                dve.wait_ge(w_here, 32)
                with dve.Fori(0, TURNS) as t:
                    steps = Steps(dve, taps, t, 2 * BY_DVE * TAPS)
                    for j in range(2):
                        dve.wait_ge(src_here[j], t * 16 + 16)
                        dve.wait_ge(activated, t * 2 * CT)
                        for k in range(TAPS):
                            for c in range(BY_DVE):
                                x = src[:, j, c, k:k + WIDE]
                                if k == 0:
                                    steps.done(dve.tensor_scalar(acc[:, j, c, :], x, cw[:, c, 0:1], None, ALU.mult))
                                else:
                                    steps.wait(back=BY_DVE - 1)
                                    steps.done(dve.scalar_tensor_tensor(out=acc[:, j, c, :], in0=x, scalar=cw[:, c, k:k + 1],
                                                                        in1=acc[:, j, c, :], op0=ALU.mult, op1=ALU.add))
                    steps.end_turn()

            @block.tensor
            def _(pe):
                pe.wait_ge(diag_made, BY_PE * TAPS)
                with pe.Fori(0, TURNS) as t:
                    for j in range(2):
                        m = t * 2 + j
                        pe.wait_ge(src_here[j], t * 16 + 16)
                        pe.wait_ge(activated, m * CT)
                        for c in range(BY_PE):
                            for k in range(TAPS):
                                mul = pe.matmul(sums[c][:, :], diag[:, c, k, :], src[:, j, BY_DVE + c, k:k + WIDE],
                                                start=k == 0, stop=k == TAPS - 1)
                            mul.then_inc(summed, 1)
                        pe.wait_ge(activated, (m + 1) * CT)
                        for a in range(TPW):
                            if a >= 2:
                                pe.wait_ge(rows_ready, m * TPW + a - 1)
                            else:
                                pe.wait_ge(rows_ready, m * TPW)
                            for c in range(XB):
                                tr = pe.transpose(turned[a % 2 * 2 + c // 4][:, c % 4 * P:(c % 4 + 1) * P],
                                                  out[:, j, c, a * P:(a + 1) * P], C.ident[:])
                            tr.then_inc(transposed, 1)

            @block.scalar
            def _(act):
                act.wait_ge(w_here, 32)
                with act.Fori(0, TURNS) as t:
                    for j in range(2):
                        m = t * 2 + j
                        act.wait_ge(bc_stored[j], t * 16)
                        act.wait_ge(transposed, t * 2 * TPW)
                        for n, c in enumerate(order):
                            if c >= BY_DVE:
                                act.wait_ge(summed, m * BY_PE + c - BY_DVE + 1)
                                x = sums[c - BY_DVE][:, :]
                            else:
                                act.wait_ge(taps, m * BY_DVE * TAPS + BY_DVE * (TAPS - 1) + c + 1)
                                x = acc[:, j, c, :]
                            act.activation(out[:, j, c, :], x, ACT.Silu, bias=cb[:, c:c + 1]).then_inc(activated, 1)
                        for a in range(TPW):
                            act.wait_ge(transposed, m * TPW + a + 1)
                            act.wait_ge(rows_stored[a % 2], (m * TPW // 2 + a // 2) * 16)
                            act.activation(rows[:, a % 2, 0:4 * P], turned[a % 2 * 2][:, :], ACT.Copy)
                            act.activation(rows[:, a % 2, 4 * P:XB * P], turned[a % 2 * 2 + 1][:, 0:(XB - 4) * P],
                                           ACT.Copy).then_inc(rows_ready, 1)
    S.clear()


def decays(nc, C, S, dt_bias, a_log):
    H2 = 2 * HEADS
    with ExitStack() as ctx:
        sb = lambda n, s: ctx.enter_context(nc.sbuf_tensor("dec_" + n, s, F32))
        bias, alog, decay = sb("bias", [P, H2]), sb("alog", [P, H2]), sb("decay", [P, H2])
        v, w = sb("v", [P, NT, H2]), sb("w", [P, NT, H2])
        to_end = sb("to_end", [P, NT, H2])
        here, soft, expd, summed = (S(n) for n in ("here", "soft", "expd", "summed"))
        sums = [C.bank[n][:, 0:NT * HEADS].rearrange("p (c h) -> p c h", h=HEADS) for n in range(6)]
        fwd, bwd = slice(0, HEADS), slice(HEADS, H2)
        with nc.Block() as block:
            @block.sync
            def _(sp):
                sp.dma_start(bias[:], dt_bias.to_broadcast([P, H2])).then_inc(here, 16)
                sp.dma_start(alog[:], a_log.to_broadcast([P, H2])).then_inc(here, 16)

            @block.vector
            def _(dve):
                steps = Steps(dve, soft)
                wide = lambda t: t[:].unsqueeze(1).to_broadcast([P, NT, H2])
                dve.wait_ge(here, 32)
                steps.then(dve.tensor_tensor(v[:], C.dt_raw[:], wide(bias), ALU.add))
                steps.then(dve.tensor_scalar(w[:], v[:], -1.0, None, ALU.mult))
                steps.then(dve.tensor_tensor(w[:], w[:], v[:], ALU.min))
                dve.wait_ge(expd, 3)
                steps.then(dve.tensor_scalar(v[:], v[:], 0.0, None, ALU.max))
                steps.then(dve.tensor_tensor(C.dt[:], v[:], w[:], ALU.add))
                steps.then(dve.tensor_tensor(v[:], C.dt[:], wide(decay), ALU.mult))
                steps.then(dve.tensor_scalar(C.adt[:], v[:], -1.0, None, ALU.mult))
                dve.wait_ge(expd, 9)
                steps.done(dve.tensor_tensor(C.dt_to_end[:], C.dt[:], to_end[:], ALU.mult))

            @block.scalar
            def _(act):
                steps = Steps(act, expd)
                act.wait_ge(here, 32)
                steps.done(act.activation(decay[:], alog[:], ACT.Exp))
                act.wait_ge(soft, 3)
                steps.then(act.activation(w[:], w[:], ACT.Exp))
                steps.then(act.activation(w[:], w[:], ACT.Ln, bias=1.0))
                for n, to in enumerate((C.from_start[:, :, fwd], to_end[:, :, fwd], C.whole[:, :, fwd],
                                        C.from_start[:, :, bwd], to_end[:, :, bwd], C.whole[:, :, bwd])):
                    act.wait_ge(summed, n + 1)
                    steps.done(act.activation(to, sums[n], ACT.Exp))

            @block.tensor
            def _(pe):
                pe.wait_ge(soft, 7)
                for n, (mask, heads) in enumerate(((C.le, fwd), (C.gt, fwd), (C.ones, fwd), (C.ge, bwd), (C.lt, bwd), (C.ones, bwd))):
                    pe.matmul(sums[n], mask[:], C.adt[:, :, heads], start=True, stop=True).then_inc(summed, 1)
    S.clear()


def slot_of(chunk, turn):
    return chunk + seq_of(turn, NT_SAMPLE // 2)


def scan_back(nc, C, S, xb):
    TURNS = NT // 2
    with ExitStack() as ctx:
        sb = lambda n, s: ctx.enter_context(nc.sbuf_tensor("bac_" + n, s, F32))
        rows = sb("rows", [P, 2, SSD + 2 * STATE])
        xw, held = sb("xw", [P, 2, SSD]), sb("held", [P, SSD])
        rows_here = [S(f"rows_here{j}") for j in range(2)]
        weighted, states, carried, held_ready = (S(n) for n in ("weighted", "states", "carried", "held_ready"))
        wide = lambda t: t.rearrange("p a h -> p (a h)").unsqueeze(2).to_broadcast([P, HEADS, HD])
        by_head = lambda t: t.rearrange("p (h d) -> p h d", h=HEADS)
        back = slice(HEADS, 2 * HEADS)
        with nc.Block() as block:
            @block.sync
            def _(sp):
                with sp.Fori(0, TURNS) as t:
                    for j in range(2):
                        row = sp.snap((NT - 1 - t * 2 - j) * P)
                        sp.wait_ge(states, t * 2)
                        sp.nop(nofuse=True)
                        sp.wait_ge(weighted, t * 2)
                        sp.nop(nofuse=True)
                        sp.dma_start(rows[:, j, :], xb[bass.ds(row, P), :]).then_inc(rows_here[j], 16)

            @block.gpsimd
            def _(pool):
                with pool.Fori(0, TURNS) as t:
                    for j in range(2):
                        c = pool.snap(NT - 1 - t * 2 - j)
                        pool.wait_ge(rows_here[j], t * 16 + 16)
                        pool.nop(nofuse=True)
                        pool.wait_ge(states, t * 2)
                        pool.nop(nofuse=True)
                        pool.tensor_tensor(by_head(xw[:, j, :]), by_head(rows[:, j, 0:SSD]),
                                           wide(C.dt_to_end[:, bass.ds(c, 1), back]), ALU.mult).then_inc(weighted, 1)

            @block.tensor
            def _(pe):
                with pe.Fori(0, TURNS) as t:
                    for j in range(2):
                        pe.wait_ge(weighted, t * 2 + j + 1)
                        pe.wait_ge(carried, t * 2)
                        for g in range(2):
                            mul = pe.matmul(C.bank[j][:, g * 256:(g + 1) * 256], rows[:, j, SSD + g * STATE:SSD + (g + 1) * STATE],
                                            xw[:, j, g * 256:(g + 1) * 256], start=True, stop=True)
                        mul.then_inc(states, 1)

            @block.vector
            def _(dve):
                dve.memset(C.h_back[:, bass.ds(NT_SAMPLE, 1), :], 0.0).then_inc(held_ready, 1)
                dve.memset(C.h_back[:, bass.ds(NT + 1, 1), :], 0.0).then_inc(held_ready, 1)
                dve.wait_ge(held_ready, 2)
                with dve.Fori(0, TURNS) as t:
                    for j in range(2):
                        m = t * 2 + j
                        c = dve.snap(NT - 1 - m)
                        slot = dve.snap(c + seq_of(TURNS - 1 - t, NT_SAMPLE // 2))
                        dve.wait_ge(carried, m)
                        dve.nop(nofuse=True)
                        dve.tensor_tensor(by_head(held[:]), by_head(C.h_back[:, bass.ds(slot + 1, 1), :].rearrange("p a n -> p (a n)")),
                                          wide(C.whole[:, bass.ds(c, 1), back]), ALU.mult).then_inc(held_ready, 1)
                        dve.wait_ge(held_ready, m + 3)
                        dve.wait_ge(states, m + 1)
                        dve.nop(nofuse=True)
                        dve.tensor_tensor(C.h_back[:, bass.ds(slot, 1), :].rearrange("p a n -> p (a n)"), held[:], C.bank[j][:, :],
                                          ALU.add).then_inc(carried, 1)
    S.clear()


def scan_forward(nc, C, S, xb, bc, zs, d_skip, y_ssd):
    with ExitStack() as ctx:
        sb = lambda n, s: ctx.enter_context(nc.sbuf_tensor("fwd_" + n, s, F32))
        h_fore = sb("h_fore", [P, NT + 2, SSD])
        rows, chan, z = sb("rows", [P, 2, SSD + 2 * STATE]), sb("chan", [P, 2, 4, P]), sb("z", [P, 2, SSD])
        sums_f, sums_b = sb("sums_f", [P, HEADS, P]), sb("sums_b", [P, HEADS, P])
        decay, mix = sb("decay", [P, HEADS, P]), sb("mix", [P, 2, HEADS, P])
        weight, weight_b = sb("weight", [P, HEADS, P]), sb("weight_b", [P, HEADS, P])
        xw, skip, held = sb("xw", [P, 2, SSD]), sb("skip", [P, 2, SSD]), sb("held", [P, SSD])
        y, off, off_b = sb("y", [P, 2, SSD]), sb("off", [P, 2, SSD]), sb("off_b", [P, SSD])
        square, total, root = sb("square", [P, SSD]), sb("total", [P, 2]), sb("root", [P, 2])
        d = sb("d", [P, HEADS])
        cb, seg, self_y, fore_y, back_y, states = (C.bank[0], C.bank[1:3], C.bank[3], C.bank[4], C.bank[5], C.bank[6:8])
        d_here, cleared, masked, expd, skipped, xw_ready, rooted, squared = (
            S(n) for n in ("d_here", "cleared", "masked", "expd", "skipped", "xw_ready", "rooted", "squared"))
        cb_mm, seg_mm, self_mm, off_mm, states_mm = (S(n) for n in ("cb_mm", "seg_mm", "self_mm", "off_mm", "states_mm"))
        weighted, mixed, off_read, carried, summed, normed = (
            S(n) for n in ("weighted", "mixed", "off_read", "carried", "summed", "normed"))
        rows_here, chan_here, z_here, stored = ([S(f"{n}{j}") for j in range(2)] for n in ("rows_here", "chan_here", "z_here", "stored"))
        by_head = lambda t: t.rearrange("p (h d) -> p h d", h=HEADS)
        wide = lambda t, n: t.rearrange("p a h -> p (a h)").unsqueeze(2).to_broadcast([P, HEADS, n])
        tri = lambda t: t[:].unsqueeze(1).to_broadcast([P, HEADS, P])
        flat = lambda a: a.rearrange("p a n -> p (a n)")
        fwd, bwd = slice(0, HEADS), slice(HEADS, 2 * HEADS)
        one = lambda n: bass.ds(n, 1) if not isinstance(n, int) else slice(n, n + 1)
        slot_of_chunk = lambda m: m if isinstance(m, int) else m + seq_of(m, NT_SAMPLE)
        piece = lambda m: bass.ds(m * P, P) if not isinstance(m, int) else slice(m * P, (m + 1) * P)

        later = lambda m: not isinstance(m, int) or m >= 2

        def chunks(eng, body):
            with eng.Fori(1, NT // 2) as t:
                for j in range(2):
                    body(t * 2 + j, j)

        with nc.Block() as block:
            @block.sync
            def _(sp):
                def load(m, j, later=True):
                    if later:
                        sp.wait_ge(self_mm, m - 1)
                        sp.nop(nofuse=True)
                    sp.dma_start(rows[:, j, :], xb[piece(m), :]).then_inc(rows_here[j], 16)
                    sp.dma_start(chan[:, j], bc[:, :, piece(m)].rearrange("c p n -> p c n")).then_inc(chan_here[j], 16)
                    if later:
                        sp.wait_ge(summed, (m - 1) * 2)
                        sp.nop(nofuse=True)
                    sp.dma_start(z[:, j, :], zs[piece(m), :]).then_inc(z_here[j], 16)

                def store(m, j):
                    sp.wait_ge(normed, m + 1)
                    sp.nop(nofuse=True)
                    sp.dma_start(y_ssd[piece(m), :], y[:, j, :]).then_inc(stored[j], 16)

                load(0, 0, later=False)
                load(1, 1, later=False)
                sp.dma_start(d[:], d_skip.to_broadcast([P, HEADS])).then_inc(d_here, 16)

                def chunk(m, j):
                    load(m, j)
                    store(m - 2, j)
                chunks(sp, chunk)
                store(NT - 2, 0)
                store(NT - 1, 1)
                for j in range(2):
                    sp.wait_ge(stored[j], 16 * NT // 2)

            @block.gpsimd
            def _(pool):
                def prepare(m, j):
                    pool.wait_ge(seg_mm, m)
                    pool.nop(nofuse=True)
                    pool.tensor_tensor(sums_f[:], tri(C.le), wide(C.adt[:, one(m), fwd], P), ALU.mult).then_inc(masked, 1)
                    pool.tensor_tensor(sums_b[:], tri(C.ge), wide(C.adt[:, one(m), bwd], P), ALU.mult).then_inc(masked, 1)
                    pool.wait_ge(rows_here[j], m // 2 * 16 + 16)
                    pool.nop(nofuse=True)
                    if later(m):
                        pool.wait_ge(self_mm, m - 1)
                        pool.nop(nofuse=True)
                    pool.tensor_tensor(by_head(xw[:, j, :]), by_head(rows[:, j, 0:SSD]),
                                       wide(C.dt_to_end[:, one(m), fwd], HD), ALU.mult).then_inc(xw_ready, 1)
                    pool.tensor_tensor(by_head(skip[:, j, :]), by_head(rows[:, j, 0:SSD]),
                                       d[:].unsqueeze(2).to_broadcast([P, HEADS, HD]), ALU.mult).then_inc(skipped, 1)

                def find_root(m, j):
                    pool.wait_ge(squared, m + 1)
                    pool.nop(nofuse=True)
                    pool.tensor_scalar(root[:, j:j + 1], total[:, j:j + 1], 1.0 / SSD, EPS, ALU.mult, ALU.add).then_inc(rooted, 1)
                    pool.wait_ge(rooted, m * 2 + 1)
                    pool.tensor_tensor(root[:, j:j + 1], root[:, j:j + 1], C.minus_half[:], ALU.pow).then_inc(rooted, 1)

                pool.wait_ge(d_here, 16)
                prepare(0, 0)
                prepare(1, 1)

                def chunk(m, j):
                    prepare(m, j)
                    find_root(m - 2, j)
                chunks(pool, chunk)
                find_root(NT - 2, 0)
                find_root(NT - 1, 1)

            @block.tensor
            def _(pe):
                def start(m, j):
                    pe.wait_ge(expd, m * 2)
                    pe.wait_ge(masked, m * 2 + 2)
                    for q in range(2):
                        heads = slice(q * 4, q * 4 + 4)
                        pe.matmul(seg[q][:, :], C.gt[:], sums_f[:, heads, :], start=True, stop=False)
                        mul = pe.matmul(seg[q][:, :], C.lt[:], sums_b[:, heads, :], start=False, stop=True)
                    mul.then_inc(seg_mm, 1)
                    pe.wait_ge(xw_ready, m + 1)
                    if later(m):
                        pe.wait_ge(carried, (m - 1) * 2)
                    for g in range(2):
                        mul = pe.matmul(states[j][:, g * 256:(g + 1) * 256], rows[:, j, SSD + g * STATE:SSD + (g + 1) * STATE],
                                        xw[:, j, g * 256:(g + 1) * 256], start=True, stop=True)
                    mul.then_inc(states_mm, 1)
                    pe.wait_ge(chan_here[j], m // 2 * 16 + 16)
                    pe.wait_ge(mixed, m * 2)
                    for g in range(2):
                        mul = pe.matmul(cb[:, g * P:(g + 1) * P], chan[:, j, g, :], chan[:, j, 2 + g, :], start=True, stop=True)
                    mul.then_inc(cb_mm, 1)

                def enter(m, j):
                    pe.wait_ge(cleared, 2)
                    pe.wait_ge(carried, m * 2)
                    pe.wait_ge(off_read, m * 3)
                    pe.nop(nofuse=True)
                    slot = slot_of_chunk(m)
                    for bank, held_in, at in ((back_y, C.h_back, slot + 1), (fore_y, h_fore, slot)):
                        for g in range(2):
                            mul = pe.matmul(bank[:, g * 256:(g + 1) * 256], chan[:, j, 2 + g, :],
                                            flat(held_in[:, one(at), g * 256:(g + 1) * 256]), start=True, stop=True)
                    mul.then_inc(off_mm, 1)

                def within(m, j, first=False):
                    pe.wait_ge(skipped, m + 1)
                    if not first:
                        pe.wait_ge(summed, m * 2)
                    pe.matmul(self_y[:, :], C.ident[:], skip[:, j, :], start=True, stop=False)
                    pe.wait_ge(mixed, (m + 1) * 2)
                    for h in range(HEADS):
                        mul = pe.matmul(self_y[:, h * HD:(h + 1) * HD], mix[:, j, h, :], rows[:, j, h * HD:(h + 1) * HD],
                                        start=False, stop=h == HEADS - 1)
                    mul.then_inc(self_mm, 1)

                start(0, 0)
                enter(0, 0)
                start(1, 1)
                within(0, 0, first=True)
                enter(1, 1)

                def chunk(m, j):
                    start(m, j)
                    within(m - 1, 1 - j)
                    enter(m, j)
                chunks(pe, chunk)
                within(NT - 1, 1)

            @block.scalar
            def _(act):
                def exps(m):
                    act.wait_ge(seg_mm, m + 1)
                    act.wait_ge(mixed, m * 2)
                    for q in range(2):
                        act.activation(decay[:, q * 4:q * 4 + 4, :], seg[q][:, :].rearrange("p (h n) -> p h n", h=4),
                                       ACT.Exp).then_inc(expd, 1)

                def squares(m, j):
                    act.wait_ge(summed, (m + 1) * 2)
                    if later(m):
                        act.wait_ge(rooted, m * 2 - 2)
                    act.activation(square[:], y[:, j, :], ACT.Square, accum_out=total[:, j:j + 1]).then_inc(squared, 1)

                exps(0)
                exps(1)
                squares(0, 0)

                def chunk(m, j):
                    exps(m)
                    squares(m - 1, 1 - j)
                chunks(act, chunk)
                squares(NT - 1, 1)

            @block.vector
            def _(dve):
                def begin(m, j, scale_last=True):
                    at = one(m)
                    slot = dve.snap(slot_of_chunk(m)) if not isinstance(m, int) else m
                    dve.tensor_tensor(weight[:], tri(C.le), wide(C.dt[:, at, fwd], P), ALU.mult).then_inc(weighted, 1)
                    dve.tensor_tensor(weight_b[:], tri(C.ge), wide(C.dt[:, at, bwd], P), ALU.mult).then_inc(weighted, 1)
                    if scale_last:
                        scale(m - 2, j)
                    dve.wait_ge(carried, m * 2)
                    dve.nop(nofuse=True)
                    dve.tensor_tensor(by_head(held[:]), by_head(flat(h_fore[:, one(slot), :])), wide(C.whole[:, at, fwd], HD),
                                      ALU.mult).then_inc(carried, 1)
                    dve.wait_ge(weighted, m * 3 + 2)
                    dve.tensor_tensor(weight[:], weight[:], weight_b[:], ALU.add).then_inc(weighted, 1)
                    dve.wait_ge(states_mm, m + 1)
                    dve.wait_ge(carried, m * 2 + 1)
                    dve.nop(nofuse=True)
                    dve.tensor_tensor(flat(h_fore[:, one(slot + 1), :]), held[:], states[j][:, :], ALU.add).then_inc(carried, 1)
                    dve.wait_ge(expd, m * 2 + 2)
                    dve.wait_ge(weighted, m * 3 + 3)
                    dve.tensor_tensor(decay[:], decay[:], weight[:], ALU.mult).then_inc(mixed, 1)
                    dve.wait_ge(off_mm, m + 1)
                    dve.nop(nofuse=True)
                    dve.tensor_tensor(by_head(off[:, j, :]), by_head(fore_y[:, :]), wide(C.from_start[:, at, fwd], HD), ALU.mult).then_inc(off_read, 1)
                    dve.wait_ge(cb_mm, m + 1)
                    dve.wait_ge(mixed, m * 2 + 1)
                    if later(m):
                        dve.wait_ge(self_mm, m - 1)
                    dve.tensor_tensor(
                        mix[:, j].rearrange("p (g r) n -> p g r n", g=2), decay[:].rearrange("p (g r) n -> p g r n", g=2),
                        cb[:, 0:2 * P].rearrange("p (g n) -> p g n", g=2).unsqueeze(2).to_broadcast([P, 2, HEADS // 2, P]),
                        ALU.mult).then_inc(mixed, 1)
                    dve.nop(nofuse=True)
                    dve.tensor_tensor(by_head(off_b[:]), by_head(back_y[:, :]), wide(C.from_start[:, at, bwd], HD), ALU.mult).then_inc(off_read, 1)

                def add_self(m, j):
                    dve.wait_ge(self_mm, m + 1)
                    dve.wait_ge(off_read, (m + 1) * 3)
                    if later(m):
                        dve.wait_ge(stored[j], m // 2 * 16)
                    dve.tensor_tensor(y[:, j, :], off[:, j, :], self_y[:, :], ALU.add).then_inc(summed, 1)

                def add_off(m, j):
                    dve.wait_ge(off_read, m * 3 + 2)
                    dve.tensor_tensor(off[:, j, :], off[:, j, :], off_b[:], ALU.add).then_inc(off_read, 1)

                def gate(m, j):
                    dve.wait_ge(z_here[j], m // 2 * 16 + 16)
                    dve.wait_ge(summed, m * 2 + 1)
                    dve.tensor_tensor(y[:, j, :], y[:, j, :], z[:, j, :], ALU.mult).then_inc(summed, 1)

                def scale(m, j):
                    dve.wait_ge(rooted, (m + 1) * 2)
                    dve.nop(nofuse=True)
                    dve.tensor_scalar(y[:, j, :], y[:, j, :], root[:, j:j + 1], None, ALU.mult).then_inc(normed, 1)

                dve.memset(h_fore[:, 0, :], 0.0).then_inc(cleared, 1)
                dve.memset(h_fore[:, NT_SAMPLE + 1, :], 0.0).then_inc(cleared, 1)
                dve.wait_ge(cleared, 2)
                begin(0, 0, scale_last=False)
                add_off(0, 0)
                begin(1, 1, scale_last=False)
                add_self(0, 0)
                add_off(1, 1)
                gate(0, 0)

                def chunk(m, j):
                    begin(m, j)
                    add_self(m - 1, 1 - j)
                    add_off(m, j)
                    gate(m - 1, 1 - j)
                chunks(dve, chunk)
                scale(NT - 2, 0)
                add_self(NT - 1, 1)
                gate(NT - 1, 1)
                scale(NT - 1, 1)
    S.clear()


def s5_tables(nc, C, S, lam_re, lam_im, log_step, b_re, b_im, d_skip):
    PD = PAIRS * 2
    with ExitStack() as ctx:
        sb = lambda n, s, dt=F32: ctx.enter_context(nc.sbuf_tensor("tab_" + n, s, dt))
        lr, li, ls = sb("lr", [P, PD]), sb("li", [P, PD]), sb("ls", [P, PD])
        b = [sb(f"b{n}", [P, PAIRS, CH5]) for n in range(2)]
        v = {n: sb(n, [P, PD]) for n in ("x", "k", "r", "p", "q", "step", "mag", "sin", "cos", "f", "g", "fr", "fi")}
        whole = sb("whole", [P, PD], I32)
        bit = sb("bit", [P, PD], I32)
        power = [sb(f"power{n}", [P, T5 + 1, PD]) for n in range(2)]
        t1, t2 = sb("t1", [P, 8, PD]), sb("t2", [P, 8, PD])
        u1, u2 = sb("u1", [P, PAIRS, 2, CH5]), sb("u2", [P, PAIRS, 2, CH5])
        d5 = ctx.enter_context(nc.sbuf_tensor("tab_d5", [CH5, SSD], F32))
        here, done = S("here"), S("done")
        with nc.Block() as block:
            @block.sync
            def _(sp):
                for to, a in ((lr, lam_re), (li, lam_im), (b[0], b_re), (b[1], b_im)):
                    sp.dma_start(to[:], a).then_inc(here, 16)
                for g in range(2):
                    sp.dma_start(ls[g * N5:(g + 1) * N5, :], log_step[g:g + 1, :].to_broadcast([N5, PD])).then_inc(here, 16)
                sp.dma_start(d5[:], d_skip.to_broadcast([CH5, SSD])).then_inc(here, 16)

            @block.vector
            def _(dve):
                steps = Steps(dve, done)
                ts = lambda o, a, s1, op0, s2=None, op1=ALU.bypass: steps.then(dve.tensor_scalar(o, a, s1, s2, op0, op1))
                tt = lambda o, a, c, op: steps.then(dve.tensor_tensor(o, a, c, op))
                stt = lambda o, a, s, c, op0, op1: steps.then(
                    dve.scalar_tensor_tensor(out=o, in0=a, scalar=s, in1=c, op0=op0, op1=op1))
                A = {n: t[:] for n, t in v.items()}
                ROUND = 12582912.0

                def exp(out, x):
                    ts(A["x"], x, -87.0, ALU.max, 88.0, ALU.min)
                    ts(A["k"], A["x"], 1.44269504, ALU.mult, ROUND, ALU.add)
                    ts(A["k"], A["k"], -ROUND, ALU.add)
                    stt(A["r"], A["k"], -0.693359375, A["x"], ALU.mult, ALU.add)
                    stt(A["r"], A["k"], 2.12194440e-4, A["r"], ALU.mult, ALU.add)
                    ts(A["p"], A["r"], 1.9875691500e-4, ALU.mult)
                    for c in (1.3981999507e-3, 8.3334519073e-3, 4.1665795894e-2, 1.6666665459e-1, 5.0000001201e-1):
                        stt(A["p"], A["p"], c, A["r"], ALU.add, ALU.mult)
                    tt(A["p"], A["p"], A["r"], ALU.mult)
                    tt(A["p"], A["p"], A["r"], ALU.add)
                    ts(A["p"], A["p"], 1.0, ALU.add)
                    ts(A["k"], A["k"], 127.0, ALU.add)
                    steps.then(dve.tensor_copy(whole[:], A["k"]))
                    ts(whole[:], whole[:], 23, ALU.logical_shift_left)
                    tt(out, A["p"], whole[:].bitcast(F32), ALU.mult)

                dve.wait_ge(here, 16 * 7)
                tt(C.d5_diag[:], d5[:].rearrange("p (g i) -> p g i", i=CH5),
                   C.ident[0:CH5, 0:CH5].unsqueeze(1).to_broadcast([CH5, G5, CH5]), ALU.mult)
                ts(lr[:], lr[:], -1e-4, ALU.min)
                exp(A["step"], ls[:])
                tt(A["q"], lr[:], A["step"], ALU.mult)
                exp(A["mag"], A["q"])
                tt(A["x"], li[:], A["step"], ALU.mult)
                ts(A["k"], A["x"], 0.63661977, ALU.mult, ROUND, ALU.add)
                ts(A["k"], A["k"], -ROUND, ALU.add)
                stt(A["r"], A["k"], -1.5703125, A["x"], ALU.mult, ALU.add)
                stt(A["r"], A["k"], -4.837512969970703e-4, A["r"], ALU.mult, ALU.add)
                stt(A["r"], A["k"], -7.549789948768648e-8, A["r"], ALU.mult, ALU.add)
                tt(A["q"], A["r"], A["r"], ALU.mult)
                ts(A["p"], A["q"], -1.9515295891e-4, ALU.mult, 8.3321608736e-3, ALU.add)
                tt(A["p"], A["p"], A["q"], ALU.mult)
                stt(A["p"], A["p"], -1.6666654611e-1, A["q"], ALU.add, ALU.mult)
                tt(A["p"], A["p"], A["r"], ALU.mult)
                tt(A["sin"], A["p"], A["r"], ALU.add)
                ts(A["p"], A["q"], 2.443315711809948e-5, ALU.mult, -1.388731625493765e-3, ALU.add)
                tt(A["p"], A["p"], A["q"], ALU.mult)
                stt(A["p"], A["p"], 4.166664568298827e-2, A["q"], ALU.add, ALU.mult)
                tt(A["p"], A["p"], A["q"], ALU.mult)
                stt(A["p"], A["q"], -0.5, A["p"], ALU.mult, ALU.add)
                ts(A["cos"], A["p"], 1.0, ALU.add)
                steps.then(dve.tensor_copy(whole[:], A["k"]))
                ts(bit[:], whole[:], 1, ALU.bitwise_and)
                steps.then(dve.tensor_copy(A["f"], bit[:]))
                ts(A["g"], A["f"], -1.0, ALU.mult, 1.0, ALU.add)
                tt(A["x"], A["sin"], A["g"], ALU.mult)
                tt(A["p"], A["cos"], A["f"], ALU.mult)
                tt(A["x"], A["x"], A["p"], ALU.add)
                tt(A["p"], A["cos"], A["g"], ALU.mult)
                tt(A["q"], A["sin"], A["f"], ALU.mult)
                tt(A["p"], A["p"], A["q"], ALU.add)
                for of, out, by_k in ((A["x"], A["sin"], 0.0), (A["p"], A["cos"], 1.0)):
                    ts(A["r"], A["k"], by_k, ALU.add)
                    steps.then(dve.tensor_copy(whole[:], A["r"]))
                    ts(bit[:], whole[:], 2, ALU.bitwise_and)
                    steps.then(dve.tensor_copy(A["f"], bit[:]))
                    ts(A["f"], A["f"], -1.0, ALU.mult, 1.0, ALU.add)
                    tt(A["f"], A["f"], A["mag"], ALU.mult)
                    tt(out, of, A["f"], ALU.mult)
                ts(power[0][:, 0, :], A["cos"], 0.0, ALU.mult, 1.0, ALU.add)
                ts(power[1][:, 0, :], A["cos"], 0.0, ALU.mult)
                steps.then(dve.tensor_copy(power[0][:, 1, :], A["cos"]))
                steps.then(dve.tensor_copy(power[1][:, 1, :], A["sin"]))
                n = 1
                while n < T5:
                    by = [power[c][:, n:n + 1, :].to_broadcast([P, n, PD]) for c in range(2)]
                    x = [power[c][:, 1:n + 1, :] for c in range(2)]
                    for out, op, pairs in ((0, ALU.subtract, ((0, 0), (1, 1))), (1, ALU.add, ((0, 1), (1, 0)))):
                        for t, (p, q) in zip((t1, t2), pairs):
                            tt(t[:, 0:n, :], x[p], by[q], ALU.mult)
                        tt(power[out][:, n + 1:2 * n + 1, :], t1[:, 0:n, :], t2[:, 0:n, :], op)
                    n *= 2
                for c in range(2):
                    w = power[c][:].rearrange("p q (a d) -> p a d q", d=2)
                    steps.then(dve.tensor_copy(C.power_w[c][:, :, 0, :], w[:, :, 0, 0:T5]))
                    steps.then(dve.tensor_copy(C.power_w[c][:, :, 1, :], w[:, :, 1, T5 - 1::-1]))
                    steps.then(dve.tensor_copy(C.power_y[c][:, :, 0, :], w[:, :, 0, :]))
                    steps.then(dve.tensor_copy(C.power_y[c][:, :, 1, :], w[:, :, 1, ::-1]))
                    steps.then(dve.tensor_copy(C.carry_re[:, c, :], power[0][:, T5, :]))
                ts(C.carry_im[:, 0, :], power[1][:, T5, :], -1.0, ALU.mult)
                steps.then(dve.tensor_copy(C.carry_im[:, 1, :], power[1][:, T5, :]))
                ts(A["cos"], A["cos"], -1.0, ALU.add)
                tt(A["x"], lr[:], lr[:], ALU.mult)
                tt(A["p"], li[:], li[:], ALU.mult)
                tt(A["x"], A["x"], A["p"], ALU.add)
                steps.then(dve.reciprocal(A["x"], A["x"]))
                for out, op, (p, q) in (("fr", ALU.add, (("cos", lr), ("sin", li))), ("fi", ALU.subtract, (("sin", lr), ("cos", li)))):
                    tt(A["q"], A[p[0]], p[1][:], ALU.mult)
                    tt(A["p"], A[q[0]], q[1][:], ALU.mult)
                    tt(A["q"], A["q"], A["p"], op)
                    tt(A[out], A["q"], A["x"], ALU.mult)
                f = [A[n].rearrange("p (a d) -> p a d", d=2).unsqueeze(3).to_broadcast([P, PAIRS, 2, CH5]) for n in ("fr", "fi")]
                bb = [t[:].unsqueeze(2).to_broadcast([P, PAIRS, 2, CH5]) for t in b]
                for out, op, (p, q) in ((0, ALU.subtract, ((0, 0), (1, 1))), (1, ALU.add, ((0, 1), (1, 0)))):
                    tt(u1[:], f[p[0]], bb[p[1]], ALU.mult)
                    tt(u2[:], f[q[0]], bb[q[1]], ALU.mult)
                    tt(C.b_bar[:, :, out], u1[:], u2[:], op)
    S.clear()


def s5_states_in(nc, C, S, u, turned_dram):
    TURNS = PAIRS // 2
    BOTH = 2 * T5 * CH5
    with ExitStack() as ctx:
        sb = lambda n, s: ctx.enter_context(nc.sbuf_tensor("sin_" + n, s, F32))
        us, up = sb("us", [C_S, T5, SSD]), sb("up", [C_P, T5, SSD])
        ps, pp = sb("ps", [C_S, 2, BOTH]), sb("pp", [C_P, 2, BOTH])
        ut = sb("ut", [P, 2, 2, HALF, C_ALL])
        pre = sb("pre", [P, 2, 2, 2, T5 * CH5])
        w = sb("w", [P, 2, 2, HALF, 2, P])
        t1, t2 = sb("t1", [P, 2, T5 * CH5]), sb("t2", [P, 2, T5 * CH5])
        u_here, picked_s, picked_p, made, dve_made, turned, ut_ready, turned_w, w_ready, added, read_out = (
            S(n) for n in ("u_here", "picked_s", "picked_p", "made", "dve_made", "turned", "ut_ready", "turned_w", "w_ready", "added", "read_out"))
        stored = [S(f"stored{j}") for j in range(2)]
        PRE = 6
        ub, wb, xb_ = C.bank[0:2], C.bank[2:4], C.bank[4:6]
        with nc.Block() as block:
            @block.sync
            def _(sp):
                sp.dma_start(us[:], u[0:SAMPLE, :].rearrange("(c t) n -> c t n", t=T5)).then_inc(u_here, 16)
                sp.dma_start(up[:], u[SAMPLE:TOK, :].rearrange("(c t) n -> c t n", t=T5)).then_inc(u_here, 16)
                with sp.Fori(0, TURNS) as t:
                    for j in range(2):
                        sp.wait_ge(ut_ready, t * 4 + j * 2 + 2)
                        sp.nop(nofuse=True)
                        sp.dma_start(turned_dram[bass.ds(t * 2 + j, 1)].rearrange("a p n -> p (a n)"),
                                     ut[:, j].rearrange("p g k c -> p (g k c)")).then_inc(stored[j], 16)
                for j in range(2):
                    sp.wait_ge(stored[j], 16 * TURNS)

            @block.gpsimd
            def _(pool):
                pool.wait_ge(u_here, 32)
                with pool.Fori(0, TURNS) as t:
                    for j in range(2):
                        a = pool.snap((t * 2 + j) * 2 * CH5)
                        pool.wait_ge(turned, t * 2)
                        pool.nop(nofuse=True)
                        for g in range(2):
                            put = pool.tensor_copy(pp[:, j, g * T5 * CH5:(g + 1) * T5 * CH5].rearrange("p (t i) -> p t i", i=CH5)[:, ::-1],
                                                   up[:, :, bass.ds(a + g * CH5, CH5)])
                        put.then_inc(picked_p, 1)

            @block.vector
            def _(dve):
                dve.wait_ge(u_here, 32)
                with dve.Fori(0, TURNS) as t:
                    steps = Steps(dve, dve_made, t, 2 * PRE)
                    for j in range(2):
                        n = dve.snap(t * 2 + j)
                        a = dve.snap(n * 2 * CH5)
                        dve.wait_ge(turned, t * 2)
                        dve.nop(nofuse=True)
                        for g in range(2):
                            put = dve.tensor_copy(ps[:, j, g * T5 * CH5:(g + 1) * T5 * CH5].rearrange("p (t i) -> p t i", i=CH5)[:, ::-1],
                                                  us[:, :, bass.ds(a + g * CH5, CH5)])
                        put.then_inc(picked_s, 1)
                        dve.wait_ge(turned_w, t * 2)
                        dve.nop(nofuse=True)
                        power = [C.power_w[c][:, bass.ds(n, 1)].rearrange("p a d t -> p (a d) t").unsqueeze(3).to_broadcast([P, 2, T5, CH5]) for c in range(2)]
                        b = [C.b_bar[:, bass.ds(n, 1), c].rearrange("p a d i -> p (a d) i").unsqueeze(2).to_broadcast([P, 2, T5, CH5]) for c in range(2)]
                        four = lambda x: x.rearrange("p d (t i) -> p d t i", i=CH5)
                        for out, op, (p, q) in ((0, ALU.subtract, ((0, 0), (1, 1))), (1, ALU.add, ((0, 1), (1, 0)))):
                            steps.done(dve.tensor_tensor(four(t1[:]), power[p[0]], b[p[1]], ALU.mult))
                            steps.then(dve.tensor_tensor(four(t2[:]), power[q[0]], b[q[1]], ALU.mult))
                            steps.then(dve.tensor_tensor(pre[:, j, out], t1[:], t2[:], op))
                        dve.wait_ge(added, t * 2 + j + 1)
                        dve.nop(nofuse=True)
                        for d in range(2):
                            way = slice(None, None, -1) if d else slice(None)
                            x = xb_[d][:, 0:2 * C_ALL].rearrange("p (r c) -> p c r", r=2)
                            to = C.states[:, :, :, :, bass.ds(n * 2 + d, 1)].rearrange("p k r s a -> p k r (s a)")
                            dve.tensor_copy(to[:, 0:C_S, :, 0], x[:, 0:C_S, :][:, way, :])
                            put = dve.tensor_copy(to[:, 0:C_P, :, 1], x[:, C_S:C_ALL, :][:, way, :])
                        put.then_inc(read_out, 1)
                    steps.end_turn()

            @block.tensor
            def _(pe):
                with pe.Fori(0, TURNS) as t:
                    for j in range(2):
                        m = t * 2 + j
                        pe.wait_ge(picked_s, m + 1)
                        pe.wait_ge(picked_p, m + 1)
                        pe.wait_ge(ut_ready, m * 2)
                        for g in range(2):
                            for k in range(HALF):
                                n = g * HALF + k
                                pe.transpose(ub[0][:, n * C_S:(n + 1) * C_S], ps[:, j, n * P:(n + 1) * P], C.ident[0:C_S, 0:C_S])
                                tr = pe.transpose(ub[1][:, n * C_P:(n + 1) * C_P], pp[:, j, n * P:(n + 1) * P], C.ident[0:C_P, 0:C_P])
                        tr.then_inc(turned, 1)
                        pe.wait_ge(dve_made, (m + 1) * PRE)
                        pe.wait_ge(w_ready, m * 2)
                        for r in range(2):
                            for k in range(HALF):
                                for d in range(2):
                                    n = k * 2 + d
                                    tr = pe.transpose(wb[r][:, n * P:(n + 1) * P], pre[:, j, r, d, k * P:(k + 1) * P], C.ident[:])
                        tr.then_inc(turned_w, 1)
                        pe.wait_ge(ut_ready, m * 2 + 2)
                        pe.wait_ge(w_ready, m * 2 + 2)
                        pe.wait_ge(read_out, m)
                        for d in range(2):
                            for r in range(2):
                                for g in range(2):
                                    for k in range(HALF):
                                        mul = pe.matmul(xb_[d][g * N5:(g + 1) * N5, r * C_ALL:(r + 1) * C_ALL],
                                                        w[:, j, r, k, d, g * N5:(g + 1) * N5], ut[:, j, g, k, :],
                                                        start=k == 0, stop=k == HALF - 1)
                        mul.then_inc(added, 1)

            @block.scalar
            def _(act):
                with act.Fori(0, TURNS) as t:
                    for j in range(2):
                        m = t * 2 + j
                        act.wait_ge(turned, m + 1)
                        act.wait_ge(stored[j], t * 16)
                        act.wait_ge(added, t * 2)
                        for s, (at, n) in enumerate(((0, C_S), (C_S, C_P))):
                            act.activation(ut[:, j, :, :, at:at + n].rearrange("p g k c -> p (g k) c"),
                                           ub[s][:, 0:4 * n].rearrange("p (a c) -> p a c", c=n), ACT.Copy).then_inc(ut_ready, 1)
                        act.wait_ge(turned_w, m + 1)
                        for r in range(2):
                            act.activation(w[:, j, r].rearrange("p k d n -> p (k d n)"), wb[r][:, :], ACT.Copy).then_inc(w_ready, 1)
    S.clear()


def s5_carry(dve, C, done, t1, t2):
    before = 0
    for lo, hi, seqs in ((1, C_P, 2), (C_P, C_S, 1)):
        by = lambda t: t[:].unsqueeze(2).to_broadcast([P, 2, seqs, 2 * PAIRS])
        with dve.Fori(lo, hi) as k:
            steps = Steps(dve, done, k - lo, 4, before)
            at = lambda n: C.states[:, bass.ds(n, 1), :, 0:seqs, :].rearrange("p k r s n -> p (k r) s n")
            last, here = at(k - 1), at(k)
            steps.done(dve.tensor_tensor(t1[:, :, 0:seqs, :], by(C.carry_re), last, ALU.mult))
            steps.then(dve.tensor_tensor(t2[:, ::-1, 0:seqs, :], by(C.carry_im)[:, ::-1], last, ALU.mult))
            steps.then(dve.tensor_tensor(t1[:, :, 0:seqs, :], t1[:, :, 0:seqs, :], t2[:, :, 0:seqs, :], ALU.add))
            steps.then(dve.tensor_tensor(here, here, t1[:, :, 0:seqs, :], ALU.add))
            steps.end_turn()
        before += 4 * (hi - lo)


def s5_outputs(nc, C, S, turned_dram, kernels, c_re, c_im, yg):
    TURNS = PAIRS // 2
    Q = T5 + 1
    TC = T5 * CH5
    LAGS = 2 * T5 - 1
    with ExitStack() as ctx:
        sb = lambda n, s: ctx.enter_context(nc.sbuf_tensor("out5_" + n, s, F32))
        c = [sb(f"c{n}", [P, PAIRS, 2, CH5]) for n in range(2)]
        e = sb("e", [P, 2, 2, 2, 2, Q * CH5])
        t1, t2 = sb("t1", [P, 2, Q * CH5]), sb("t2", [P, 2, Q * CH5])
        bs = sb("bs", [P, 2, 2, 2, CH5])
        lags = sb("lags", [CH5, 2, 2, LAGS * CH5])
        toe = sb("toe", [P, 2, 2, HALF, TC])
        ut = sb("ut", [P, 2, 2, HALF, C_ALL])
        st = sb("st", [P, 2, 2, 2, C_ALL])
        ys, yp = sb("ys", [C_S, T5, SSD]), sb("yp", [C_P, T5, SSD])
        c_here, dve_made, b_picked, zeroed, entered, kernel_mm, lag_steps, y_mm, gelued, out = (
            S(n) for n in ("c_here", "dve_made", "b_picked", "zeroed", "entered", "kernel_mm", "lag_steps", "y_mm", "gelued", "out"))
        lags_stored, toe_here, ut_here = ([S(f"{n}{j}") for j in range(2)] for n in ("lags_stored", "toe_here", "ut_here"))
        kf, kb = C.bank[0:2]
        yb = C.bank[2:6]
        PRE, LAG = 8, 4
        with nc.Block() as block:
            @block.sync
            def _(sp):
                sp.dma_start(c[0][:], c_re).then_inc(c_here, 16)
                sp.dma_start(c[1][:], c_im).then_inc(c_here, 16)
                with sp.Fori(0, TURNS) as t:
                    for j in range(2):
                        n = sp.snap(t * 2 + j)
                        sp.wait_ge(y_mm, t * 4)
                        sp.nop(nofuse=True)
                        sp.dma_start(ut[:, j].rearrange("p g k c -> p (g k c)"),
                                     turned_dram[bass.ds(n, 1)].rearrange("a p n -> p (a n)")).then_inc(ut_here[j], 16)
                    for j in range(2):
                        sp.wait_ge(lag_steps, (t * 2 + j + 1) * LAG)
                        sp.nop(nofuse=True)
                        sp.dma_start(kernels[j].rearrange("g i n -> i g n"), lags[:, j]).then_inc(lags_stored[j], 16)
                        sp.wait_ge(lags_stored[j], t * 16 + 16)
                        sp.nop(nofuse=True)
                        for g in range(2):
                            for k in range(HALF):
                                rows = bass.AP(tensor=kernels.tensor, offset=((j * 2 + g) * CH5 * LAGS * CH5) + k * SPK * CH5,
                                               ap=[[CH5, SPK], [LAGS * CH5, CH5], [1, TC]])
                                sp.dma_start(toe[:, j, g, k, :], rows).then_inc(toe_here[j], 16)
                sp.wait_ge(gelued, 2 * PAIRS)
                sp.dma_start(yg[0:SAMPLE, :].rearrange("(c t) n -> c t n", t=T5), ys[:]).then_inc(out, 16)
                sp.dma_start(yg[SAMPLE:TOK, :].rearrange("(c t) n -> c t n", t=T5), yp[:]).then_inc(out, 16)
                sp.wait_ge(out, 32)

            @block.gpsimd
            def _(pool):
                pool.memset(e[:], 0.0).then_inc(zeroed, 1)
                pool.memset(st[:], 0.0).then_inc(zeroed, 1)
                pool.wait_ge(zeroed, 2)
                with pool.Fori(0, TURNS) as t:
                    for j in range(2):
                        n = pool.snap(t * 2 + j)
                        pool.wait_ge(kernel_mm, t * 2)
                        pool.nop(nofuse=True)
                        pool.tensor_copy(bs[:, j], C.b_bar[:, bass.ds(n, 1)].rearrange("p a r d i -> p (a r) d i")).then_inc(b_picked, 1)
                        pool.wait_ge(y_mm, t * 4)
                        pool.nop(nofuse=True)
                        for d in range(2):
                            x = C.states[:, :, :, :, bass.ds(n * 2 + d, 1)].rearrange("p k r s a -> p r k (s a)")
                            for s, (at, m) in enumerate(((0, C_S), (C_S, C_P))):
                                if d == 0:
                                    put = pool.tensor_copy(st[:, j, :, d, at + 1:at + m], x[:, :, 0:m - 1, s])
                                else:
                                    put = pool.tensor_copy(st[:, j, :, d, at:at + m - 1][:, :, ::-1], x[:, :, 0:m - 1, s])
                        put.then_inc(entered, 1)

            @block.vector
            def _(dve):
                dve.wait_ge(c_here, 32)
                dve.wait_ge(zeroed, 1)
                with dve.Fori(0, TURNS) as t:
                    steps = Steps(dve, dve_made, t, 2 * PRE)
                    lag = Steps(dve, lag_steps, t, 2 * LAG)
                    for j in range(2):
                        n = dve.snap(t * 2 + j)
                        dve.wait_ge(y_mm, t * 4)
                        dve.nop(nofuse=True)
                        four = lambda x: x.rearrange("p d (q i) -> p d q i", i=CH5)
                        power = [C.power_y[r][:, bass.ds(n, 1)].rearrange("p a d q -> p (a d) q").unsqueeze(3).to_broadcast([P, 2, Q, CH5]) for r in range(2)]
                        cc = [c[r][:, bass.ds(n, 1)].rearrange("p a d i -> p (a d) i").unsqueeze(2).to_broadcast([P, 2, Q, CH5]) for r in range(2)]
                        steps.done(dve.tensor_tensor(four(t1[:]), cc[0], power[0], ALU.mult))
                        steps.then(dve.tensor_tensor(four(t2[:]), cc[1], power[1], ALU.mult))
                        for g in range(2):
                            own = slice(g * N5, (g + 1) * N5)
                            steps.done(dve.tensor_tensor(e[own, j, 0, :, g], t1[own], t2[own], ALU.subtract))
                        steps.wait()
                        steps.done(dve.tensor_tensor(four(t1[:]), cc[0], power[1], ALU.mult))
                        steps.then(dve.tensor_tensor(four(t2[:]), cc[1], power[0], ALU.mult))
                        for g in range(2):
                            own = slice(g * N5, (g + 1) * N5)
                            steps.done(dve.scalar_tensor_tensor(out=e[own, j, 1, :, g], in0=t1[own], scalar=-1.0, in1=t2[own],
                                                                op0=ALU.mult, op1=ALU.subtract))
                        steps.wait()
                        dve.wait_ge(kernel_mm, t * 2 + j + 1)
                        dve.wait_ge(lags_stored[j], t * 16)
                        dve.nop(nofuse=True)
                        to = lags[:, j]
                        f, b = (x[0:CH5, :].rearrange("p (g n) -> p g n", g=2) for x in (kf, kb))
                        L0 = (T5 - 1) * CH5
                        lag.done(dve.tensor_copy(to[:, :, 0:L0], b[:, :, 0:L0]))
                        lag.done(dve.tensor_copy(to[:, :, L0 + CH5:], f[:, :, CH5:TC]))
                        lag.then(dve.tensor_tensor(to[:, :, L0:L0 + CH5], f[:, :, 0:CH5], C.d5_diag[:, bass.ds(n * 2, 2), :], ALU.add))
                        lag.then(dve.tensor_tensor(to[:, :, L0:L0 + CH5], b[:, :, L0:TC], to[:, :, L0:L0 + CH5], ALU.add))
                    steps.end_turn()
                    lag.end_turn()

            @block.tensor
            def _(pe):
                with pe.Fori(0, TURNS) as t:
                    for j in range(2):
                        m = t * 2 + j
                        pe.wait_ge(dve_made, (m + 1) * PRE)
                        pe.wait_ge(b_picked, m + 1)
                        pe.wait_ge(lag_steps, m * LAG)
                        for d, bank in enumerate((kf, kb)):
                            for r in range(2):
                                mul = pe.matmul(bank[0:CH5, :].rearrange("p (g n) -> p g n", g=2), bs[:, j, r, d, :],
                                                e[:, j, r, d, :, d * CH5:d * CH5 + TC], start=r == 0, stop=r == 1)
                        mul.then_inc(kernel_mm, 1)
                    for j in range(2):
                        m = t * 2 + j
                        pe.wait_ge(entered, m + 1)
                        pe.wait_ge(ut_here[j], t * 16 + 16)
                        pe.wait_ge(gelued, t * 4)
                        for s, (at, n) in enumerate(((0, C_S), (C_S, C_P))):
                            bank = yb[j * 2 + s][0:n, :]
                            for d in range(2):
                                for r in range(2):
                                    pe.matmul(bank.rearrange("p (g n) -> p g n", g=2), st[:, j, r, d, at:at + n],
                                              e[:, j, r, d, :, (1 - d) * CH5:(1 - d) * CH5 + TC], start=d == 0 and r == 0, stop=False)
                            if s == 0:
                                pe.wait_ge(toe_here[j], (t + 1) * 16 * 2 * HALF)
                            for g in range(2):
                                for k in range(HALF):
                                    mul = pe.matmul(bank[:, g * TC:(g + 1) * TC], ut[:, j, g, k, at:at + n], toe[:, j, g, k, :],
                                                    start=False, stop=g == 1 and k == HALF - 1)
                            mul.then_inc(y_mm, 1)

            @block.scalar
            def _(act):
                with act.Fori(0, TURNS) as t:
                    for j in range(2):
                        m = t * 2 + j
                        cols = act.snap(m * 2 * CH5)
                        for s, (y, n) in enumerate(((ys, C_S), (yp, C_P))):
                            act.wait_ge(y_mm, m * 2 + s + 1)
                            act.nop(nofuse=True)
                            act.activation(y[:, :, bass.ds(cols, 2 * CH5)].rearrange("p t (g i) -> p g t i", g=2),
                                           yb[j * 2 + s][0:n, :].rearrange("p (g t i) -> p g t i", g=2, t=T5), ACT.Gelu_apprx_tanh).then_inc(gelued, 1)
    S.clear()


def load_across(eng, to, row, sem):
    eng.dma_start(to, row.to_broadcast([P, row.shape[-1]])).then_inc(sem, 16)


def mix_out(nc, C, S, y_ssd, yg, x, mod, W, x1_dram, h_dram):
    TURNS = NWIDE // 2
    KY = SSD // P
    EVENTS = 3 * KY
    with ExitStack() as ctx:
        sb = lambda n, s: ctx.enter_context(nc.sbuf_tensor("mix_" + n, s, F32))
        wg, wo, wr = sb("wg", [P, KY, SSD]), sb("wo", [P, KT, D]), sb("wr", [P, KT, NE])
        norm_w, b_glu = sb("norm_w", [P, KY]), sb("b_glu", [P, KY])
        g1, scale, shift = sb("g1", [P, 2, D]), sb("scale", [P, 2, D]), sb("shift", [P, 2, D])
        ln_g, ln_b = sb("ln_g", [P, D]), sb("ln_b", [P, D])
        ya, yb = sb("ya", [P, TPW, SSD]), sb("yb", [P, TPW, SSD])
        xt = sb("xt", [P, 2, TPW, D])
        yt, gt, sg = sb("yt", [P, 2, KT, WIDE]), sb("gt", [P, KY, WIDE]), sb("sg", [P, KY, WIDE])
        v, h, ht = sb("v", [P, 2, D]), sb("h", [P, 2, D]), sb("ht", [P, KT, P])
        stats, mean = sb("stats", [P, 2, 6]), sb("mean", [P, 2, 2])
        flat = lambda a: a.rearrange("p a n -> p (a n)")
        w_here, y_here, one_added, turned, taken, gated, mixed, mix_read, ln, rooted, h_made = (
            S(n) for n in ("w_here", "y_here", "one_added", "turned", "taken", "gated", "mixed", "mix_read", "ln", "rooted", "h_made"))
        h_turned, h_taken, routed, kept = (S(n) for n in ("h_turned", "h_taken", "routed", "kept"))
        x_here, x1_stored, h_stored = ([S(f"{n}{j}") for j in range(2)] for n in ("x_here", "x1_stored", "h_stored"))
        LN = 8
        with nc.Block() as block:
            @block.sync
            def _(sp):
                loads = 0

                def load(to, src):
                    nonlocal loads
                    sp.dma_start(to, src).then_inc(w_here, 16)
                    loads += 16

                load(norm_w[:], W["ssd_norm_w"])
                load(b_glu[:], W["s5_b_glu"])
                load(wg[:], W["s5_w_glu"][0].rearrange("(k p) n -> p k n", p=P))
                load(wr[:], W["w_router"].rearrange("(k p) n -> p k n", p=P))
                load(wo[:], W["w_out"][0].rearrange("(k p) n -> p k n", p=P))
                for s in range(2):
                    for kind, to in ((2, g1), (4, scale), (3, shift)):
                        load(to[:, s, :], mod[s:s + 1, kind * D:(kind + 1) * D].to_broadcast([P, D]))
                load(ln_g[:], W["ln1_g"].to_broadcast([P, D]))
                load(ln_b[:], W["ln1_b"].to_broadcast([P, D]))
                assert loads == C.mix_loads
                with sp.Fori(0, TURNS) as t:
                    for j in range(2):
                        m = t * 2 + j
                        sp.wait_ge(turned, m * EVENTS)
                        sp.nop(nofuse=True)
                        sp.wait_ge(ln, t * 2 * TPW * LN)
                        sp.nop(nofuse=True)
                        wide = bass.ds(m * WIDE, WIDE)
                        sp.dma_start(yb[:], yg[wide, :].rearrange("(a p) n -> p a n", p=P)).then_inc(y_here, 16)
                        sp.dma_start(ya[:], y_ssd[wide, :].rearrange("(a p) n -> p a n", p=P)).then_inc(y_here, 16)
                        sp.dma_start(xt[:, j], x[wide, :].rearrange("(a p) n -> p a n", p=P)).then_inc(x_here[j], 16)

            @block.gpsimd
            def _(pool):
                pool.wait_ge(w_here, C.mix_loads)
                pool.tensor_scalar(scale[:], scale[:], 1.0, None, ALU.add).then_inc(one_added, 1)
                pool.wait_ge(one_added, 1)
                with pool.Fori(0, TURNS) as t:
                    for j in range(2):
                        s = pool.snap(seq_of(t, WIDE_SAMPLE // 2))
                        for a in range(TPW):
                            r = a % 2
                            n = (t * 2 + j) * TPW + a
                            pool.wait_ge(ln, n * LN + 5)
                            pool.nop(nofuse=True)
                            pool.tensor_scalar(mean[:, r, 1:2], mean[:, r, 1:2], EPS, None, ALU.add).then_inc(rooted, 1)
                            pool.wait_ge(rooted, n * 2 + 1)
                            pool.tensor_tensor(mean[:, r, 1:2], mean[:, r, 1:2], C.minus_half[:], ALU.pow).then_inc(rooted, 1)
                            pool.wait_ge(h_turned, (n - r) * 2)
                            pool.nop(nofuse=True)
                            pool.wait_ge(h_stored[r], (t * 2 + j) * 32 + a // 2 * 16)
                            pool.nop(nofuse=True)
                            pool.wait_ge(ln, (n + 1) * LN)
                            pool.nop(nofuse=True)
                            pool.tensor_tensor(h[:, r, :], v[:, r, :], flat(scale[:, bass.ds(s, 1), :]), ALU.mult).then_inc(h_made, 1)
                            pool.wait_ge(h_made, n * 2 + 1)
                            pool.nop(nofuse=True)
                            pool.tensor_tensor(h[:, r, :], h[:, r, :], flat(shift[:, bass.ds(s, 1), :]), ALU.add).then_inc(h_made, 1)

            @block.vector
            def _(dve):
                dve.wait_ge(w_here, C.mix_loads)
                with dve.Fori(0, TURNS) as t:
                    steps = Steps(dve, ln, t, 2 * TPW * LN)
                    for j in range(2):
                        m = dve.snap(t * 2 + j)
                        s = dve.snap(seq_of(t, WIDE_SAMPLE // 2))
                        for k in range(KY):
                            dve.wait_ge(taken, m * EVENTS + 2 * KY + k + 1)
                            dve.tensor_tensor(yt[:, j, KY + k, :], sg[:, k, :], gt[:, k, :], ALU.mult).then_inc(gated, 1)
                        dve.wait_ge(x_here[j], t * 16 + 16)
                        for a in range(TPW):
                            r = a % 2
                            dve.wait_ge(mixed, m * TPW + a + 1)
                            dve.wait_ge(x1_stored[r], m * 32 + a // 2 * 16)
                            dve.wait_ge(h_made, m * 2 * TPW + (a - r) * 2)
                            dve.nop(nofuse=True)
                            banks = C.bank[2 + 2 * r:4 + 2 * r]
                            steps.done(dve.tensor_tensor(v[:, r, 0:WIDE], banks[0][:, :], flat(g1[:, bass.ds(s, 1), 0:WIDE]), ALU.mult))
                            dve.tensor_tensor(v[:, r, WIDE:D], banks[1][:, :], flat(g1[:, bass.ds(s, 1), WIDE:D]), ALU.mult).then_inc(mix_read, 1)
                            dve.wait_ge(mix_read, m * TPW + a + 1)
                            steps.then(dve.scalar_tensor_tensor(out=v[:, r, :], in0=xt[:, j, a, :], scalar=ALPHA, in1=v[:, r, :],
                                                                op0=ALU.mult, op1=ALU.add))
                            for q in range(2):
                                steps.done(dve.bn_stats(stats[:, q, :], v[:, r, q * WIDE:(q + 1) * WIDE]))
                            steps.wait()
                            dve.nop(nofuse=True)
                            steps.done(dve.bn_aggr(mean[:, r, :], flat(stats[:])))
                            dve.wait_ge(rooted, (m * TPW + a + 1) * 2)
                            steps.then(dve.tensor_scalar(v[:, r, :], v[:, r, :], mean[:, r, 0:1], mean[:, r, 1:2], ALU.subtract, ALU.mult))
                            steps.then(dve.tensor_tensor(v[:, r, :], v[:, r, :], ln_g[:], ALU.mult))
                            steps.done(dve.tensor_tensor(v[:, r, :], v[:, r, :], ln_b[:], ALU.add))
                    steps.end_turn()

            def in_order(turn_gate, products, logits):
                def last_turn_or_not(m, j, more):
                    for a in range(TPW):
                        products(m, j, a)
                        if a:
                            logits(m, a - 1)
                    if more:
                        turn_gate(m + 1, 1 - j)
                    logits(m, TPW - 1)
                return last_turn_or_not

            @block.tensor
            def _(pe):
                def turn_gate(m, j):
                    pe.wait_ge(y_here, (m + 1) * 32)
                    for e in range(2 * KY):
                        pe.wait_ge(taken, m * EVENTS + max(e - 1, 0))
                        k, src = e % KY, yb if e < KY else ya
                        for a in range(TPW):
                            tr = pe.transpose(C.bank[e % 2][:, a * P:(a + 1) * P], src[:, a, k * P:(k + 1) * P], C.ident[:])
                        tr.then_inc(turned, 1)
                    for c in range(KY):
                        pe.wait_ge(taken, m * EVENTS + 2 * KY + c - 1)
                        for k in range(KY):
                            mul = pe.matmul(C.bank[c % 2][:, :], wg[:, k, c * P:(c + 1) * P], gt[:, k, :], start=k == 0, stop=k == KY - 1)
                        mul.then_inc(turned, 1)

                def products(m, j, a):
                    if a == 0:
                        pe.wait_ge(gated, (m + 1) * KY)
                    pe.wait_ge(mix_read, m * TPW + max(a - 1, 0))
                    for q in range(2):
                        for k in range(KT):
                            mul = pe.matmul(C.bank[2 + 2 * (a % 2) + q][:, :], yt[:, j, k, a * P:(a + 1) * P], wo[:, k, q * WIDE:(q + 1) * WIDE],
                                            start=k == 0, stop=k == KT - 1)
                    mul.then_inc(mixed, 1)

                def logits(m, a):
                    n = m * TPW + a
                    pe.wait_ge(h_made, n * 2 + 2)
                    for q in range(2):
                        pe.wait_ge(h_taken, n * 2 + q)
                        for k in range(4):
                            tr = pe.transpose(C.bank[6][:, k * P:(k + 1) * P], h[:, a % 2, (q * 4 + k) * P:(q * 4 + k + 1) * P], C.ident[:])
                        tr.then_inc(h_turned, 1)
                    pe.wait_ge(h_taken, n * 2 + 2)
                    pe.wait_ge(kept, n)
                    for k in range(KT):
                        mul = pe.matmul(C.bank[7][:, 0:NE], ht[:, k, :], wr[:, k, :], start=k == 0, stop=k == KT - 1)
                    mul.then_inc(routed, 1)

                pe.wait_ge(w_here, C.mix_loads)
                wide = in_order(turn_gate, products, logits)
                turn_gate(0, 0)
                with pe.Fori(0, TURNS - 1) as t:
                    for j in range(2):
                        wide(t * 2 + j, j, True)
                wide(NWIDE - 2, 0, True)
                wide(NWIDE - 1, 1, False)

            @block.scalar
            def _(act):
                def turn_gate(m, j):
                    act.wait_ge(gated, m * KY)
                    for e in range(EVENTS):
                        act.wait_ge(turned, m * EVENTS + e + 1)
                        k, bank = e % KY, C.bank[e % 2][:, :]
                        if e < KY:
                            take = act.activation(gt[:, k, :], bank, ACT.Copy)
                        elif e < 2 * KY:
                            take = act.activation(yt[:, j, k, :], bank, ACT.Copy, scale=norm_w[:, k:k + 1])
                        else:
                            take = act.activation(sg[:, k, :], bank, ACT.Sigmoid, bias=b_glu[:, k:k + 1])
                        take.then_inc(taken, 1)

                def products(m, j, a):
                    pass

                def logits(m, a):
                    n, r = m * TPW + a, a % 2
                    rows = bass.ds(n * P, P) if not isinstance(n, int) else slice(n * P, (n + 1) * P)
                    act.wait_ge(ln, (n + 1) * LN)
                    act.nop(nofuse=True)
                    act.dma_start(x1_dram[rows, :], v[:, r, :]).then_inc(x1_stored[r], 16)
                    act.wait_ge(h_made, n * 2 + 2)
                    act.nop(nofuse=True)
                    act.dma_start(h_dram[rows, :], h[:, r, :]).then_inc(h_stored[r], 16)
                    act.wait_ge(routed, n)
                    for q in range(2):
                        act.wait_ge(h_turned, n * 2 + q + 1)
                        act.activation(ht[:, q * 4:q * 4 + 4, :].rearrange("p k n -> p (k n)"), C.bank[6][:, :], ACT.Copy).then_inc(h_taken, 1)
                    act.wait_ge(routed, n + 1)
                    act.nop(nofuse=True)
                    where = bass.ds(n, 1) if not isinstance(n, int) else slice(n, n + 1)
                    act.activation(flat(C.logits[:, where, :]), C.bank[7][:, 0:NE], ACT.Copy).then_inc(kept, 1)

                act.wait_ge(w_here, C.mix_loads)
                wide = in_order(turn_gate, products, logits)
                turn_gate(0, 0)
                with act.Fori(0, TURNS - 1) as t:
                    for j in range(2):
                        wide(t * 2 + j, j, True)
                wide(NWIDE - 2, 0, True)
                wide(NWIDE - 1, 1, False)
                for r in range(2):
                    act.wait_ge(x1_stored[r], NT // 2 * 16)
                    act.wait_ge(h_stored[r], NT // 2 * 16)
    S.clear()


def route(nc, C, S, b_router, row_token):
    with ExitStack() as ctx:
        sb = lambda n, s, dt=F32: ctx.enter_context(nc.sbuf_tensor("rou_" + n, s, dt))
        b = sb("b", [P, NE])
        prob, masked, tie, both = (sb(n, [P, NT, NE]) for n in ("prob", "masked", "tie", "both"))
        first, second = sb("first", [P, NT, NE]), sb("second", [P, NT, NE])
        top, top2, one = sb("top", [P, NT]), sb("top2", [P, NT]), sb("one", [P, NT])
        group, group_tie = sb("group", [P, NT, NG]), sb("group_tie", [P, NT, NG])
        down_i, down = sb("down_i", [P, NE], I32), sb("down", [P, NE])
        base = sb("base", [P, NT + 1, NE])
        filled, filled_i, ends = sb("filled", [P, NE]), sb("filled_i", [P, NE], I32), sb("ends", [P, NE])
        place = sb("place", [P, NT, 2])
        starts_i, starts = sb("starts_i", [P, NBLK], I32), sb("starts", [P, NBLK])
        behind, owner = sb("behind", [P, NBLK, NE]), sb("owner", [P, NBLK])
        token, zero = sb("token", [P, NT], I32), sb("zero", [P, ROWS // P], I32)
        index, value = sb("index", [P, 8], I32), sb("value", [P, 8], I32)
        rows_i, rows_f = sb("rows_i", [NBLK, BLK], I32), sb("rows_f", [NBLK, BLK])
        b_here, made, steps_done, expd, counted, cleared, read_back, rows_turned, picked = (
            S(n) for n in ("b_here", "made", "steps_done", "expd", "counted", "cleared", "read_back", "rows_turned", "picked"))
        scattered = S("scattered", pool_dma=True)
        with nc.Block() as block:
            @block.sync
            def _(sp):
                sp.dma_start(b[:], b_router.to_broadcast([P, NE])).then_inc(b_here, 16)
                sp.wait_ge(made, 4)
                sp.dma_start(row_token.rearrange("(p n) a -> p (n a)", p=P), zero[:]).then_inc(cleared, 16)
                sp.wait_ge(scattered, 16 * 2 * NT)
                sp.dma_start(rows_i[:], row_token.rearrange("(b p) a -> b (p a)", p=BLK)).then_inc(read_back, 16)

            @block.gpsimd
            def _(pool):
                pool.iota(down_i[:], pattern=[[-1, NE]], base=NE, channel_multiplier=0).then_inc(made, 1)
                pool.iota(starts_i[:], pattern=[[BLK, NBLK]], base=0, channel_multiplier=0).then_inc(made, 1)
                pool.iota(token[:], pattern=[[P, NT]], base=0, channel_multiplier=1).then_inc(made, 1)
                pool.memset(zero[:], 0).then_inc(made, 1)
                pool.wait_ge(cleared, 16)
                pool.wait_ge(made, 4)
                pool.wait_ge(steps_done, C.route_placed)
                with pool.Fori(0, NT // 4) as t:
                    pool.wait_ge(scattered, t * 8 * 16)
                    pool.nop(nofuse=True)
                    dest = C.dest[:, bass.ds(t * 4, 4), :].rearrange("p t k -> p (t k)")
                    pool.tensor_copy(index[:], dest).then_inc(picked, 1)
                    pool.tensor_copy(value[:].rearrange("p (t k) -> p t k", k=2),
                                     token[:, bass.ds(t * 4, 4)].unsqueeze(2).to_broadcast([P, 4, 2])).then_inc(picked, 1)
                    pool.wait_ge(picked, t * 2 + 2)
                    pool.nop(nofuse=True)
                    for n in range(8):
                        pool.indirect_dma_start(out=row_token, out_offset=bass.IndirectOffsetOnAxis(ap=index[:, n:n + 1], axis=0),
                                                in_=value[:, n:n + 1], in_offset=None).then_inc(scattered, 16)

            @block.vector
            def _(dve):
                steps = Steps(dve, steps_done)
                tt = lambda o, a, c, op: steps.then(dve.tensor_tensor(o, a, c, op))
                ts = lambda o, a, s1, op0, s2=None, op1=ALU.bypass: steps.then(dve.tensor_scalar(o, a, s1, s2, op0, op1))
                red = lambda o, a, op: steps.then(dve.tensor_reduce(o, a, AX.X, op))
                per = lambda a, n: a.unsqueeze(2).to_broadcast([P, NT, n])
                row = lambda a: a.unsqueeze(1).to_broadcast([P, NT, NE])
                dve.wait_ge(b_here, 16)
                dve.wait_ge(made, 4)
                steps.then(dve.tensor_copy(down[:], down_i[:]))
                steps.then(dve.tensor_copy(starts[:], starts_i[:]))
                tt(prob[:], C.logits[:], row(b[:]), ALU.add)
                red(top[:], prob[:], ALU.max)
                tt(prob[:], prob[:], per(top[:], NE), ALU.subtract)
                C.route_shifted = steps.n
                dve.wait_ge(expd, 1)
                red(one[:], prob[:], ALU.add)
                steps.then(dve.reciprocal(one[:], one[:]))
                tt(prob[:], prob[:], per(one[:], NE), ALU.mult)
                red(group[:], prob[:].rearrange("p t (g e) -> p t g e", g=NG), ALU.max)
                red(top[:], group[:], ALU.max)
                tt(group_tie[:], group[:], per(top[:], NG), ALU.is_equal)
                tt(group_tie[:], group_tie[:], down[:, NE - NG:NE].unsqueeze(1).to_broadcast([P, NT, NG]), ALU.mult)
                red(one[:], group_tie[:], ALU.max)
                tt(group[:], group_tie[:], per(one[:], NG), ALU.is_equal)
                inside = group[:].unsqueeze(3).to_broadcast([P, NT, NG, EPG])
                four = lambda a: a.rearrange("p t (g e) -> p t g e", g=NG)
                tt(four(masked[:]), four(prob[:]), inside, ALU.mult)
                steps.then(dve.tensor_copy(four(tie[:]), inside))
                steps.then(dve.scalar_tensor_tensor(out=masked[:], in0=tie[:], scalar=-1.0, in1=masked[:], op0=ALU.add, op1=ALU.add))
                for best, pick in ((top, first), (top2, second)):
                    red(best[:], masked[:], ALU.max)
                    tt(tie[:], masked[:], per(best[:], NE), ALU.is_equal)
                    tt(tie[:], tie[:], row(down[:]), ALU.mult)
                    red(one[:], tie[:], ALU.max)
                    tt(pick[:], tie[:], per(one[:], NE), ALU.is_equal)
                    if pick is first:
                        steps.then(dve.scalar_tensor_tensor(out=masked[:], in0=first[:], scalar=-4.0, in1=masked[:], op0=ALU.mult, op1=ALU.add))
                tt(one[:], top[:], top2[:], ALU.add)
                steps.then(dve.reciprocal(one[:], one[:]))
                tt(C.gate[:, :, 0], top[:], one[:], ALU.mult)
                tt(C.gate[:, :, 1], top2[:], one[:], ALU.mult)
                tt(both[:], first[:], second[:], ALU.add)
                C.route_chosen = steps.n
                steps.then(dve.memset(base[:, 0, :], 0.0))
                dve.wait_ge(counted, 2)
                total = C.bank[1][:, 0:NT * NE].rearrange("p (t e) -> p t e", e=NE)
                with dve.Fori(0, NT) as t:
                    loop = Steps(dve, steps_done, t, 1, steps.n)
                    loop.then(dve.tensor_tensor(base[:, bass.ds(t + 1, 1), :], base[:, bass.ds(t, 1), :], total[:, bass.ds(t, 1), :], ALU.add))
                steps.n += NT
                ts(filled[:], base[:, NT, :], float(BLK - 1), ALU.add)
                steps.then(dve.tensor_copy(filled_i[:], filled[:]))
                ts(filled_i[:], filled_i[:], 7, ALU.logical_shift_right, 7, ALU.logical_shift_left)
                steps.then(dve.tensor_copy(filled[:], filled_i[:]))
                steps.then(dve.tensor_copy(ends[:], filled[:]))
                with dve.Fori(1, NE) as e:
                    loop = Steps(dve, steps_done, e - 1, 1, steps.n)
                    loop.then(dve.tensor_tensor(ends[:, bass.ds(e, 1)], ends[:, bass.ds(e, 1)], ends[:, bass.ds(e - 1, 1)], ALU.add))
                steps.n += NE - 1
                tt(filled[:], ends[:], filled[:], ALU.subtract)
                before = C.bank[0][:, 0:NT * NE].rearrange("p (t e) -> p t e", e=NE)
                tt(base[:, 0:NT, :], base[:, 0:NT, :], row(filled[:]), ALU.add)
                tt(base[:, 0:NT, :], base[:, 0:NT, :], before, ALU.add)
                for k, pick in enumerate((first, second)):
                    tt(tie[:], pick[:], base[:, 0:NT, :], ALU.mult)
                    red(place[:, :, k], tie[:], ALU.add)
                steps.then(dve.tensor_copy(C.dest[:], place[:]))
                assert steps.n == C.route_placed, steps.n
                tt(behind[:], ends[:].unsqueeze(1).to_broadcast([P, NBLK, NE]), starts[:].unsqueeze(2).to_broadcast([P, NBLK, NE]), ALU.is_le)
                red(owner[:], behind[:], ALU.add)
                ts(owner[:], owner[:], float(NE - 1), ALU.min)
                steps.then(dve.tensor_copy(C.expert[:], owner[:]))
                steps.then(dve.tensor_copy(filled_i[:], ends[:]))
                ts(C.blocks_end[:], filled_i[:], 7, ALU.logical_shift_right)
                dve.wait_ge(read_back, 16)
                steps.then(dve.tensor_copy(rows_f[:], rows_i[:]))
                C.route_read = steps.n
                dve.wait_ge(rows_turned, 1)
                steps.then(dve.tensor_copy(C.source[:], C.bank[2][:, 0:NBLK]))

            @block.scalar
            def _(act):
                act.wait_ge(steps_done, C.route_shifted)
                act.activation(prob[:], prob[:], ACT.Exp).then_inc(expd, 1)

            @block.tensor
            def _(pe):
                pe.wait_ge(steps_done, C.route_chosen)
                for n, mask in enumerate((C.lt, C.ones)):
                    pe.matmul(C.bank[n][:, 0:NT * NE].rearrange("p (t e) -> p t e", e=NE), mask[:], both[:], start=True, stop=True).then_inc(counted, 1)
                pe.wait_ge(steps_done, C.route_read)
                pe.transpose(C.bank[2][:, 0:NBLK], rows_f[:], C.ident[0:NBLK, 0:NBLK]).then_inc(rows_turned, 1)
    S.clear()


def experts(nc, C, S, h_dram, w_gate, w_up, w_down, rows_out):
    TURNS = (NBLK - 3) // 2
    assert NBLK == 2 * TURNS + 3
    KD = DE // P
    with ExitStack() as ctx:
        sb = lambda n, s, dt=F32: ctx.enter_context(nc.sbuf_tensor("exp_" + n, s, dt))
        wg, wu, wd = sb("wg", [P, 2, KT * DE]), sb("wu", [P, 2, KT * DE]), sb("wd", [P, 2, KD * D])
        index = sb("index", [P, 2], I32)
        h, ht = sb("h", [P, 2, D]), sb("ht", [P, 2, KT, P])
        silu, hid, hid_t = sb("silu", [P, DE]), sb("hid", [P, DE]), sb("hid_t", [P, 2, KD, P])
        out = sb("out", [P, 2, D])
        x0, x1, gate_b, up_b, hid_b, out0, out1 = (C.bank[n] for n in range(7))
        picked, turned, taken0, taken1, gate_mm, up_mm, down_mm, silu_done, hid_done, hid_turned, hid_taken, out0_read, out1_read = (
            S(n) for n in ("picked", "turned", "taken0", "taken1", "gate_mm", "up_mm", "down_mm", "silu_done", "hid_done",
                           "hid_turned", "hid_taken", "out0_read", "out1_read"))
        wg_here, wu_here, wd_here, h_here, stored = (
            [S(f"{n}{j}", pool_dma=n in ("h_here", "stored")) for j in range(2)] for n in ("wg_here", "wu_here", "wd_here", "h_here", "stored"))
        gv = w_gate.rearrange("e (p k) n -> e p (k n)", p=P)
        uv = w_up.rearrange("e (p k) n -> e p (k n)", p=P)
        dv = w_down.rearrange("e (p k) n -> e p (k n)", p=P)

        flat = lambda a: a.rearrange("p a n -> p (a n)")

        def blocks(eng, body, first, last):
            first()
            body(1, 1)
            with eng.Fori(1, TURNS + 1) as t:
                for j in range(2):
                    body(t * 2 + j, j)
            last()

        with nc.Block() as block:
            @block.sync
            def _(sp):
                for e in range(2):
                    for to, of, here in ((wg, gv, wg_here), (wu, uv, wu_here), (wd, dv, wd_here)):
                        sp.dma_start(to[:, e, :], of[e]).then_inc(here[e], 16)
                with sp.Fori(1, NE // 2) as t:
                    for j in range(2):
                        e = t * 2 + j
                        last = sp.value_load(C.blocks_end[0:1, bass.ds(e - 2, 1)], min_val=0, max_val=NBLK)
                        for to, of, here, free in ((wg, gv, wg_here, gate_mm), (wu, uv, wu_here, up_mm), (wd, dv, wd_here, down_mm)):
                            sp.wait_ge(free, last)
                            sp.nop(nofuse=True)
                            sp.dma_start(to[:, j, :], of[bass.ds(e, 1)].rearrange("a p n -> p (a n)")).then_inc(here[j], 16)

            @block.gpsimd
            def _(pool):
                def gather(b, j, wait=True):
                    if wait:
                        pool.wait_ge(turned, (b - 1) * 2)
                        pool.nop(nofuse=True)
                    one = bass.ds(b, 1) if not isinstance(b, int) else slice(b, b + 1)
                    pool.tensor_copy(index[:, j:j + 1], C.source[:, one]).then_inc(picked, 1)
                    pool.wait_ge(picked, b + 1)
                    pool.nop(nofuse=True)
                    pool.indirect_dma_start(out=h[:, j, :], out_offset=None, in_=h_dram,
                                            in_offset=bass.IndirectOffsetOnAxis(ap=index[:, j:j + 1], axis=0)).then_inc(h_here[j], 16)

                def store(b, j):
                    pool.wait_ge(out0_read, b + 1)
                    pool.nop(nofuse=True)
                    pool.wait_ge(out1_read, b + 1)
                    pool.nop(nofuse=True)
                    rows = bass.ds(b * BLK, BLK) if not isinstance(b, int) else slice(b * BLK, (b + 1) * BLK)
                    pool.dma_start(rows_out[rows, :], out[:, j, :]).then_inc(stored[j], 16)

                gather(0, 0, wait=False)
                gather(1, 1, wait=False)
                with pool.Fori(1, NBLK // 2) as t:
                    for j in range(2):
                        b = t * 2 + j
                        gather(b, j)
                        store(b - 2, j)
                gather(NBLK - 1, 0)
                store(NBLK - 3, 0)
                store(NBLK - 2, 1)
                store(NBLK - 1, 0)
                for j in range(2):
                    pool.wait_ge(stored[j], (NBLK + 1 - j) // 2 * 16)

            @block.tensor
            def _(pe):
                def turn(b, j):
                    pe.wait_ge(h_here[j], b // 2 * 16 + 16)
                    pe.wait_ge(taken0, b)
                    for k in range(4):
                        tr = pe.transpose(x0[:, k * P:(k + 1) * P], h[:, j, k::KT], C.ident[:])
                    tr.then_inc(turned, 1)
                    pe.wait_ge(taken1, b)
                    for k in range(4, KT):
                        tr = pe.transpose(x1[:, (k - 4) * P:(k - 3) * P], h[:, j, k::KT], C.ident[:])
                    tr.then_inc(turned, 1)

                def expert_of(b):
                    one = bass.ds(b, 1) if not isinstance(b, int) else slice(b, b + 1)
                    return pe.value_load(C.expert[0:1, one], min_val=0, max_val=NE - 1)

                def wait_for_weights(here, e):
                    pe.wait_ge(here[0], (e // 2 + 1) * 16)
                    pe.wait_ge(here[1], (e + 1) // 2 * 16)
                    pe.nop(nofuse=True)

                def hidden(b, j, e, of, bank, here, done, read):
                    wait_for_weights(here, e)
                    pe.wait_ge(read, b)
                    pe.wait_ge(taken0, b + 1)
                    pe.wait_ge(taken1, b + 1)
                    pe.nop(nofuse=True)
                    for k in range(KT):
                        mul = pe.matmul(bank[:, :], ht[:, j, k, :], flat(of[:, bass.ds(e % 2, 1), k * DE:(k + 1) * DE]),
                                        start=k == 0, stop=k == KT - 1)
                    mul.then_inc(done, 1)

                def turn_hidden(b, j):
                    pe.wait_ge(hid_done, b + 1)
                    pe.wait_ge(hid_taken, b)
                    for k in range(KD):
                        tr = pe.transpose(hid_b[:, k * P:(k + 1) * P], hid[:, k::KD], C.ident[:])
                    tr.then_inc(hid_turned, 1)

                def down(b, j, e):
                    wait_for_weights(wd_here, e)
                    pe.wait_ge(hid_taken, b + 1)
                    for bank, read, q in ((out0, out0_read, 0), (out1, out1_read, 1)):
                        pe.wait_ge(read, b)
                        pe.nop(nofuse=True)
                        for k in range(KD):
                            mul = pe.matmul(bank[:, :], hid_t[:, j, k, :],
                                            flat(wd[:, bass.ds(e % 2, 1), k * D + q * WIDE:k * D + (q + 1) * WIDE]),
                                            start=k == 0, stop=k == KD - 1)
                    mul.then_inc(down_mm, 1)

                def part(b, j, e):
                    down(b - 1, 1 - j, e[0])
                    hidden(b, j, e[1], wu, up_b, wu_here, up_mm, hid_done)
                    turn(b + 1, 1 - j)
                    turn_hidden(b, j)
                    hidden(b + 1, 1 - j, e[2], wg, gate_b, wg_here, gate_mm, silu_done)

                turn(0, 0)
                e = [expert_of(b) for b in range(3)]
                hidden(0, 0, e[0], wg, gate_b, wg_here, gate_mm, silu_done)
                hidden(0, 0, e[0], wu, up_b, wu_here, up_mm, hid_done)
                turn(1, 1)
                turn_hidden(0, 0)
                hidden(1, 1, e[1], wg, gate_b, wg_here, gate_mm, silu_done)
                part(1, 1, e)
                with pe.Fori(1, TURNS + 1) as t:
                    e = [expert_of(t * 2 - 1 + n) for n in range(4)]
                    for j in range(2):
                        part(t * 2 + j, j, e[j:])
                e = [expert_of(b) for b in (NBLK - 2, NBLK - 1)]
                down(NBLK - 2, 1, e[0])
                hidden(NBLK - 1, 0, e[1], wu, up_b, wu_here, up_mm, hid_done)
                turn_hidden(NBLK - 1, 0)
                down(NBLK - 1, 0, e[1])

            @block.scalar
            def _(act):
                def take(b, j):
                    act.wait_ge(turned, b * 2 + 1)
                    act.activation(ht[:, j, 0:4, :].rearrange("p k n -> p (k n)"), x0[:, :], ACT.Copy).then_inc(taken0, 1)

                def gate(b):
                    act.wait_ge(gate_mm, b + 1)
                    act.wait_ge(hid_done, b)
                    act.activation(silu[:], gate_b[:, :], ACT.Silu).then_inc(silu_done, 1)

                def hidden(b, j):
                    act.wait_ge(hid_turned, b + 1)
                    act.activation(hid_t[:, j].rearrange("p k n -> p (k n)"), hid_b[:, :], ACT.Copy).then_inc(hid_taken, 1)

                def result(b, j):
                    act.wait_ge(down_mm, b + 1)
                    act.wait_ge(stored[j], b // 2 * 16)
                    act.activation(out[:, j, 0:WIDE], out0[:, :], ACT.Copy).then_inc(out0_read, 1)

                def first():
                    take(0, 0)
                    gate(0)
                    take(1, 1)
                    hidden(0, 0)

                def body(b, j, more=True):
                    gate(b)
                    result(b - 1, 1 - j)
                    if more:
                        take(b + 1, 1 - j)
                    hidden(b, j)

                def last():
                    body(NBLK - 1, 0, more=False)
                    result(NBLK - 1, 0)
                blocks(act, body, first, last)

            @block.vector
            def _(dve):
                def take(b, j):
                    dve.wait_ge(turned, b * 2 + 2)
                    dve.tensor_copy(ht[:, j, 4:KT, :].rearrange("p k n -> p (k n)"), x1[:, :]).then_inc(taken1, 1)

                def hidden(b):
                    dve.wait_ge(up_mm, b + 1)
                    dve.wait_ge(silu_done, b + 1)
                    dve.wait_ge(hid_turned, b)
                    dve.tensor_tensor(hid[:], silu[:], up_b[:, :], ALU.mult).then_inc(hid_done, 1)

                def result(b, j):
                    dve.wait_ge(down_mm, b + 1)
                    dve.wait_ge(stored[j], b // 2 * 16)
                    dve.tensor_copy(out[:, j, WIDE:D], out1[:, :]).then_inc(out1_read, 1)

                def first():
                    take(0, 0)
                    hidden(0)
                    take(1, 1)

                def body(b, j, more=True):
                    result(b - 1, 1 - j)
                    hidden(b)
                    if more:
                        take(b + 1, 1 - j)

                def last():
                    body(NBLK - 1, 0, more=False)
                    result(NBLK - 1, 0)
                blocks(dve, body, first, last)
    S.clear()


def combine(nc, C, S, rows_out, x1_dram, mod, ln_g_row, ln_b_row, out_sample, out_prompt):
    TURNS = NT // 2
    with ExitStack() as ctx:
        sb = lambda n, s, dt=F32: ctx.enter_context(nc.sbuf_tensor("com_" + n, s, dt))
        g2, ln_g, ln_b = sb("g2", [P, 2, D]), sb("ln_g", [P, D]), sb("ln_b", [P, D])
        index = sb("index", [P, 2, 2], I32)
        r, x1, v = sb("r", [P, 2, 2, D]), sb("x1", [P, 2, D]), sb("v", [P, 2, D])
        stats, mean, y = sb("stats", [P, 2, 6]), sb("mean", [P, 2, 2]), sb("y", [P, 2, D])
        flat = lambda a: a.rearrange("p a n -> p (a n)")
        minus = sb("minus", [P, 2, 1])
        w_here, picked, weighted, ln, rooted, normed, scaled, shifted = (
            S(n) for n in ("w_here", "picked", "weighted", "ln", "rooted", "normed", "scaled", "shifted"))
        x1_here, stored = ([S(f"{n}{j}") for j in range(2)] for n in ("x1_here", "stored"))
        r_here = [S(f"r_here{j}", pool_dma=True) for j in range(2)]
        SUM, GATED, X1_ADDED, STATS0, STATS1, MEAN = range(1, 7)
        LN = MEAN
        one = lambda n: bass.ds(n, 1) if not isinstance(n, int) else slice(n, n + 1)

        def tiles(eng, body, first=2):
            with eng.Fori(first // 2, TURNS) as t:
                for j in range(2):
                    body(t * 2 + j, j)

        with nc.Block() as block:
            @block.sync
            def _(sp):
                def store(n, j, to):
                    sp.wait_ge(shifted, n + 1)
                    sp.nop(nofuse=True)
                    sp.dma_start(to, y[:, j, :]).then_inc(stored[j], 16)

                for j in range(2):
                    sp.dma_start(x1[:, j, :], x1_dram[j * P:(j + 1) * P, :]).then_inc(x1_here[j], 16)
                for s in range(2):
                    sp.dma_start(g2[:, s, :], mod[s:s + 1, 5 * D:6 * D].to_broadcast([P, D])).then_inc(w_here, 16)
                sp.dma_start(ln_g[:], ln_g_row.to_broadcast([P, D])).then_inc(w_here, 16)
                sp.dma_start(ln_b[:], ln_b_row.to_broadcast([P, D])).then_inc(w_here, 16)
                for lo, hi, start, out in ((1, NT_SAMPLE // 2 + 1, 0, out_sample), (NT_SAMPLE // 2 + 1, TURNS, NT_SAMPLE, out_prompt)):
                    with sp.Fori(lo, hi) as t:
                        for j in range(2):
                            n = t * 2 + j
                            sp.wait_ge(ln, (n - 2) * LN + X1_ADDED)
                            sp.nop(nofuse=True)
                            sp.dma_start(x1[:, j, :], x1_dram[bass.ds(n * P, P), :]).then_inc(x1_here[j], 16)
                            store(n - 2, j, out[0, bass.ds((n - 2 - start) * P, P), :])
                for j in range(2):
                    store(NT - 2 + j, j, out_prompt[0, PROMPT - (2 - j) * P:PROMPT - (1 - j) * P, :])
                for j in range(2):
                    sp.wait_ge(stored[j], TURNS * 16)

            @block.gpsimd
            def _(pool):
                def gather(n, j, wait=True):
                    if wait:
                        pool.wait_ge(ln, (n - 2) * LN + SUM)
                        pool.nop(nofuse=True)
                    pool.tensor_copy(index[:, j, :], flat(C.dest[:, one(n), :])).then_inc(picked, 1)
                    pool.wait_ge(picked, n + 1)
                    pool.nop(nofuse=True)
                    for k in range(2):
                        pool.indirect_dma_start(out=r[:, j, k, :], out_offset=None, in_=rows_out,
                                                in_offset=bass.IndirectOffsetOnAxis(ap=index[:, j, k:k + 1], axis=0)).then_inc(r_here[j], 16)

                def shift(n, j):
                    pool.wait_ge(scaled, n + 1)
                    pool.wait_ge(stored[j], n // 2 * 16)
                    pool.tensor_tensor(y[:, j, :], v[:, j, :], ln_b[:], ALU.add).then_inc(shifted, 1)

                def root(n, j):
                    pool.wait_ge(ln, n * LN + MEAN)
                    pool.wait_ge(normed, n)
                    pool.nop(nofuse=True)
                    pool.tensor_scalar(mean[:, j, 1:2], mean[:, j, 1:2], EPS, None, ALU.add).then_inc(rooted, 1)
                    pool.wait_ge(rooted, n * 3 + 1)
                    pool.tensor_tensor(mean[:, j, 1:2], mean[:, j, 1:2], C.minus_half[:], ALU.pow).then_inc(rooted, 1)
                    pool.wait_ge(rooted, n * 3 + 2)
                    pool.nop(nofuse=True)
                    pool.tensor_scalar(minus[:, j, :], mean[:, j, 0:1], mean[:, j, 1:2], -1.0, ALU.mult, ALU.mult).then_inc(rooted, 1)

                gather(0, 0, wait=False)
                gather(1, 1, wait=False)
                pool.wait_ge(w_here, 64)
                gather(2, 0)
                root(0, 0)
                gather(3, 1)
                shift(0, 0)
                root(1, 1)

                def tile(n, j):
                    gather(n, j)
                    shift(n - 3, 1 - j)
                    root(n - 2, j)
                tiles(pool, tile, first=4)
                shift(NT - 3, 1)
                root(NT - 2, 0)
                shift(NT - 2, 0)
                root(NT - 1, 1)
                shift(NT - 1, 1)

            @block.scalar
            def _(act):
                def weight(n, j):
                    act.wait_ge(r_here[j], n // 2 * 32 + 32)
                    act.nop(nofuse=True)
                    act.activation(r[:, j, 0, :], r[:, j, 0, :], ACT.Copy, scale=flat(C.gate[:, one(n), 0:1])).then_inc(weighted, 1)

                def norm(n, j):
                    act.wait_ge(rooted, n * 3 + 3)
                    act.activation(v[:, j, :], v[:, j, :], ACT.Identity, scale=mean[:, j, 1:2], bias=minus[:, j, :]).then_inc(normed, 1)

                weight(0, 0)
                weight(1, 1)
                norm(0, 0)

                def tile(n, j):
                    weight(n, j)
                    norm(n - 1, 1 - j)
                tiles(act, tile)
                norm(NT - 1, 1)

            @block.vector
            def _(dve):
                def scale(n, j):
                    dve.wait_ge(normed, n + 1)
                    dve.tensor_tensor(v[:, j, :], v[:, j, :], ln_g[:], ALU.mult).then_inc(scaled, 1)

                def tile(n, j, before=True):
                    dve.wait_ge(weighted, n + 1)
                    if not isinstance(n, int):
                        dve.wait_ge(shifted, n - 1)
                        dve.nop(nofuse=True)
                    s = dve.snap(seq_of(n, NT_SAMPLE)) if not isinstance(n, int) else 0
                    dve.scalar_tensor_tensor(out=v[:, j, :], in0=r[:, j, 1, :], scalar=flat(C.gate[:, one(n), 1:2]),
                                             in1=r[:, j, 0, :], op0=ALU.mult, op1=ALU.add).then_inc(ln, 1)
                    dve.wait_ge(ln, n * LN + SUM)
                    dve.nop(nofuse=True)
                    dve.tensor_tensor(v[:, j, :], v[:, j, :], flat(g2[:, one(s), :]), ALU.mult).then_inc(ln, 1)
                    dve.wait_ge(ln, n * LN + GATED)
                    dve.wait_ge(x1_here[j], n // 2 * 16 + 16)
                    dve.scalar_tensor_tensor(out=v[:, j, :], in0=x1[:, j, :], scalar=ALPHA, in1=v[:, j, :], op0=ALU.mult, op1=ALU.add).then_inc(ln, 1)
                    if before:
                        scale(n - 1, 1 - j)
                    dve.wait_ge(ln, n * LN + X1_ADDED)
                    for q in range(2):
                        dve.bn_stats(stats[:, q, :], v[:, j, q * WIDE:(q + 1) * WIDE]).then_inc(ln, 1)
                    dve.wait_ge(ln, n * LN + STATS1)
                    dve.nop(nofuse=True)
                    dve.bn_aggr(mean[:, j, :], flat(stats[:])).then_inc(ln, 1)

                dve.wait_ge(w_here, 64)
                tile(0, 0, before=False)
                tile(1, 1)
                tiles(dve, tile)
                scale(NT - 1, 1)
    S.clear()


class Kept:
    pass


def encoder(nc, A, out_sample, out_prompt, upto=99, debug=()):
    def scratch(name, shape, dt=F32):
        kind = "ExternalOutput" if name in debug else "Internal"
        return nc.dram_tensor(name, shape, dt, kind=kind).ap()

    with ExitStack() as ctx:
        C = Kept()
        S = Semaphores(nc, ctx)
        kept = lambda name, shape, dt=F32: ctx.enter_context(nc.sbuf_tensor(name, shape, dt))
        C.ident, C.le, C.ge, C.gt, C.lt, C.ones = (kept(n, [P, P]) for n in ("ident", "le", "ge", "gt", "lt", "ones"))
        C.minus_half = kept("minus_half", [P, 1])
        C.dt_raw = kept("dt_raw", [P, NT, 2 * HEADS])
        C.bank = [ctx.enter_context(nc.psum_tensor(f"bank{b}", [P, WIDE], F32)) for b in range(8)]
        C.dt, C.adt, C.dt_to_end, C.from_start, C.whole = (
            kept(n, [P, NT, 2 * HEADS]) for n in ("dt", "adt", "dt_to_end", "from_start", "whole"))
        mod = scratch("mod", [2, 6 * D])
        zs, u = scratch("zs", [TOK, SSD]), scratch("u", [TOK, SSD])
        raw, bc = scratch("raw", [CONV_CH, RAW_COLS]), scratch("bc", [CT - SSD // P, P, TOK])
        xb, y_ssd = scratch("xb", [TOK, SSD + 2 * STATE]), scratch("y_ssd", [TOK, SSD])
        constants(nc, C, S)
        with ExitStack() as of_w_in:
            C.w_in = of_w_in.enter_context(nc.sbuf_tensor("w_in", [P, KT, IN_COLS], F32))
            C.w_in_here = ctx.enter_context(nc.semaphore("w_in_here"))

            def load_w_in(sp):
                sp.dma_start(C.w_in[:], A["w_in"][0].rearrange("(p k) n -> p k n", p=P)).then_inc(C.w_in_here, 16)

            adapt(nc, C, S, A["c"], A["w_ada"][0], A["b_ada"], mod, range(0, 2), ahead=load_w_in)
            if upto < 1: return
            project(nc, C, S, A["x"], mod, zs, raw, u)
        if upto < 2: return
        convolve(nc, C, S, raw, A["conv_w"], A["conv_b"], xb, bc)
        decays(nc, C, S, A["ssd_dt_bias"], A["ssd_a_log"])
        with ExitStack() as of_ssd:
            C.h_back = of_ssd.enter_context(nc.sbuf_tensor("h_back", [P, NT + 2, SSD], F32))
            scan_back(nc, C, S, xb)
            scan_forward(nc, C, S, xb, bc, zs, A["ssd_d"], y_ssd)
        if upto < 3: return
        yg = scratch("yg", [TOK, SSD])
        with ExitStack() as of_s5:
            sb = lambda n, s: of_s5.enter_context(nc.sbuf_tensor(n, s, F32))
            C.states = sb("states", [P, C_S, 2, 2, 2 * PAIRS])
            C.power_y = [sb(f"power_y{c}", [P, PAIRS, 2, T5 + 1]) for c in range(2)]
            C.b_bar = sb("b_bar", [P, PAIRS, 2, 2, CH5])
            C.d5_diag = sb("d5_diag", [CH5, G5, CH5])
            turned = scratch("turned", [PAIRS, P, 2 * HALF * C_ALL])
            kernels = scratch("kernels", [2, 2, CH5, (2 * T5 - 1) * CH5])
            with ExitStack() as of_states:
                sb = lambda n, s: of_states.enter_context(nc.sbuf_tensor(n, s, F32))
                C.power_w = [sb(f"power_w{c}", [P, PAIRS, 2, T5]) for c in range(2)]
                C.carry_re, C.carry_im = sb("carry_re", [P, 2, 2 * PAIRS]), sb("carry_im", [P, 2, 2 * PAIRS])
                s5_tables(nc, C, S, A["s5_lam_re"], A["s5_lam_im"], A["s5_log_step"], A["s5_b_re"], A["s5_b_im"], A["s5_d"])
                s5_states_in(nc, C, S, u, turned)
                t1, t2 = sb("car_t1", [P, 2, 2, 2 * PAIRS]), sb("car_t2", [P, 2, 2, 2 * PAIRS])
                carried = S("carried")
                adapt(nc, C, S, A["c"], A["w_ada"][0], A["b_ada"], mod, range(2, 6), beside=lambda dve: s5_carry(dve, C, carried, t1, t2))
            s5_outputs(nc, C, S, turned, kernels, A["s5_c_re"], A["s5_c_im"], yg)
        if upto < 4: return
        C.logits, C.gate = kept("logits", [P, NT, NE]), kept("gate", [P, NT, 2])
        C.blocks_end = kept("blocks_end", [P, NE], I32)
        C.dest, C.expert, C.source = kept("dest", [P, NT, 2], I32), kept("expert", [P, NBLK], I32), kept("source", [P, NBLK], I32)
        C.mix_loads = 16 * 13
        x1, h = scratch("x1", [TOK, D]), scratch("h", [TOK, D])
        mix_out(nc, C, S, y_ssd, yg, A["x"], mod, A, x1, h)
        if upto < 5: return
        C.route_placed = 86
        row_token = scratch("row_token", [ROWS, 1], I32)
        route(nc, C, S, A["b_router"], row_token)
        if upto < 6: return
        rows_out = scratch("rows_out", [ROWS, D])
        experts(nc, C, S, h, A["w_gate"][0], A["w_up"][0], A["w_down"][0], rows_out)
        combine(nc, C, S, rows_out, x1, mod, A["ln2_g"], A["ln2_b"], out_sample, out_prompt)


def layout(a):
    a = dict(a)
    t = np.ascontiguousarray
    for n in ("x", "c"):
        if n not in a:
            a[n] = np.concatenate([a[n + "_sample"].reshape(-1, D), a[n + "_prompt"].reshape(-1, D)])
            del a[n + "_sample"], a[n + "_prompt"]
    a["conv_w"] = t(a["conv_w"][0].T.reshape(CT, P, TAPS).transpose(1, 0, 2))
    a["conv_b"] = t(a["conv_b"][0].reshape(CT, P).T)
    for n in ("ssd_dt_bias", "ssd_a_log"):
        a[n] = a[n].reshape(1, 2 * HEADS)
    for n in ("ssd_norm_w", "s5_b_glu"):
        a[n] = t(a[n][0].reshape(-1, P).T)
    a["b_router"] = a["b_router"].reshape(1, NE)
    by_state = lambda x: t(x.reshape(2, PAIRS, 2, N5).transpose(2, 3, 1, 0).reshape(P, 2 * PAIRS))
    a["s5_lam_re"], a["s5_lam_im"] = by_state(a["s5_lam_re"][0]), by_state(a["s5_lam_im"][0])
    a["s5_log_step"] = t(a["s5_log_step"][0].reshape(2, PAIRS, 2).transpose(2, 1, 0).reshape(2, 2 * PAIRS))
    for n in ("s5_b_re", "s5_b_im"):
        a[n] = t(a[n][0].reshape(PAIRS, 2, N5, CH5).transpose(1, 2, 0, 3).reshape(P, PAIRS, CH5))
    for n in ("s5_c_re", "s5_c_im"):
        a[n] = t(a[n][0].reshape(2, PAIRS, 2, CH5, N5).transpose(2, 4, 1, 0, 3).reshape(P, PAIRS, 2, CH5))
    return a


OUTPUTS = ((1, PROMPT, D), (1, SAMPLE, D))


def kernel(**inputs):
    import concourse.bacc as bacc
    from concourse.bass_utils import run_bass_kernel_spmd

    nc = bacc.Bacc("TRN2", target_bir_lowering=False, num_devices=1)
    arrays, aps = {}, {}
    for name, a in layout({n: np.asarray(v) for n, v in inputs.items()}).items():
        arrays[f"in_{name}"] = np.ascontiguousarray(a)
        aps[name] = nc.dram_tensor(f"in_{name}", a.shape, mybir.dt.from_np(a.dtype), kind="ExternalInput").ap()
    outs = [nc.dram_tensor(f"out_{i}", s, F32, kind="ExternalOutput").ap() for i, s in enumerate(OUTPUTS)]
    encoder(nc, aps, outs[1], outs[0])
    r = run_bass_kernel_spmd(nc, [arrays], core_ids=[0]).results[0]
    return r["out_0"], r["out_1"]
```

```python
from contextlib import ExitStack

import numpy as np

import concourse.bass as bass
from concourse import mybir

F32 = mybir.dt.float32
I32 = mybir.dt.int32
ALU = mybir.AluOpType
ACT = mybir.ActivationFunctionType
AX = mybir.AxisListType

P = 128
D = 1024
SAMPLE, PROMPT = 2048, 1024
TOK = SAMPLE + PROMPT
KT = D // P
WIDE = 512
NWIDE = TOK // WIDE
WIDE_SAMPLE = SAMPLE // WIDE
TPW = WIDE // P
NT = TOK // P
NT_SAMPLE = SAMPLE // P
EPS = 1e-5
ALPHA = 2.0 ** 0.25

SSD = 512
HEADS, HD = 8, 64
STATE = 128
CONV_CH, TAPS = 1024, 5
CT = CONV_CH // P
HALO = TAPS // 2
Z0, XBC0, DT0, U0 = 0, SSD, SSD + CONV_CH, SSD + CONV_CH + 2 * HEADS
IN_COLS = U0 + SSD
RAW_COLS = TOK + 4 * HALO

G5, CH5, N5 = 32, 16, 64
PAIRS = G5 // 2
T5 = 16
C_S, C_P = SAMPLE // T5, PROMPT // T5
C_ALL = C_S + C_P
HALF = T5 * CH5 // P
SPK = T5 // HALF

NE, NG, EPG, DE = 16, 4, 4, 512
BLK = 128
NBLK = 2 * TOK // BLK + NE - 1
ROWS = NBLK * BLK


class Semaphores:

    def __init__(self, nc, ctx):
        self.nc, self.ctx, self.made = nc, ctx, 0
        self.free, self.used = [], []

    def __call__(self, name, pool_dma=False):
        if self.free and not pool_dma:
            s = self.free.pop()
        else:
            s = self.ctx.enter_context(self.nc.semaphore(f"count{self.made}_{name}"))
            self.made += 1
        if not pool_dma:
            self.used.append(s)
        return s

    def clear(self):
        with self.nc.Block() as block:
            @block.gpsimd
            def _(pool):
                for s in self.used:
                    pool.sem_clear(s)
        self.free += self.used[::-1]
        self.used = []


class Steps:

    def __init__(self, eng, sem, turn=None, per_turn=0, before=0):
        self.eng, self.sem, self.turn, self.per_turn, self.n, self.before = eng, sem, turn, per_turn, 0, before

    def done(self, ins):
        ins.then_inc(self.sem, 1)
        self.n += 1

    def wait(self, back=0):
        at = self.before + self.n - back
        self.eng.wait_ge(self.sem, at if self.turn is None else self.turn * self.per_turn + at)

    def then(self, ins):
        self.done(ins)
        self.wait()

    def end_turn(self):
        assert self.n == self.per_turn, (self.n, self.per_turn)


def seq_of(turn, turns_of_sample):
    return turn // turns_of_sample


def constants(nc, C, S):
    made = S("made")
    with nc.Block() as block:
        @block.gpsimd
        def _(pool):
            steps = Steps(pool, made)
            steps.done(pool.memset(C.ident[:], 0.0))
            for t in (C.le, C.ge, C.gt, C.lt, C.ones):
                steps.done(pool.memset(t[:], 1.0))
            steps.done(pool.memset(C.minus_half[:], -0.5))
            steps.wait()
            for t, sign, op, fill in ((C.ident, 1, ALU.not_equal, 1.0), (C.le, 1, ALU.is_ge, 0.0), (C.ge, -1, ALU.is_ge, 0.0),
                                      (C.gt, -1, ALU.is_gt, 0.0), (C.lt, 1, ALU.is_gt, 0.0)):
                steps.done(pool.affine_select(out=t[:], in_=t[:], compare_op=op, fill=fill, base=0, pattern=[[sign, P]],
                                              channel_multiplier=-sign))
            steps.wait()
    S.clear()


def adapt(nc, C, S, c_all, w_ada, b_ada, mod, kinds, ahead=None, beside=None):
    PIECE = 512
    lo, hi = kinds.start * D, kinds.stop * D
    TURNS = (hi - lo) // PIECE // 2
    w = w_ada.rearrange("(p k) n -> p k n", p=P)
    with ExitStack() as ctx:
        sb = lambda n, s: ctx.enter_context(nc.sbuf_tensor(f"ada{lo}_{n}", s, F32))
        ct, cs = sb("ct", [P, 2, KT]), sb("cs", [P, KT, 2])
        wt = sb("wt", [P, 2, KT, PIECE])
        rows, bias = sb("rows", [2, hi - lo]), sb("bias", [2, hi - lo])
        acc = C.bank[0:2]
        c_in, b_in, act_c, mm, kept, added, out = (S(n) for n in ("c_in", "b_in", "act_c", "mm", "kept", "added", "out"))
        w_in = [S(f"w_in{j}") for j in range(2)]
        with nc.Block() as block:
            @block.sync
            def _(sp):
                sp.dma_start(ct[:], c_all.rearrange("s (p k) -> p s k", p=P)).then_inc(c_in, 16)
                for j in range(2):
                    sp.dma_start(wt[:, j], w[:, :, lo + j * PIECE:lo + (j + 1) * PIECE]).then_inc(w_in[j], 16)
                for s in range(2):
                    sp.dma_start(bias[s:s + 1, :], b_ada[:, lo:hi]).then_inc(b_in, 16)
                with sp.Fori(0, TURNS - 1) as t:
                    for j in range(2):
                        sp.wait_ge(mm, t * 2 + j + 1)
                        sp.dma_start(wt[:, j], w[:, :, bass.ds((t * 2 + j + 2) * PIECE + lo, PIECE)]).then_inc(w_in[j], 16)
                if ahead:
                    ahead(sp)
                sp.wait_ge(added, 1)
                sp.dma_start(mod[:, lo:hi], rows[:]).then_inc(out, 16)
                sp.wait_ge(out, 16)

            @block.gpsimd
            def _(pool):
                pool.wait_ge(b_in, 32)
                pool.wait_ge(kept, 2 * TURNS)
                pool.tensor_tensor(rows[:], rows[:], bias[:], ALU.add).then_inc(added, 1)

            @block.scalar
            def _(act):
                act.wait_ge(c_in, 16)
                act.activation(cs[:], ct[:].rearrange("p s k -> p k s"), ACT.Silu).then_inc(act_c, 1)
                with act.Fori(0, TURNS) as t:
                    for j in range(2):
                        act.wait_ge(mm, t * 2 + j + 1)
                        act.nop(nofuse=True)
                        act.activation(rows[:, bass.ds((t * 2 + j) * PIECE, PIECE)], acc[j][0:2, :], ACT.Copy).then_inc(kept, 1)

            @block.tensor
            def _(pe):
                pe.wait_ge(act_c, 1)
                with pe.Fori(0, TURNS) as t:
                    for j in range(2):
                        pe.wait_ge(w_in[j], t * 16 + 16)
                        pe.wait_ge(kept, t * 2)
                        for k in range(KT):
                            mul = pe.matmul(acc[j][0:2, :], cs[:, k, :], wt[:, j, k, :], start=k == 0, stop=k == KT - 1)
                        mul.then_inc(mm, 1)

            @block.vector
            def _(dve):
                if beside:
                    beside(dve)
    S.clear()


def project(nc, C, S, x, mod, zs, raw, u):
    TURNS = NWIDE // 2
    SAMPLE_TURNS = WIDE_SAMPLE // 2
    RING = 4
    OUTS = CT + 2 * TPW
    with ExitStack() as ctx:
        sb = lambda n, s: ctx.enter_context(nc.sbuf_tensor("pro_" + n, s, F32))
        w = C.w_in
        xt = sb("xt", [P, 2, TPW, D])
        ht = sb("ht", [P, 2, KT, WIDE])
        scale, shift = sb("scale", [P, 2, KT]), sb("shift", [P, 2, KT])
        zero = sb("zero", [P, CT, 2 * HALO])
        stage = sb("stage", [P, RING, WIDE])
        turned, acc, dt_acc = C.bank[0:2], C.bank[2:2 + RING], C.bank[6]
        mod_here, one_added, zeroed, padded = (S(n) for n in ("mod_here", "one_added", "zeroed", "padded"))
        x_here = [S(f"x_here{j}", pool_dma=True) for j in range(2)]
        transposed, h_ready, product, staged, dt_mm, dt_kept = (
            S(n) for n in ("transposed", "h_ready", "product", "staged", "dt_mm", "dt_kept"))
        stored = [S(f"stored{r}") for r in range(RING)]
        with nc.Block() as block:
            @block.gpsimd
            def _(pool):
                with pool.Fori(0, TURNS) as t:
                    for j in range(2):
                        pool.wait_ge(transposed, t * 2 * KT)
                        pool.dma_start(xt[:, j], x[bass.ds((t * 2 + j) * WIDE, WIDE), :].rearrange(
                            "(a p) n -> p a n", p=P)).then_inc(x_here[j], 16)

            @block.sync
            def _(sp):
                for kind, sc in ((1, scale), (0, shift)):
                    sp.dma_start(sc[:], mod[:, kind * D:(kind + 1) * D].rearrange("s (p k) -> p s k", p=P)).then_inc(mod_here, 16)
                sp.wait_ge(zeroed, 1)
                rows = raw.rearrange("(c p) n -> p c n", p=P)
                for at, n in ((0, HALO), (HALO + SAMPLE, 2 * HALO), (RAW_COLS - HALO, HALO)):
                    sp.dma_start(rows[:, :, at:at + n], zero[:, :, 0:n]).then_inc(padded, 16)
                with sp.Fori(0, TURNS) as t:
                    for j in range(2):
                        m = t * 2 + j
                        col = m * WIDE + HALO + seq_of(t, SAMPLE_TURNS) * (2 * HALO)
                        for o in range(OUTS):
                            sp.wait_ge(staged, m * OUTS + o + 1)
                            r = o % RING
                            if o < CT:
                                to = raw[o * P:(o + 1) * P, bass.ds(col, WIDE)]
                            else:
                                to = (zs if o < CT + TPW else u)[bass.ds(m * WIDE + (o - CT) % TPW * P, P), :]
                            sp.dma_start(to, stage[:, r, :]).then_inc(stored[r], 16)
                sp.wait_ge(padded, 48)
                for r in range(RING):
                    sp.wait_ge(stored[r], 16 * NWIDE * OUTS // RING)

            @block.vector
            def _(dve):
                dve.memset(zero[:], 0.0).then_inc(zeroed, 1)
                dve.wait_ge(mod_here, 32)
                dve.tensor_scalar(scale[:], scale[:], 1.0, None, ALU.add).then_inc(one_added, 1)
                dve.wait_ge(one_added, 1)
                with dve.Fori(0, TURNS) as t:
                    s = seq_of(t, SAMPLE_TURNS)
                    for j in range(2):
                        m = t * 2 + j
                        for k in range(KT):
                            dve.wait_ge(transposed, m * KT + k + 1)
                            dve.tensor_scalar(ht[:, j, k, :], turned[k % 2][:, :], scale[:, bass.ds(s, 1), k:k + 1].rearrange("p a b -> p (a b)"),
                                              shift[:, bass.ds(s, 1), k:k + 1].rearrange("p a b -> p (a b)"),
                                              ALU.mult, ALU.add).then_inc(h_ready, 1)
                        dve.wait_ge(dt_mm, m + 1)
                        dve.tensor_copy(C.dt_raw[:, bass.ds(m * TPW, TPW), :],
                                        dt_acc[:, 0:TPW * 2 * HEADS].rearrange("p (a c) -> p a c", a=TPW)).then_inc(dt_kept, 1)

            @block.tensor
            def _(pe):
                def turn(m, j, k):
                    if k == 0:
                        pe.wait_ge(x_here[j], m // 2 * 16 + 16)
                    if k >= 2:
                        pe.wait_ge(h_ready, m * KT + k - 1)
                    else:
                        pe.wait_ge(h_ready, m * KT)
                    for a in range(TPW):
                        tr = pe.transpose(turned[k % 2][:, a * P:(a + 1) * P], xt[:, j, a, k::KT], C.ident[:])
                    tr.then_inc(transposed, 1)

                def products(m, j, more=True):
                    pe.wait_ge(h_ready, (m + 1) * KT)
                    pe.wait_ge(dt_kept, m)
                    for a in range(TPW):
                        for k in range(KT):
                            mul = pe.matmul(dt_acc[:, a * 2 * HEADS:(a + 1) * 2 * HEADS], ht[:, j, k, a * P:(a + 1) * P],
                                            w[:, k, DT0:DT0 + 2 * HEADS], start=k == 0, stop=k == KT - 1)
                    mul.then_inc(dt_mm, 1)
                    for o in range(OUTS):
                        if o >= RING:
                            pe.wait_ge(staged, m * OUTS + o - RING + 1)
                        else:
                            pe.wait_ge(staged, m * OUTS)
                        for k in range(KT):
                            if o < CT:
                                left, right = w[:, k, XBC0 + o * P:XBC0 + (o + 1) * P], ht[:, j, k, :]
                            else:
                                a = (o - CT) % TPW
                                at = Z0 if o < CT + TPW else U0
                                left, right = ht[:, j, k, a * P:(a + 1) * P], w[:, k, at:at + SSD]
                            mul = pe.matmul(acc[o % RING][:, :], left, right, start=k == 0, stop=k == KT - 1)
                        mul.then_inc(product, 1)
                        if more and 1 <= o <= KT:
                            turn(m + 1, 1 - j, o - 1)

                for k in range(KT):
                    turn(0, 0, k)
                pe.wait_ge(C.w_in_here, 16)
                with pe.Fori(0, TURNS - 1) as t:
                    for j in range(2):
                        products(t * 2 + j, j)
                products(NWIDE - 2, 0)
                products(NWIDE - 1, 1, more=False)

            @block.scalar
            def _(act):
                with act.Fori(0, TURNS) as t:
                    for j in range(2):
                        m = t * 2 + j
                        for o in range(OUTS):
                            r = o % RING
                            act.wait_ge(product, m * OUTS + o + 1)
                            act.wait_ge(stored[r], (m * (OUTS // RING) + o // RING) * 16)
                            act.activation(stage[:, r, :], acc[r][:, :],
                                           ACT.Silu if CT <= o < CT + TPW else ACT.Copy).then_inc(staged, 1)
    S.clear()


def convolve(nc, C, S, raw, conv_w, conv_b, xb, bc):
    TURNS = NWIDE // 2
    BY_DVE = 5
    BY_PE = CT - BY_DVE
    XB = SSD // P + 2
    with ExitStack() as ctx:
        sb = lambda n, s: ctx.enter_context(nc.sbuf_tensor("con_" + n, s, F32))
        cw, cb = sb("cw", [P, CT, TAPS]), sb("cb", [P, CT])
        diag = sb("diag", [P, BY_PE, TAPS, P])
        src = sb("src", [P, 2, CT, WIDE + 2 * HALO])
        acc = sb("acc", [P, 2, BY_DVE, WIDE])
        out = sb("out", [P, 2, CT, WIDE])
        rows = sb("rows", [P, 2, XB * P])
        sums, turned = C.bank[0:BY_PE], C.bank[4:8]
        w_here, diag_made, taps, summed, activated, transposed, rows_ready = (
            S(n) for n in ("w_here", "diag_made", "taps", "summed", "activated", "transposed", "rows_ready"))
        src_here = [S(f"src_here{j}", pool_dma=True) for j in range(2)]
        bc_stored, rows_stored = ([S(f"{n}{j}") for j in range(2)] for n in ("bc_stored", "rows_stored"))
        order = [*range(BY_DVE, CT), *range(BY_DVE)]
        with nc.Block() as block:
            @block.sync
            def _(sp):
                sp.dma_start(cw[:], conv_w).then_inc(w_here, 16)
                sp.dma_start(cb[:], conv_b).then_inc(w_here, 16)
                with sp.Fori(0, TURNS) as t:
                    for j in range(2):
                        m = t * 2 + j
                        sp.wait_ge(activated, (m + 1) * CT)
                        sp.nop(nofuse=True)
                        sp.dma_start(bc[:, :, bass.ds(m * WIDE, WIDE)].rearrange("c p n -> p c n"),
                                     out[:, j, SSD // P:CT, :]).then_inc(bc_stored[j], 16)
                        for a in range(TPW):
                            sp.wait_ge(rows_ready, m * TPW + a + 1)
                            sp.nop(nofuse=True)
                            sp.dma_start(xb[bass.ds(m * WIDE + a * P, P), :], rows[:, a % 2, :]).then_inc(rows_stored[a % 2], 16)
                for j in range(2):
                    sp.wait_ge(bc_stored[j], 16 * TURNS)
                    sp.wait_ge(rows_stored[j], 16 * NT // 2)

            @block.gpsimd
            def _(pool):
                for j in range(2):
                    pool.dma_start(src[:, j], raw[:, j * WIDE:(j + 1) * WIDE + 2 * HALO].rearrange("(c p) n -> p c n", p=P)).then_inc(src_here[j], 16)
                pool.wait_ge(w_here, 32)
                for c in range(BY_PE):
                    for k in range(TAPS):
                        pool.tensor_scalar(diag[:, c, k, :], C.ident[:], cw[:, BY_DVE + c, k:k + 1], None, ALU.mult).then_inc(diag_made, 1)
                with pool.Fori(1, TURNS) as t:
                    for j in range(2):
                        m = t * 2 + j
                        col = pool.snap(m * WIDE + seq_of(t, WIDE_SAMPLE // 2) * (2 * HALO))
                        pool.wait_ge(taps, (m - 1) * BY_DVE * TAPS)
                        pool.wait_ge(summed, (m - 1) * BY_PE)
                        pool.nop(nofuse=True)
                        pool.dma_start(src[:, j], raw[:, bass.ds(col, WIDE + 2 * HALO)].rearrange("(c p) n -> p c n", p=P)).then_inc(src_here[j], 16)

            @block.vector
            def _(dve):
                dve.wait_ge(w_here, 32)
                with dve.Fori(0, TURNS) as t:
                    steps = Steps(dve, taps, t, 2 * BY_DVE * TAPS)
                    for j in range(2):
                        dve.wait_ge(src_here[j], t * 16 + 16)
                        dve.wait_ge(activated, t * 2 * CT)
                        for k in range(TAPS):
                            for c in range(BY_DVE):
                                x = src[:, j, c, k:k + WIDE]
                                if k == 0:
                                    steps.done(dve.tensor_scalar(acc[:, j, c, :], x, cw[:, c, 0:1], None, ALU.mult))
                                else:
                                    steps.wait(back=BY_DVE - 1)
                                    steps.done(dve.scalar_tensor_tensor(out=acc[:, j, c, :], in0=x, scalar=cw[:, c, k:k + 1],
                                                                        in1=acc[:, j, c, :], op0=ALU.mult, op1=ALU.add))
                    steps.end_turn()

            @block.tensor
            def _(pe):
                pe.wait_ge(diag_made, BY_PE * TAPS)
                with pe.Fori(0, TURNS) as t:
                    for j in range(2):
                        m = t * 2 + j
                        pe.wait_ge(src_here[j], t * 16 + 16)
                        pe.wait_ge(activated, m * CT)
                        for c in range(BY_PE):
                            for k in range(TAPS):
                                mul = pe.matmul(sums[c][:, :], diag[:, c, k, :], src[:, j, BY_DVE + c, k:k + WIDE],
                                                start=k == 0, stop=k == TAPS - 1)
                            mul.then_inc(summed, 1)
                        pe.wait_ge(activated, (m + 1) * CT)
                        for a in range(TPW):
                            if a >= 2:
                                pe.wait_ge(rows_ready, m * TPW + a - 1)
                            else:
                                pe.wait_ge(rows_ready, m * TPW)
                            for c in range(XB):
                                tr = pe.transpose(turned[a % 2 * 2 + c // 4][:, c % 4 * P:(c % 4 + 1) * P],
                                                  out[:, j, c, a * P:(a + 1) * P], C.ident[:])
                            tr.then_inc(transposed, 1)

            @block.scalar
            def _(act):
                act.wait_ge(w_here, 32)
                with act.Fori(0, TURNS) as t:
                    for j in range(2):
                        m = t * 2 + j
                        act.wait_ge(bc_stored[j], t * 16)
                        act.wait_ge(transposed, t * 2 * TPW)
                        for n, c in enumerate(order):
                            if c >= BY_DVE:
                                act.wait_ge(summed, m * BY_PE + c - BY_DVE + 1)
                                x = sums[c - BY_DVE][:, :]
                            else:
                                act.wait_ge(taps, m * BY_DVE * TAPS + BY_DVE * (TAPS - 1) + c + 1)
                                x = acc[:, j, c, :]
                            act.activation(out[:, j, c, :], x, ACT.Silu, bias=cb[:, c:c + 1]).then_inc(activated, 1)
                        for a in range(TPW):
                            act.wait_ge(transposed, m * TPW + a + 1)
                            act.wait_ge(rows_stored[a % 2], (m * TPW // 2 + a // 2) * 16)
                            act.activation(rows[:, a % 2, 0:4 * P], turned[a % 2 * 2][:, :], ACT.Copy)
                            act.activation(rows[:, a % 2, 4 * P:XB * P], turned[a % 2 * 2 + 1][:, 0:(XB - 4) * P],
                                           ACT.Copy).then_inc(rows_ready, 1)
    S.clear()


def decays(nc, C, S, dt_bias, a_log):
    H2 = 2 * HEADS
    with ExitStack() as ctx:
        sb = lambda n, s: ctx.enter_context(nc.sbuf_tensor("dec_" + n, s, F32))
        bias, alog, decay = sb("bias", [P, H2]), sb("alog", [P, H2]), sb("decay", [P, H2])
        v, w = sb("v", [P, NT, H2]), sb("w", [P, NT, H2])
        to_end = sb("to_end", [P, NT, H2])
        here, soft, expd, summed = (S(n) for n in ("here", "soft", "expd", "summed"))
        sums = [C.bank[n][:, 0:NT * HEADS].rearrange("p (c h) -> p c h", h=HEADS) for n in range(6)]
        fwd, bwd = slice(0, HEADS), slice(HEADS, H2)
        with nc.Block() as block:
            @block.sync
            def _(sp):
                sp.dma_start(bias[:], dt_bias.to_broadcast([P, H2])).then_inc(here, 16)
                sp.dma_start(alog[:], a_log.to_broadcast([P, H2])).then_inc(here, 16)

            @block.vector
            def _(dve):
                steps = Steps(dve, soft)
                wide = lambda t: t[:].unsqueeze(1).to_broadcast([P, NT, H2])
                dve.wait_ge(here, 32)
                steps.then(dve.tensor_tensor(v[:], C.dt_raw[:], wide(bias), ALU.add))
                steps.then(dve.tensor_scalar(w[:], v[:], -1.0, None, ALU.mult))
                steps.then(dve.tensor_tensor(w[:], w[:], v[:], ALU.min))
                dve.wait_ge(expd, 3)
                steps.then(dve.tensor_scalar(v[:], v[:], 0.0, None, ALU.max))
                steps.then(dve.tensor_tensor(C.dt[:], v[:], w[:], ALU.add))
                steps.then(dve.tensor_tensor(v[:], C.dt[:], wide(decay), ALU.mult))
                steps.then(dve.tensor_scalar(C.adt[:], v[:], -1.0, None, ALU.mult))
                dve.wait_ge(expd, 9)
                steps.done(dve.tensor_tensor(C.dt_to_end[:], C.dt[:], to_end[:], ALU.mult))

            @block.scalar
            def _(act):
                steps = Steps(act, expd)
                act.wait_ge(here, 32)
                steps.done(act.activation(decay[:], alog[:], ACT.Exp))
                act.wait_ge(soft, 3)
                steps.then(act.activation(w[:], w[:], ACT.Exp))
                steps.then(act.activation(w[:], w[:], ACT.Ln, bias=1.0))
                for n, to in enumerate((C.from_start[:, :, fwd], to_end[:, :, fwd], C.whole[:, :, fwd],
                                        C.from_start[:, :, bwd], to_end[:, :, bwd], C.whole[:, :, bwd])):
                    act.wait_ge(summed, n + 1)
                    steps.done(act.activation(to, sums[n], ACT.Exp))

            @block.tensor
            def _(pe):
                pe.wait_ge(soft, 7)
                for n, (mask, heads) in enumerate(((C.le, fwd), (C.gt, fwd), (C.ones, fwd), (C.ge, bwd), (C.lt, bwd), (C.ones, bwd))):
                    pe.matmul(sums[n], mask[:], C.adt[:, :, heads], start=True, stop=True).then_inc(summed, 1)
    S.clear()


def slot_of(chunk, turn):
    return chunk + seq_of(turn, NT_SAMPLE // 2)


def scan_back(nc, C, S, xb):
    TURNS = NT // 2
    with ExitStack() as ctx:
        sb = lambda n, s: ctx.enter_context(nc.sbuf_tensor("bac_" + n, s, F32))
        rows = sb("rows", [P, 2, SSD + 2 * STATE])
        xw, held = sb("xw", [P, 2, SSD]), sb("held", [P, SSD])
        rows_here = [S(f"rows_here{j}") for j in range(2)]
        weighted, states, carried, held_ready = (S(n) for n in ("weighted", "states", "carried", "held_ready"))
        wide = lambda t: t.rearrange("p a h -> p (a h)").unsqueeze(2).to_broadcast([P, HEADS, HD])
        by_head = lambda t: t.rearrange("p (h d) -> p h d", h=HEADS)
        back = slice(HEADS, 2 * HEADS)
        with nc.Block() as block:
            @block.sync
            def _(sp):
                for j in range(2):
                    sp.dma_start(rows[:, j, :], xb[(NT - 1 - j) * P:(NT - j) * P, :]).then_inc(rows_here[j], 16)
                with sp.Fori(1, TURNS) as t:
                    for j in range(2):
                        row = sp.snap((NT - 1 - t * 2 - j) * P)
                        sp.wait_ge(states, t * 2 + j - 1)
                        sp.nop(nofuse=True)
                        sp.dma_start(rows[:, j, :], xb[bass.ds(row, P), :]).then_inc(rows_here[j], 16)

            @block.gpsimd
            def _(pool):
                with pool.Fori(0, TURNS) as t:
                    for j in range(2):
                        c = pool.snap(NT - 1 - t * 2 - j)
                        pool.wait_ge(rows_here[j], t * 16 + 16)
                        pool.nop(nofuse=True)
                        pool.wait_ge(states, t * 2)
                        pool.nop(nofuse=True)
                        pool.tensor_tensor(by_head(xw[:, j, :]), by_head(rows[:, j, 0:SSD]),
                                           wide(C.dt_to_end[:, bass.ds(c, 1), back]), ALU.mult).then_inc(weighted, 1)

            @block.tensor
            def _(pe):
                with pe.Fori(0, TURNS) as t:
                    for j in range(2):
                        pe.wait_ge(weighted, t * 2 + j + 1)
                        pe.wait_ge(carried, t * 2)
                        for g in range(2):
                            mul = pe.matmul(C.bank[j][:, g * 256:(g + 1) * 256], rows[:, j, SSD + g * STATE:SSD + (g + 1) * STATE],
                                            xw[:, j, g * 256:(g + 1) * 256], start=True, stop=True)
                        mul.then_inc(states, 1)

            @block.vector
            def _(dve):
                dve.memset(C.h_back[:, bass.ds(NT_SAMPLE, 1), :], 0.0).then_inc(held_ready, 1)
                dve.memset(C.h_back[:, bass.ds(NT + 1, 1), :], 0.0).then_inc(held_ready, 1)
                dve.wait_ge(held_ready, 2)
                with dve.Fori(0, TURNS) as t:
                    for j in range(2):
                        m = t * 2 + j
                        c = dve.snap(NT - 1 - m)
                        slot = dve.snap(c + seq_of(TURNS - 1 - t, NT_SAMPLE // 2))
                        dve.wait_ge(carried, m)
                        dve.nop(nofuse=True)
                        dve.tensor_tensor(by_head(held[:]), by_head(C.h_back[:, bass.ds(slot + 1, 1), :].rearrange("p a n -> p (a n)")),
                                          wide(C.whole[:, bass.ds(c, 1), back]), ALU.mult).then_inc(held_ready, 1)
                        dve.wait_ge(held_ready, m + 3)
                        dve.wait_ge(states, m + 1)
                        dve.nop(nofuse=True)
                        dve.tensor_tensor(C.h_back[:, bass.ds(slot, 1), :].rearrange("p a n -> p (a n)"), held[:], C.bank[j][:, :],
                                          ALU.add).then_inc(carried, 1)
    S.clear()


def scan_forward(nc, C, S, xb, bc, zs, d_skip, y_ssd):
    with ExitStack() as ctx:
        sb = lambda n, s: ctx.enter_context(nc.sbuf_tensor("fwd_" + n, s, F32))
        h_fore = sb("h_fore", [P, NT + 2, SSD])
        rows, chan, z = sb("rows", [P, 2, SSD + 2 * STATE]), sb("chan", [P, 2, 4, P]), sb("z", [P, 2, SSD])
        sums_f, sums_b = sb("sums_f", [P, HEADS, P]), sb("sums_b", [P, HEADS, P])
        decay, mix = sb("decay", [P, HEADS, P]), sb("mix", [P, 2, HEADS, P])
        weight, weight_f, weight_b = (sb(n, [P, HEADS, P]) for n in ("weight", "weight_f", "weight_b"))
        xw, skip, held = sb("xw", [P, 2, SSD]), sb("skip", [P, 2, SSD]), sb("held", [P, SSD])
        y, off, off_b = sb("y", [P, 2, SSD]), sb("off", [P, 2, SSD]), sb("off_b", [P, SSD])
        square, total, root = sb("square", [P, SSD]), sb("total", [P, 2]), sb("root", [P, 2])
        d = sb("d", [P, HEADS])
        cb, seg, self_y, fore_y, back_y, states = (C.bank[0], C.bank[1:3], C.bank[3], C.bank[4], C.bank[5], C.bank[6:8])
        d_here, cleared, masked, expd, skipped, xw_ready, rooted, squared = (
            S(n) for n in ("d_here", "cleared", "masked", "expd", "skipped", "xw_ready", "rooted", "squared"))
        cb_mm, seg_mm, self_mm, off_mm, states_mm = (S(n) for n in ("cb_mm", "seg_mm", "self_mm", "off_mm", "states_mm"))
        weight_f_made, weight_b_made = S("weight_f_made"), S("weight_b_made")
        weighted, mixed, off_read, carried, summed, normed = (
            S(n) for n in ("weighted", "mixed", "off_read", "carried", "summed", "normed"))
        rows_here, chan_here, z_here, stored = ([S(f"{n}{j}") for j in range(2)] for n in ("rows_here", "chan_here", "z_here", "stored"))
        by_head = lambda t: t.rearrange("p (h d) -> p h d", h=HEADS)
        wide = lambda t, n: t.rearrange("p a h -> p (a h)").unsqueeze(2).to_broadcast([P, HEADS, n])
        tri = lambda t: t[:].unsqueeze(1).to_broadcast([P, HEADS, P])
        flat = lambda a: a.rearrange("p a n -> p (a n)")
        fwd, bwd = slice(0, HEADS), slice(HEADS, 2 * HEADS)
        one = lambda n: bass.ds(n, 1) if not isinstance(n, int) else slice(n, n + 1)
        slot_of_chunk = lambda m: m if isinstance(m, int) else m + seq_of(m, NT_SAMPLE)
        piece = lambda m: bass.ds(m * P, P) if not isinstance(m, int) else slice(m * P, (m + 1) * P)

        later = lambda m: not isinstance(m, int) or m >= 2

        def chunks(eng, body, last=NT):
            with eng.Fori(1, last // 2) as t:
                for j in range(2):
                    body(t * 2 + j, j)

        with nc.Block() as block:
            @block.sync
            def _(sp):
                def load(m, j, later=True):
                    if later:
                        sp.wait_ge(self_mm, m - 1)
                        sp.nop(nofuse=True)
                    sp.dma_start(rows[:, j, :], xb[piece(m), :]).then_inc(rows_here[j], 16)
                    sp.dma_start(chan[:, j], bc[:, :, piece(m)].rearrange("c p n -> p c n")).then_inc(chan_here[j], 16)
                    if later:
                        sp.wait_ge(summed, (m - 1) * 2)
                        sp.nop(nofuse=True)
                    sp.dma_start(z[:, j, :], zs[piece(m), :]).then_inc(z_here[j], 16)

                def store(m, j):
                    sp.wait_ge(normed, m + 1)
                    sp.nop(nofuse=True)
                    sp.dma_start(y_ssd[piece(m), :], y[:, j, :]).then_inc(stored[j], 16)

                load(0, 0, later=False)
                load(1, 1, later=False)
                sp.dma_start(d[:], d_skip.to_broadcast([P, HEADS])).then_inc(d_here, 16)

                def chunk(m, j):
                    load(m, j)
                    store(m - 2, j)
                chunks(sp, chunk)
                store(NT - 2, 0)
                store(NT - 1, 1)
                for j in range(2):
                    sp.wait_ge(stored[j], 16 * NT // 2)

            @block.gpsimd
            def _(pool):
                def prepare(m, j):
                    pool.wait_ge(seg_mm, m)
                    pool.nop(nofuse=True)
                    pool.tensor_tensor(sums_f[:], tri(C.le), wide(C.adt[:, one(m), fwd], P), ALU.mult).then_inc(masked, 1)
                    pool.tensor_tensor(sums_b[:], tri(C.ge), wide(C.adt[:, one(m), bwd], P), ALU.mult).then_inc(masked, 1)
                    pool.wait_ge(rows_here[j], m // 2 * 16 + 16)
                    pool.nop(nofuse=True)
                    if later(m):
                        pool.wait_ge(self_mm, m - 1)
                        pool.nop(nofuse=True)
                    pool.tensor_tensor(by_head(xw[:, j, :]), by_head(rows[:, j, 0:SSD]),
                                       wide(C.dt_to_end[:, one(m), fwd], HD), ALU.mult).then_inc(xw_ready, 1)
                    pool.tensor_tensor(by_head(skip[:, j, :]), by_head(rows[:, j, 0:SSD]),
                                       d[:].unsqueeze(2).to_broadcast([P, HEADS, HD]), ALU.mult).then_inc(skipped, 1)

                    pool.wait_ge(weighted, m)
                    pool.nop(nofuse=True)
                    pool.tensor_tensor(weight_b[:], tri(C.ge), wide(C.dt[:, one(m), bwd], P), ALU.mult).then_inc(weight_b_made, 1)

                def find_root(m, j):
                    pool.wait_ge(squared, m + 1)
                    pool.nop(nofuse=True)
                    pool.tensor_scalar(root[:, j:j + 1], total[:, j:j + 1], 1.0 / SSD, EPS, ALU.mult, ALU.add).then_inc(rooted, 1)
                    pool.wait_ge(rooted, m * 2 + 1)
                    pool.tensor_tensor(root[:, j:j + 1], root[:, j:j + 1], C.minus_half[:], ALU.pow).then_inc(rooted, 1)

                pool.wait_ge(d_here, 16)
                prepare(0, 0)
                prepare(1, 1)

                def chunk(m, j):
                    prepare(m, j)
                    find_root(m - 2, j)
                chunks(pool, chunk)
                find_root(NT - 2, 0)
                find_root(NT - 1, 1)

            @block.tensor
            def _(pe):
                def start(m, j):
                    pe.wait_ge(expd, m * 2)
                    pe.wait_ge(masked, m * 2 + 2)
                    for q in range(2):
                        heads = slice(q * 4, q * 4 + 4)
                        pe.matmul(seg[q][:, :], C.gt[:], sums_f[:, heads, :], start=True, stop=False)
                        mul = pe.matmul(seg[q][:, :], C.lt[:], sums_b[:, heads, :], start=False, stop=True)
                    mul.then_inc(seg_mm, 1)
                    pe.wait_ge(xw_ready, m + 1)
                    if later(m):
                        pe.wait_ge(carried, (m - 1) * 2)
                    for g in range(2):
                        mul = pe.matmul(states[j][:, g * 256:(g + 1) * 256], rows[:, j, SSD + g * STATE:SSD + (g + 1) * STATE],
                                        xw[:, j, g * 256:(g + 1) * 256], start=True, stop=True)
                    mul.then_inc(states_mm, 1)
                    pe.wait_ge(chan_here[j], m // 2 * 16 + 16)
                    pe.wait_ge(mixed, m * 2)
                    for g in range(2):
                        mul = pe.matmul(cb[:, g * P:(g + 1) * P], chan[:, j, g, :], chan[:, j, 2 + g, :], start=True, stop=True)
                    mul.then_inc(cb_mm, 1)

                def enter(m, j):
                    pe.wait_ge(cleared, 2)
                    pe.wait_ge(carried, m * 2)
                    pe.wait_ge(off_read, m * 3)
                    pe.nop(nofuse=True)
                    slot = slot_of_chunk(m)
                    for bank, held_in, at in ((back_y, C.h_back, slot + 1), (fore_y, h_fore, slot)):
                        for g in range(2):
                            mul = pe.matmul(bank[:, g * 256:(g + 1) * 256], chan[:, j, 2 + g, :],
                                            flat(held_in[:, one(at), g * 256:(g + 1) * 256]), start=True, stop=True)
                    mul.then_inc(off_mm, 1)

                def within(m, j, first=False):
                    pe.wait_ge(skipped, m + 1)
                    if not first:
                        pe.wait_ge(summed, m * 2)
                    pe.matmul(self_y[:, :], C.ident[:], skip[:, j, :], start=True, stop=False)
                    pe.wait_ge(mixed, (m + 1) * 2)
                    for h in range(HEADS):
                        mul = pe.matmul(self_y[:, h * HD:(h + 1) * HD], mix[:, j, h, :], rows[:, j, h * HD:(h + 1) * HD],
                                        start=False, stop=h == HEADS - 1)
                    mul.then_inc(self_mm, 1)

                start(0, 0)
                enter(0, 0)
                start(1, 1)
                within(0, 0, first=True)
                enter(1, 1)

                def chunk(m, j):
                    start(m, j)
                    within(m - 1, 1 - j)
                    enter(m, j)
                chunks(pe, chunk)
                within(NT - 1, 1)

            @block.scalar
            def _(act):
                def exps(m):
                    act.wait_ge(seg_mm, m + 1)
                    act.wait_ge(mixed, m * 2)
                    for q in range(2):
                        act.activation(decay[:, q * 4:q * 4 + 4, :], seg[q][:, :].rearrange("p (h n) -> p h n", h=4),
                                       ACT.Exp).then_inc(expd, 1)

                def squares(m, j):
                    act.wait_ge(summed, (m + 1) * 2)
                    if later(m):
                        act.wait_ge(rooted, m * 2 - 2)
                    act.activation(square[:], y[:, j, :], ACT.Square, accum_out=total[:, j:j + 1]).then_inc(squared, 1)

                def weight_fore(m):
                    act.wait_ge(weighted, m)
                    act.nop(nofuse=True)
                    for h in range(HEADS):
                        put = act.activation(weight_f[:, h, :], C.le[:], ACT.Copy, scale=flat(C.dt[:, one(m), h:h + 1]))
                    put.then_inc(weight_f_made, 1)

                weight_fore(0)
                exps(0)
                weight_fore(1)
                exps(1)
                weight_fore(2)
                squares(0, 0)

                def chunk(m, j):
                    exps(m)
                    weight_fore(m + 1)
                    squares(m - 1, 1 - j)
                chunks(act, chunk, last=NT - 2)
                chunk(NT - 2, 0)
                exps(NT - 1)
                squares(NT - 2, 0)
                squares(NT - 1, 1)

            @block.vector
            def _(dve):
                def begin(m, j, scale_last=True):
                    at = one(m)
                    slot = dve.snap(slot_of_chunk(m)) if not isinstance(m, int) else m
                    if scale_last:
                        scale(m - 2, j)
                    dve.wait_ge(carried, m * 2)
                    dve.nop(nofuse=True)
                    dve.tensor_tensor(by_head(held[:]), by_head(flat(h_fore[:, one(slot), :])), wide(C.whole[:, at, fwd], HD),
                                      ALU.mult).then_inc(carried, 1)
                    dve.wait_ge(weight_f_made, m + 1)
                    dve.wait_ge(weight_b_made, m + 1)
                    dve.tensor_tensor(weight[:], weight_f[:], weight_b[:], ALU.add).then_inc(weighted, 1)
                    dve.wait_ge(states_mm, m + 1)
                    dve.wait_ge(carried, m * 2 + 1)
                    dve.nop(nofuse=True)
                    dve.tensor_tensor(flat(h_fore[:, one(slot + 1), :]), held[:], states[j][:, :], ALU.add).then_inc(carried, 1)
                    dve.wait_ge(expd, m * 2 + 2)
                    dve.wait_ge(weighted, m + 1)
                    dve.tensor_tensor(decay[:], decay[:], weight[:], ALU.mult).then_inc(mixed, 1)
                    dve.wait_ge(off_mm, m + 1)
                    dve.nop(nofuse=True)
                    dve.tensor_tensor(by_head(off[:, j, :]), by_head(fore_y[:, :]), wide(C.from_start[:, at, fwd], HD), ALU.mult).then_inc(off_read, 1)
                    dve.wait_ge(cb_mm, m + 1)
                    dve.wait_ge(mixed, m * 2 + 1)
                    if later(m):
                        dve.wait_ge(self_mm, m - 1)
                    dve.tensor_tensor(
                        mix[:, j].rearrange("p (g r) n -> p g r n", g=2), decay[:].rearrange("p (g r) n -> p g r n", g=2),
                        cb[:, 0:2 * P].rearrange("p (g n) -> p g n", g=2).unsqueeze(2).to_broadcast([P, 2, HEADS // 2, P]),
                        ALU.mult).then_inc(mixed, 1)
                    dve.nop(nofuse=True)
                    dve.tensor_tensor(by_head(off_b[:]), by_head(back_y[:, :]), wide(C.from_start[:, at, bwd], HD), ALU.mult).then_inc(off_read, 1)

                def add_self(m, j):
                    dve.wait_ge(self_mm, m + 1)
                    dve.wait_ge(off_read, (m + 1) * 3)
                    if later(m):
                        dve.wait_ge(stored[j], m // 2 * 16)
                    dve.tensor_tensor(y[:, j, :], off[:, j, :], self_y[:, :], ALU.add).then_inc(summed, 1)

                def add_off(m, j):
                    dve.wait_ge(off_read, m * 3 + 2)
                    dve.tensor_tensor(off[:, j, :], off[:, j, :], off_b[:], ALU.add).then_inc(off_read, 1)

                def gate(m, j):
                    dve.wait_ge(z_here[j], m // 2 * 16 + 16)
                    dve.wait_ge(summed, m * 2 + 1)
                    dve.tensor_tensor(y[:, j, :], y[:, j, :], z[:, j, :], ALU.mult).then_inc(summed, 1)

                def scale(m, j):
                    dve.wait_ge(rooted, (m + 1) * 2)
                    dve.nop(nofuse=True)
                    dve.tensor_scalar(y[:, j, :], y[:, j, :], root[:, j:j + 1], None, ALU.mult).then_inc(normed, 1)

                dve.memset(h_fore[:, 0, :], 0.0).then_inc(cleared, 1)
                dve.memset(h_fore[:, NT_SAMPLE + 1, :], 0.0).then_inc(cleared, 1)
                dve.wait_ge(cleared, 2)
                begin(0, 0, scale_last=False)
                add_off(0, 0)
                begin(1, 1, scale_last=False)
                add_self(0, 0)
                add_off(1, 1)
                gate(0, 0)

                def chunk(m, j):
                    begin(m, j)
                    add_self(m - 1, 1 - j)
                    add_off(m, j)
                    gate(m - 1, 1 - j)
                chunks(dve, chunk)
                scale(NT - 2, 0)
                add_self(NT - 1, 1)
                gate(NT - 1, 1)
                scale(NT - 1, 1)
    S.clear()


def s5_tables(nc, C, S, lam_re, lam_im, log_step, b_re, b_im, d_skip):
    PD = PAIRS * 2
    with ExitStack() as ctx:
        sb = lambda n, s, dt=F32: ctx.enter_context(nc.sbuf_tensor("tab_" + n, s, dt))
        lr, li, ls = sb("lr", [P, PD]), sb("li", [P, PD]), sb("ls", [P, PD])
        b = [sb(f"b{n}", [P, PAIRS, CH5]) for n in range(2)]
        v = {n: sb(n, [P, PD]) for n in ("x", "k", "r", "p", "q", "step", "mag", "sin", "cos", "f", "g", "fr", "fi")}
        whole = sb("whole", [P, PD], I32)
        bit = sb("bit", [P, PD], I32)
        power = [sb(f"power{n}", [P, T5 + 1, PD]) for n in range(2)]
        t1, t2 = sb("t1", [P, 8, PD]), sb("t2", [P, 8, PD])
        u1, u2 = sb("u1", [P, PAIRS, 2, CH5]), sb("u2", [P, PAIRS, 2, CH5])
        d5 = ctx.enter_context(nc.sbuf_tensor("tab_d5", [CH5, SSD], F32))
        here, done = S("here"), S("done")
        with nc.Block() as block:
            @block.sync
            def _(sp):
                for to, a in ((lr, lam_re), (li, lam_im), (b[0], b_re), (b[1], b_im)):
                    sp.dma_start(to[:], a).then_inc(here, 16)
                for g in range(2):
                    sp.dma_start(ls[g * N5:(g + 1) * N5, :], log_step[g:g + 1, :].to_broadcast([N5, PD])).then_inc(here, 16)
                sp.dma_start(d5[:], d_skip.to_broadcast([CH5, SSD])).then_inc(here, 16)

            @block.vector
            def _(dve):
                steps = Steps(dve, done)
                ts = lambda o, a, s1, op0, s2=None, op1=ALU.bypass: steps.then(dve.tensor_scalar(o, a, s1, s2, op0, op1))
                tt = lambda o, a, c, op: steps.then(dve.tensor_tensor(o, a, c, op))
                stt = lambda o, a, s, c, op0, op1: steps.then(
                    dve.scalar_tensor_tensor(out=o, in0=a, scalar=s, in1=c, op0=op0, op1=op1))
                A = {n: t[:] for n, t in v.items()}
                ROUND = 12582912.0

                def exp(out, x):
                    ts(A["x"], x, -87.0, ALU.max, 88.0, ALU.min)
                    ts(A["k"], A["x"], 1.44269504, ALU.mult, ROUND, ALU.add)
                    ts(A["k"], A["k"], -ROUND, ALU.add)
                    stt(A["r"], A["k"], -0.693359375, A["x"], ALU.mult, ALU.add)
                    stt(A["r"], A["k"], 2.12194440e-4, A["r"], ALU.mult, ALU.add)
                    ts(A["p"], A["r"], 1.9875691500e-4, ALU.mult)
                    for c in (1.3981999507e-3, 8.3334519073e-3, 4.1665795894e-2, 1.6666665459e-1, 5.0000001201e-1):
                        stt(A["p"], A["p"], c, A["r"], ALU.add, ALU.mult)
                    tt(A["p"], A["p"], A["r"], ALU.mult)
                    tt(A["p"], A["p"], A["r"], ALU.add)
                    ts(A["p"], A["p"], 1.0, ALU.add)
                    ts(A["k"], A["k"], 127.0, ALU.add)
                    steps.then(dve.tensor_copy(whole[:], A["k"]))
                    ts(whole[:], whole[:], 23, ALU.logical_shift_left)
                    tt(out, A["p"], whole[:].bitcast(F32), ALU.mult)

                dve.wait_ge(here, 16 * 7)
                tt(C.d5_diag[:], d5[:].rearrange("p (g i) -> p g i", i=CH5),
                   C.ident[0:CH5, 0:CH5].unsqueeze(1).to_broadcast([CH5, G5, CH5]), ALU.mult)
                ts(lr[:], lr[:], -1e-4, ALU.min)
                exp(A["step"], ls[:])
                tt(A["q"], lr[:], A["step"], ALU.mult)
                exp(A["mag"], A["q"])
                tt(A["x"], li[:], A["step"], ALU.mult)
                ts(A["k"], A["x"], 0.63661977, ALU.mult, ROUND, ALU.add)
                ts(A["k"], A["k"], -ROUND, ALU.add)
                stt(A["r"], A["k"], -1.5703125, A["x"], ALU.mult, ALU.add)
                stt(A["r"], A["k"], -4.837512969970703e-4, A["r"], ALU.mult, ALU.add)
                stt(A["r"], A["k"], -7.549789948768648e-8, A["r"], ALU.mult, ALU.add)
                tt(A["q"], A["r"], A["r"], ALU.mult)
                ts(A["p"], A["q"], -1.9515295891e-4, ALU.mult, 8.3321608736e-3, ALU.add)
                tt(A["p"], A["p"], A["q"], ALU.mult)
                stt(A["p"], A["p"], -1.6666654611e-1, A["q"], ALU.add, ALU.mult)
                tt(A["p"], A["p"], A["r"], ALU.mult)
                tt(A["sin"], A["p"], A["r"], ALU.add)
                ts(A["p"], A["q"], 2.443315711809948e-5, ALU.mult, -1.388731625493765e-3, ALU.add)
                tt(A["p"], A["p"], A["q"], ALU.mult)
                stt(A["p"], A["p"], 4.166664568298827e-2, A["q"], ALU.add, ALU.mult)
                tt(A["p"], A["p"], A["q"], ALU.mult)
                stt(A["p"], A["q"], -0.5, A["p"], ALU.mult, ALU.add)
                ts(A["cos"], A["p"], 1.0, ALU.add)
                steps.then(dve.tensor_copy(whole[:], A["k"]))
                ts(bit[:], whole[:], 1, ALU.bitwise_and)
                steps.then(dve.tensor_copy(A["f"], bit[:]))
                ts(A["g"], A["f"], -1.0, ALU.mult, 1.0, ALU.add)
                tt(A["x"], A["sin"], A["g"], ALU.mult)
                tt(A["p"], A["cos"], A["f"], ALU.mult)
                tt(A["x"], A["x"], A["p"], ALU.add)
                tt(A["p"], A["cos"], A["g"], ALU.mult)
                tt(A["q"], A["sin"], A["f"], ALU.mult)
                tt(A["p"], A["p"], A["q"], ALU.add)
                for of, out, by_k in ((A["x"], A["sin"], 0.0), (A["p"], A["cos"], 1.0)):
                    ts(A["r"], A["k"], by_k, ALU.add)
                    steps.then(dve.tensor_copy(whole[:], A["r"]))
                    ts(bit[:], whole[:], 2, ALU.bitwise_and)
                    steps.then(dve.tensor_copy(A["f"], bit[:]))
                    ts(A["f"], A["f"], -1.0, ALU.mult, 1.0, ALU.add)
                    tt(A["f"], A["f"], A["mag"], ALU.mult)
                    tt(out, of, A["f"], ALU.mult)
                ts(power[0][:, 0, :], A["cos"], 0.0, ALU.mult, 1.0, ALU.add)
                ts(power[1][:, 0, :], A["cos"], 0.0, ALU.mult)
                steps.then(dve.tensor_copy(power[0][:, 1, :], A["cos"]))
                steps.then(dve.tensor_copy(power[1][:, 1, :], A["sin"]))
                n = 1
                while n < T5:
                    by = [power[c][:, n:n + 1, :].to_broadcast([P, n, PD]) for c in range(2)]
                    x = [power[c][:, 1:n + 1, :] for c in range(2)]
                    for out, op, pairs in ((0, ALU.subtract, ((0, 0), (1, 1))), (1, ALU.add, ((0, 1), (1, 0)))):
                        for t, (p, q) in zip((t1, t2), pairs):
                            tt(t[:, 0:n, :], x[p], by[q], ALU.mult)
                        tt(power[out][:, n + 1:2 * n + 1, :], t1[:, 0:n, :], t2[:, 0:n, :], op)
                    n *= 2
                for c in range(2):
                    w = power[c][:].rearrange("p q (a d) -> p a d q", d=2)
                    steps.then(dve.tensor_copy(C.power_w[c][:, :, 0, :], w[:, :, 0, 0:T5]))
                    steps.then(dve.tensor_copy(C.power_w[c][:, :, 1, :], w[:, :, 1, T5 - 1::-1]))
                    steps.then(dve.tensor_copy(C.power_y[c][:, :, 0, :], w[:, :, 0, :]))
                    steps.then(dve.tensor_copy(C.power_y[c][:, :, 1, :], w[:, :, 1, ::-1]))
                    steps.then(dve.tensor_copy(C.carry_re[:, c, :], power[0][:, T5, :]))
                ts(C.carry_im[:, 0, :], power[1][:, T5, :], -1.0, ALU.mult)
                steps.then(dve.tensor_copy(C.carry_im[:, 1, :], power[1][:, T5, :]))
                ts(A["cos"], A["cos"], -1.0, ALU.add)
                tt(A["x"], lr[:], lr[:], ALU.mult)
                tt(A["p"], li[:], li[:], ALU.mult)
                tt(A["x"], A["x"], A["p"], ALU.add)
                steps.then(dve.reciprocal(A["x"], A["x"]))
                for out, op, (p, q) in (("fr", ALU.add, (("cos", lr), ("sin", li))), ("fi", ALU.subtract, (("sin", lr), ("cos", li)))):
                    tt(A["q"], A[p[0]], p[1][:], ALU.mult)
                    tt(A["p"], A[q[0]], q[1][:], ALU.mult)
                    tt(A["q"], A["q"], A["p"], op)
                    tt(A[out], A["q"], A["x"], ALU.mult)
                f = [A[n].rearrange("p (a d) -> p a d", d=2).unsqueeze(3).to_broadcast([P, PAIRS, 2, CH5]) for n in ("fr", "fi")]
                bb = [t[:].unsqueeze(2).to_broadcast([P, PAIRS, 2, CH5]) for t in b]
                for out, op, (p, q) in ((0, ALU.subtract, ((0, 0), (1, 1))), (1, ALU.add, ((0, 1), (1, 0)))):
                    tt(u1[:], f[p[0]], bb[p[1]], ALU.mult)
                    tt(u2[:], f[q[0]], bb[q[1]], ALU.mult)
                    tt(C.b_bar[:, :, out], u1[:], u2[:], op)
    S.clear()


def s5_states_in(nc, C, S, u, turned_dram):
    TURNS = PAIRS // 2
    BOTH = 2 * T5 * CH5
    with ExitStack() as ctx:
        sb = lambda n, s: ctx.enter_context(nc.sbuf_tensor("sin_" + n, s, F32))
        us, up = sb("us", [C_S, T5, SSD]), sb("up", [C_P, T5, SSD])
        ps, pp = sb("ps", [C_S, 2, BOTH]), sb("pp", [C_P, 2, BOTH])
        ut = sb("ut", [P, 2, 2, HALF, C_ALL])
        pre = sb("pre", [P, 2, 2, 2, T5 * CH5])
        w = sb("w", [P, 2, 2, HALF, 2, P])
        t1, t2 = sb("t1", [P, 2, T5 * CH5]), sb("t2", [P, 2, T5 * CH5])
        u_here, picked_s, picked_p, made, dve_made, turned, ut_ready, turned_w, w_ready, added, read_out = (
            S(n) for n in ("u_here", "picked_s", "picked_p", "made", "dve_made", "turned", "ut_ready", "turned_w", "w_ready", "added", "read_out"))
        stored = [S(f"stored{j}") for j in range(2)]
        PRE = 6
        ub, wb, sums = C.bank[0:2], C.bank[2:4], C.bank[4:8]
        later = lambda m: not isinstance(m, int) or m >= 2
        one = lambda n: bass.ds(n, 1) if not isinstance(n, int) else slice(n, n + 1)

        def pairs(eng, body):
            body(0, 0)
            body(1, 1)
            with eng.Fori(1, TURNS) as t:
                for j in range(2):
                    body(t * 2 + j, j)

        def pick(eng, turned, to, of, picked, m, j):
            if later(m):
                eng.wait_ge(turned, m - 1)
                eng.nop(nofuse=True)
            at = eng.snap(m * 2 * CH5) if not isinstance(m, int) else m * 2 * CH5
            for g in range(2):
                put = eng.tensor_copy(to[:, j, g * T5 * CH5:(g + 1) * T5 * CH5].rearrange("p (t i) -> p t i", i=CH5)[:, ::-1],
                                      of[:, :, bass.ds(at + g * CH5, CH5)])
            put.then_inc(picked, 1)

        with nc.Block() as block:
            @block.sync
            def _(sp):
                sp.dma_start(us[:], u[0:SAMPLE, :].rearrange("(c t) n -> c t n", t=T5)).then_inc(u_here, 16)
                sp.dma_start(up[:], u[SAMPLE:TOK, :].rearrange("(c t) n -> c t n", t=T5)).then_inc(u_here, 16)

                def pair(m, j):
                    sp.wait_ge(ut_ready, m * 2 + 2)
                    sp.nop(nofuse=True)
                    sp.dma_start(turned_dram[one(m)].rearrange("a p n -> p (a n)"),
                                 ut[:, j].rearrange("p g k c -> p (g k c)")).then_inc(stored[j], 16)
                pairs(sp, pair)
                for j in range(2):
                    sp.wait_ge(stored[j], 16 * TURNS)

            @block.gpsimd
            def _(pool):
                pool.wait_ge(u_here, 32)
                pairs(pool, lambda m, j: pick(pool, turned, pp, up, picked_p, m, j))

            @block.vector
            def _(dve):
                def weights(m, j):
                    steps = Steps(dve, dve_made, m, PRE)
                    if later(m):
                        dve.wait_ge(turned_w, m - 1)
                        dve.nop(nofuse=True)
                    power = [C.power_w[c][:, one(m)].rearrange("p a d t -> p (a d) t").unsqueeze(3).to_broadcast([P, 2, T5, CH5]) for c in range(2)]
                    b = [C.b_bar[:, one(m), c].rearrange("p a d i -> p (a d) i").unsqueeze(2).to_broadcast([P, 2, T5, CH5]) for c in range(2)]
                    four = lambda x: x.rearrange("p d (t i) -> p d t i", i=CH5)
                    for out, op, (p, q) in ((0, ALU.subtract, ((0, 0), (1, 1))), (1, ALU.add, ((0, 1), (1, 0)))):
                        steps.done(dve.tensor_tensor(four(t1[:]), power[p[0]], b[p[1]], ALU.mult))
                        steps.then(dve.tensor_tensor(four(t2[:]), power[q[0]], b[q[1]], ALU.mult))
                        steps.then(dve.tensor_tensor(pre[:, j, out], t1[:], t2[:], op))
                    steps.end_turn()

                def read(m, j):
                    dve.wait_ge(added, m + 1)
                    dve.nop(nofuse=True)
                    for d in range(2):
                        way = slice(None, None, -1) if d else slice(None)
                        x = sums[2 * j + d][:, 0:2 * C_ALL].rearrange("p (r c) -> p c r", r=2)
                        to = C.states[:, :, :, :, one(m * 2 + d)].rearrange("p k r s a -> p k r (s a)")
                        dve.tensor_copy(to[:, 0:C_S, :, 0], x[:, 0:C_S, :][:, way, :])
                        put = dve.tensor_copy(to[:, 0:C_P, :, 1], x[:, C_S:C_ALL, :][:, way, :])
                    put.then_inc(read_out, 1)

                def pair(m, j):
                    pick(dve, turned, ps, us, picked_s, m, j)
                    weights(m, j)
                    if not isinstance(m, int) or m >= 1:
                        read(m - 1, 1 - j)

                dve.wait_ge(u_here, 32)
                pairs(dve, pair)
                read(PAIRS - 1, 1)

            @block.tensor
            def _(pe):
                def turn_u(m, j):
                    pe.wait_ge(picked_s, m + 1)
                    pe.wait_ge(picked_p, m + 1)
                    pe.wait_ge(ut_ready, m * 2)
                    for g in range(2):
                        for k in range(HALF):
                            n = g * HALF + k
                            pe.transpose(ub[0][:, n * C_S:(n + 1) * C_S], ps[:, j, n * P:(n + 1) * P], C.ident[0:C_S, 0:C_S])
                            tr = pe.transpose(ub[1][:, n * C_P:(n + 1) * C_P], pp[:, j, n * P:(n + 1) * P], C.ident[0:C_P, 0:C_P])
                    tr.then_inc(turned, 1)

                def turn_weights(m, j):
                    pe.wait_ge(dve_made, (m + 1) * PRE)
                    pe.wait_ge(w_ready, m * 2)
                    for r in range(2):
                        for k in range(HALF):
                            for d in range(2):
                                n = k * 2 + d
                                tr = pe.transpose(wb[r][:, n * P:(n + 1) * P], pre[:, j, r, d, k * P:(k + 1) * P], C.ident[:])
                    tr.then_inc(turned_w, 1)

                def products(m, j):
                    pe.wait_ge(ut_ready, m * 2 + 2)
                    pe.wait_ge(w_ready, m * 2 + 2)
                    if later(m):
                        pe.wait_ge(read_out, m - 1)
                    for d in range(2):
                        for r in range(2):
                            for g in range(2):
                                for k in range(HALF):
                                    mul = pe.matmul(sums[2 * j + d][g * N5:(g + 1) * N5, r * C_ALL:(r + 1) * C_ALL],
                                                    w[:, j, r, k, d, g * N5:(g + 1) * N5], ut[:, j, g, k, :],
                                                    start=k == 0, stop=k == HALF - 1)
                    mul.then_inc(added, 1)

                def pair(m, j):
                    turn_u(m, j)
                    if not isinstance(m, int) or m >= 1:
                        products(m - 1, 1 - j)
                    turn_weights(m, j)
                pairs(pe, pair)
                products(PAIRS - 1, 1)

            @block.scalar
            def _(act):
                def pair(m, j):
                    act.wait_ge(turned, m + 1)
                    if later(m):
                        act.wait_ge(stored[j], m // 2 * 16)
                        act.wait_ge(added, m - 1)
                    for s, (at, n) in enumerate(((0, C_S), (C_S, C_P))):
                        act.activation(ut[:, j, :, :, at:at + n].rearrange("p g k c -> p (g k) c"),
                                       ub[s][:, 0:4 * n].rearrange("p (a c) -> p a c", c=n), ACT.Copy).then_inc(ut_ready, 1)
                    act.wait_ge(turned_w, m + 1)
                    for r in range(2):
                        act.activation(w[:, j, r].rearrange("p k d n -> p (k d n)"), wb[r][:, :], ACT.Copy).then_inc(w_ready, 1)
                pairs(act, pair)
    S.clear()


def s5_carry(dve, C, done, t1, t2):
    before = 0
    for lo, hi, seqs, unroll in ((1, C_P, 2, 7), (C_P, C_S, 1, 8)):
        by = lambda t: t[:].unsqueeze(2).to_broadcast([P, 2, seqs, 2 * PAIRS])
        turns = (hi - lo) // unroll
        assert turns * unroll == hi - lo
        with dve.Fori(0, turns) as t:
            steps = Steps(dve, done, t, 4 * unroll, before)
            for n in range(unroll):
                k = t * unroll + lo + n
                at = lambda n: C.states[:, bass.ds(n, 1), :, 0:seqs, :].rearrange("p k r s n -> p (k r) s n")
                last, here = at(k - 1), at(k)
                steps.done(dve.tensor_tensor(t1[:, :, 0:seqs, :], by(C.carry_re), last, ALU.mult))
                steps.done(dve.tensor_tensor(t2[:, ::-1, 0:seqs, :], by(C.carry_im)[:, ::-1], last, ALU.mult))
                steps.wait(back=1)
                dve.nop(nofuse=True)
                steps.then(dve.tensor_tensor(here, here, t1[:, :, 0:seqs, :], ALU.add))
                steps.then(dve.tensor_tensor(here, here, t2[:, :, 0:seqs, :], ALU.add))
            steps.end_turn()
        before += 4 * (hi - lo)


def s5_outputs(nc, C, S, turned_dram, kernels, c_re, c_im, yg):
    TURNS = PAIRS // 2
    Q = T5 + 1
    TC = T5 * CH5
    LAGS = 2 * T5 - 1
    with ExitStack() as ctx:
        sb = lambda n, s: ctx.enter_context(nc.sbuf_tensor("out5_" + n, s, F32))
        c = [sb(f"c{n}", [P, PAIRS, 2, CH5]) for n in range(2)]
        e = sb("e", [P, 2, 2, 2, 2, Q * CH5])
        t1, t2 = sb("t1", [P, 2, Q * CH5]), sb("t2", [P, 2, Q * CH5])
        bs = sb("bs", [P, 2, 2, 2, CH5])
        lags = sb("lags", [CH5, 2, 2, LAGS * CH5])
        toe = sb("toe", [P, 2, 2, HALF, TC])
        ut = sb("ut", [P, 2, 2, HALF, C_ALL])
        st = sb("st", [P, 2, 2, 2, C_ALL])
        ys, yp = sb("ys", [C_S, T5, SSD]), sb("yp", [C_P, T5, SSD])
        c_here, dve_made, b_picked, zeroed, entered, kernel_mm, lag_steps, enter_mm, y_mm, gelued, out = (
            S(n) for n in ("c_here", "dve_made", "b_picked", "zeroed", "entered", "kernel_mm", "lag_steps", "enter_mm", "y_mm", "gelued", "out"))
        lags_stored, toe_here, ut_here = ([S(f"{n}{j}") for j in range(2)] for n in ("lags_stored", "toe_here", "ut_here"))
        kf, kb = C.bank[0:2]
        yb = C.bank[2:6]
        PRE, LAG = 8, 4
        later = lambda m: not isinstance(m, int) or m >= 2
        one = lambda n: bass.ds(n, 1) if not isinstance(n, int) else slice(n, n + 1)

        def pairs(eng, body, last=PAIRS):
            body(0, 0)
            body(1, 1)
            with eng.Fori(1, last // 2) as t:
                for j in range(2):
                    body(t * 2 + j, j)

        with nc.Block() as block:
            @block.sync
            def _(sp):
                sp.dma_start(c[0][:], c_re).then_inc(c_here, 16)
                sp.dma_start(c[1][:], c_im).then_inc(c_here, 16)

                def pair(m, j):
                    if later(m):
                        sp.wait_ge(y_mm, (m - 1) * 2)
                        sp.nop(nofuse=True)
                    sp.dma_start(ut[:, j].rearrange("p g k c -> p (g k c)"),
                                 turned_dram[one(m)].rearrange("a p n -> p (a n)")).then_inc(ut_here[j], 16)
                    sp.wait_ge(lag_steps, (m + 1) * LAG)
                    sp.nop(nofuse=True)
                    sp.dma_start(kernels[j].rearrange("g i n -> i g n"), lags[:, j]).then_inc(lags_stored[j], 16)
                    sp.wait_ge(lags_stored[j], m // 2 * 16 + 16)
                    sp.nop(nofuse=True)
                    for g in range(2):
                        for k in range(HALF):
                            rows = bass.AP(tensor=kernels.tensor, offset=((j * 2 + g) * CH5 * LAGS * CH5) + k * SPK * CH5,
                                           ap=[[CH5, SPK], [LAGS * CH5, CH5], [1, TC]])
                            sp.dma_start(toe[:, j, g, k, :], rows).then_inc(toe_here[j], 16)
                pairs(sp, pair)
                sp.wait_ge(gelued, 2 * PAIRS)
                sp.dma_start(yg[0:SAMPLE, :].rearrange("(c t) n -> c t n", t=T5), ys[:]).then_inc(out, 16)
                sp.dma_start(yg[SAMPLE:TOK, :].rearrange("(c t) n -> c t n", t=T5), yp[:]).then_inc(out, 16)
                sp.wait_ge(out, 32)

            @block.gpsimd
            def _(pool):
                pool.memset(e[:], 0.0).then_inc(zeroed, 1)
                pool.memset(st[:], 0.0).then_inc(zeroed, 1)
                pool.wait_ge(zeroed, 2)

                def pair(m, j):
                    if later(m):
                        pool.wait_ge(kernel_mm, m - 1)
                        pool.nop(nofuse=True)
                    pool.tensor_copy(bs[:, j], C.b_bar[:, one(m)].rearrange("p a r d i -> p (a r) d i")).then_inc(b_picked, 1)
                    if later(m):
                        pool.wait_ge(enter_mm, m - 1)
                        pool.nop(nofuse=True)
                    for d in range(2):
                        x = C.states[:, :, :, :, one(m * 2 + d)].rearrange("p k r s a -> p r k (s a)")
                        for s, (at, n) in enumerate(((0, C_S), (C_S, C_P))):
                            if d == 0:
                                put = pool.tensor_copy(st[:, j, :, d, at + 1:at + n], x[:, :, 0:n - 1, s])
                            else:
                                put = pool.tensor_copy(st[:, j, :, d, at:at + n - 1][:, :, ::-1], x[:, :, 0:n - 1, s])
                    put.then_inc(entered, 1)
                pairs(pool, pair)

            @block.vector
            def _(dve):
                dve.wait_ge(c_here, 32)
                dve.wait_ge(zeroed, 1)

                def pair(m, j):
                    steps, lag = Steps(dve, dve_made, m, PRE), Steps(dve, lag_steps, m, LAG)
                    if later(m):
                        dve.wait_ge(enter_mm, m - 1)
                        dve.nop(nofuse=True)
                    four = lambda x: x.rearrange("p d (q i) -> p d q i", i=CH5)
                    power = [C.power_y[r][:, one(m)].rearrange("p a d q -> p (a d) q").unsqueeze(3).to_broadcast([P, 2, Q, CH5]) for r in range(2)]
                    cc = [c[r][:, one(m)].rearrange("p a d i -> p (a d) i").unsqueeze(2).to_broadcast([P, 2, Q, CH5]) for r in range(2)]
                    steps.done(dve.tensor_tensor(four(t1[:]), cc[0], power[0], ALU.mult))
                    steps.then(dve.tensor_tensor(four(t2[:]), cc[1], power[1], ALU.mult))
                    for g in range(2):
                        own = slice(g * N5, (g + 1) * N5)
                        steps.done(dve.tensor_tensor(e[own, j, 0, :, g], t1[own], t2[own], ALU.subtract))
                    steps.wait()
                    steps.done(dve.tensor_tensor(four(t1[:]), cc[0], power[1], ALU.mult))
                    steps.then(dve.tensor_tensor(four(t2[:]), cc[1], power[0], ALU.mult))
                    for g in range(2):
                        own = slice(g * N5, (g + 1) * N5)
                        steps.done(dve.scalar_tensor_tensor(out=e[own, j, 1, :, g], in0=t1[own], scalar=-1.0, in1=t2[own],
                                                            op0=ALU.mult, op1=ALU.subtract))
                    steps.wait()
                    dve.wait_ge(kernel_mm, m + 1)
                    dve.wait_ge(lags_stored[j], m // 2 * 16)
                    dve.nop(nofuse=True)
                    to = lags[:, j]
                    f, b = (x[0:CH5, :].rearrange("p (g n) -> p g n", g=2) for x in (kf, kb))
                    L0 = (T5 - 1) * CH5
                    lag.done(dve.tensor_copy(to[:, :, 0:L0], b[:, :, 0:L0]))
                    lag.done(dve.tensor_copy(to[:, :, L0 + CH5:], f[:, :, CH5:TC]))
                    lag.then(dve.tensor_tensor(to[:, :, L0:L0 + CH5], f[:, :, 0:CH5], C.d5_diag[:, bass.ds(m * 2, 2) if not isinstance(m, int) else slice(m * 2, m * 2 + 2), :], ALU.add))
                    lag.then(dve.tensor_tensor(to[:, :, L0:L0 + CH5], b[:, :, L0:TC], to[:, :, L0:L0 + CH5], ALU.add))
                    steps.end_turn()
                    lag.end_turn()
                pairs(dve, pair)

            @block.tensor
            def _(pe):
                def kernel_of(m, j):
                    pe.wait_ge(dve_made, (m + 1) * PRE)
                    pe.wait_ge(b_picked, m + 1)
                    pe.wait_ge(lag_steps, m * LAG)
                    for d, bank in enumerate((kf, kb)):
                        for r in range(2):
                            mul = pe.matmul(bank[0:CH5, :].rearrange("p (g n) -> p g n", g=2), bs[:, j, r, d, :],
                                            e[:, j, r, d, :, d * CH5:d * CH5 + TC], start=r == 0, stop=r == 1)
                    mul.then_inc(kernel_mm, 1)

                def output(m, j):
                    pe.wait_ge(entered, m + 1)
                    if later(m):
                        pe.wait_ge(gelued, (m - 1) * 2)
                    chunks = ((0, C_S), (C_S, C_P))
                    for s, (at, n) in enumerate(chunks):
                        bank = yb[j * 2 + s][0:n, :].rearrange("p (g n) -> p g n", g=2)
                        for d in range(2):
                            for r in range(2):
                                mul = pe.matmul(bank, st[:, j, r, d, at:at + n], e[:, j, r, d, :, (1 - d) * CH5:(1 - d) * CH5 + TC],
                                                start=d == 0 and r == 0, stop=False)
                    mul.then_inc(enter_mm, 1)
                    pe.wait_ge(ut_here[j], m // 2 * 16 + 16)
                    pe.wait_ge(toe_here[j], (m // 2 + 1) * 16 * 2 * HALF)
                    for s, (at, n) in enumerate(chunks):
                        for g in range(2):
                            for k in range(HALF):
                                mul = pe.matmul(yb[j * 2 + s][0:n, g * TC:(g + 1) * TC], ut[:, j, g, k, at:at + n], toe[:, j, g, k, :],
                                                start=False, stop=g == 1 and k == HALF - 1)
                        mul.then_inc(y_mm, 1)

                def pair(m, j):
                    output(m, j)
                    kernel_of(m + 1, 1 - j)
                kernel_of(0, 0)
                pairs(pe, pair, last=PAIRS - 2)
                pair(PAIRS - 2, 0)
                output(PAIRS - 1, 1)

            @block.scalar
            def _(act):
                def pair(m, j):
                    cols = act.snap(m * 2 * CH5) if not isinstance(m, int) else m * 2 * CH5
                    for s, (y, n) in enumerate(((ys, C_S), (yp, C_P))):
                        act.wait_ge(y_mm, m * 2 + s + 1)
                        act.nop(nofuse=True)
                        act.activation(y[:, :, bass.ds(cols, 2 * CH5)].rearrange("p t (g i) -> p g t i", g=2),
                                       yb[j * 2 + s][0:n, :].rearrange("p (g t i) -> p g t i", g=2, t=T5), ACT.Gelu_apprx_tanh).then_inc(gelued, 1)
                pairs(act, pair)
    S.clear()


def load_across(eng, to, row, sem):
    eng.dma_start(to, row.to_broadcast([P, row.shape[-1]])).then_inc(sem, 16)


def mix_out(nc, C, S, y_ssd, yg, x, mod, W, x1_dram, h_dram):
    TURNS = NWIDE // 2
    KY = SSD // P
    EVENTS = 3 * KY
    with ExitStack() as ctx:
        sb = lambda n, s: ctx.enter_context(nc.sbuf_tensor("mix_" + n, s, F32))
        wg, wo, wr = sb("wg", [P, KY, SSD]), sb("wo", [P, KT, D]), sb("wr", [P, KT, NE])
        norm_w, b_glu = sb("norm_w", [P, KY]), sb("b_glu", [P, KY])
        g1, scale, shift = sb("g1", [P, 2, D]), sb("scale", [P, 2, D]), sb("shift", [P, 2, D])
        ln_g, ln_b = sb("ln_g", [P, D]), sb("ln_b", [P, D])
        ya, yb = sb("ya", [P, TPW, SSD]), sb("yb", [P, TPW, SSD])
        xt = sb("xt", [P, 2, TPW, D])
        yt, gt, sg = sb("yt", [P, 2, KT, WIDE]), sb("gt", [P, KY, WIDE]), sb("sg", [P, KY, WIDE])
        v, h, ht = sb("v", [P, 2, D]), sb("h", [P, 2, D]), sb("ht", [P, KT, P])
        stats, mean = sb("stats", [P, 2, 6]), sb("mean", [P, 2, 2])
        flat = lambda a: a.rearrange("p a n -> p (a n)")
        w_here, gate_here, y_here, one_added, turned, taken, gated, mixed, mix_read, ln, rooted, h_made = (
            S(n) for n in ("w_here", "gate_here", "y_here", "one_added", "turned", "taken", "gated", "mixed", "mix_read", "ln", "rooted", "h_made"))
        h_turned, h_taken, routed, kept = (S(n) for n in ("h_turned", "h_taken", "routed", "kept"))
        x_here, x1_stored, h_stored = ([S(f"{n}{j}") for j in range(2)] for n in ("x_here", "x1_stored", "h_stored"))
        LN = 8
        with nc.Block() as block:
            @block.sync
            def _(sp):
                loads = {gate_here: 0, w_here: 0}

                def load(to, src, here=w_here):
                    sp.dma_start(to, src).then_inc(here, 16)
                    loads[here] += 16

                def load_y(m):
                    wide = bass.ds(m * WIDE, WIDE) if not isinstance(m, int) else slice(m * WIDE, (m + 1) * WIDE)
                    sp.dma_start(yb[:], yg[wide, :].rearrange("(a p) n -> p a n", p=P)).then_inc(y_here, 16)
                    sp.dma_start(ya[:], y_ssd[wide, :].rearrange("(a p) n -> p a n", p=P)).then_inc(y_here, 16)

                def load_x(m, j):
                    wide = bass.ds(m * WIDE, WIDE) if not isinstance(m, int) else slice(m * WIDE, (m + 1) * WIDE)
                    sp.dma_start(xt[:, j], x[wide, :].rearrange("(a p) n -> p a n", p=P)).then_inc(x_here[j], 16)

                load(norm_w[:], W["ssd_norm_w"], gate_here)
                load(b_glu[:], W["s5_b_glu"], gate_here)
                load_y(0)
                load(wg[:], W["s5_w_glu"][0].rearrange("(k p) n -> p k n", p=P), gate_here)
                load(wo[:], W["w_out"][0].rearrange("(k p) n -> p k n", p=P))
                load_x(0, 0)
                load(wr[:], W["w_router"].rearrange("(k p) n -> p k n", p=P))
                for s in range(2):
                    for kind, to in ((2, g1), (4, scale), (3, shift)):
                        load(to[:, s, :], mod[s:s + 1, kind * D:(kind + 1) * D].to_broadcast([P, D]))
                load(ln_g[:], W["ln1_g"].to_broadcast([P, D]))
                load(ln_b[:], W["ln1_b"].to_broadcast([P, D]))
                assert (loads[gate_here], loads[w_here]) == (C.mix_gate_loads, C.mix_loads)
                sp.wait_ge(turned, EVENTS)
                load_y(1)
                load_x(1, 1)
                with sp.Fori(1, TURNS) as t:
                    for j in range(2):
                        m = t * 2 + j
                        sp.wait_ge(turned, m * EVENTS)
                        sp.nop(nofuse=True)
                        load_y(m)
                        sp.wait_ge(ln, (m - 1) * TPW * LN)
                        sp.nop(nofuse=True)
                        load_x(m, j)

            @block.gpsimd
            def _(pool):
                pool.wait_ge(w_here, C.mix_loads)
                pool.tensor_scalar(scale[:], scale[:], 1.0, None, ALU.add).then_inc(one_added, 1)
                pool.wait_ge(one_added, 1)
                with pool.Fori(0, TURNS) as t:
                    for j in range(2):
                        s = pool.snap(seq_of(t, WIDE_SAMPLE // 2))
                        for a in range(TPW):
                            r = a % 2
                            n = (t * 2 + j) * TPW + a
                            pool.wait_ge(ln, n * LN + 5)
                            pool.nop(nofuse=True)
                            pool.tensor_scalar(mean[:, r, 1:2], mean[:, r, 1:2], EPS, None, ALU.add).then_inc(rooted, 1)
                            pool.wait_ge(rooted, n * 2 + 1)
                            pool.tensor_tensor(mean[:, r, 1:2], mean[:, r, 1:2], C.minus_half[:], ALU.pow).then_inc(rooted, 1)
                            pool.wait_ge(h_turned, (n - r) * 2)
                            pool.nop(nofuse=True)
                            pool.wait_ge(h_stored[r], (t * 2 + j) * 32 + a // 2 * 16)
                            pool.nop(nofuse=True)
                            pool.wait_ge(ln, (n + 1) * LN)
                            pool.nop(nofuse=True)
                            pool.tensor_tensor(h[:, r, :], v[:, r, :], flat(scale[:, bass.ds(s, 1), :]), ALU.mult).then_inc(h_made, 1)
                            pool.wait_ge(h_made, n * 2 + 1)
                            pool.nop(nofuse=True)
                            pool.tensor_tensor(h[:, r, :], h[:, r, :], flat(shift[:, bass.ds(s, 1), :]), ALU.add).then_inc(h_made, 1)

            @block.vector
            def _(dve):
                dve.wait_ge(w_here, C.mix_loads)
                with dve.Fori(0, TURNS) as t:
                    steps = Steps(dve, ln, t, 2 * TPW * LN)
                    for j in range(2):
                        m = dve.snap(t * 2 + j)
                        s = dve.snap(seq_of(t, WIDE_SAMPLE // 2))
                        for k in range(KY):
                            dve.wait_ge(taken, m * EVENTS + 2 * KY + k + 1)
                            dve.tensor_tensor(yt[:, j, KY + k, :], sg[:, k, :], gt[:, k, :], ALU.mult).then_inc(gated, 1)
                        dve.wait_ge(x_here[j], t * 16 + 16)
                        for a in range(TPW):
                            r = a % 2
                            dve.wait_ge(mixed, m * TPW + a + 1)
                            dve.wait_ge(x1_stored[r], m * 32 + a // 2 * 16)
                            dve.wait_ge(h_made, m * 2 * TPW + (a - r) * 2)
                            dve.nop(nofuse=True)
                            banks = C.bank[2 + 2 * r:4 + 2 * r]
                            steps.done(dve.tensor_tensor(v[:, r, 0:WIDE], banks[0][:, :], flat(g1[:, bass.ds(s, 1), 0:WIDE]), ALU.mult))
                            dve.tensor_tensor(v[:, r, WIDE:D], banks[1][:, :], flat(g1[:, bass.ds(s, 1), WIDE:D]), ALU.mult).then_inc(mix_read, 1)
                            dve.wait_ge(mix_read, m * TPW + a + 1)
                            steps.then(dve.scalar_tensor_tensor(out=v[:, r, :], in0=xt[:, j, a, :], scalar=ALPHA, in1=v[:, r, :],
                                                                op0=ALU.mult, op1=ALU.add))
                            for q in range(2):
                                steps.done(dve.bn_stats(stats[:, q, :], v[:, r, q * WIDE:(q + 1) * WIDE]))
                            steps.wait()
                            dve.nop(nofuse=True)
                            steps.done(dve.bn_aggr(mean[:, r, :], flat(stats[:])))
                            dve.wait_ge(rooted, (m * TPW + a + 1) * 2)
                            steps.then(dve.tensor_scalar(v[:, r, :], v[:, r, :], mean[:, r, 0:1], mean[:, r, 1:2], ALU.subtract, ALU.mult))
                            steps.then(dve.tensor_tensor(v[:, r, :], v[:, r, :], ln_g[:], ALU.mult))
                            steps.done(dve.tensor_tensor(v[:, r, :], v[:, r, :], ln_b[:], ALU.add))
                    steps.end_turn()

            def in_order(turn_gate, products, turn_h, logits):
                def wide(m, j, more=True, first=False):
                    for a in range(TPW):
                        products(m, j, a, 0)
                        if a >= 2:
                            logits(m, a - 2)
                        elif not first:
                            logits(m - 1, a + 2)
                        products(m, j, a, 1)
                        if a:
                            turn_h(m, a - 1)
                        elif not first:
                            turn_h(m - 1, TPW - 1)
                    if more:
                        turn_gate(m + 1, 1 - j)
                return wide

            @block.tensor
            def _(pe):
                def turn_gate(m, j):
                    pe.wait_ge(y_here, (m + 1) * 32)
                    for e in range(2 * KY):
                        pe.wait_ge(taken, m * EVENTS + max(e - 1, 0))
                        k, src = e % KY, yb if e < KY else ya
                        for a in range(TPW):
                            tr = pe.transpose(C.bank[e % 2][:, a * P:(a + 1) * P], src[:, a, k * P:(k + 1) * P], C.ident[:])
                        tr.then_inc(turned, 1)
                    for c in range(KY):
                        pe.wait_ge(taken, m * EVENTS + 2 * KY + c - 1)
                        for k in range(KY):
                            mul = pe.matmul(C.bank[c % 2][:, :], wg[:, k, c * P:(c + 1) * P], gt[:, k, :], start=k == 0, stop=k == KY - 1)
                        mul.then_inc(turned, 1)

                def products(m, j, a, q):
                    if a == 0 and q == 0:
                        pe.wait_ge(gated, (m + 1) * KY)
                    if q == 0:
                        pe.wait_ge(mix_read, m * TPW + max(a - 1, 0))
                    for k in range(KT):
                        mul = pe.matmul(C.bank[2 + 2 * (a % 2) + q][:, :], yt[:, j, k, a * P:(a + 1) * P], wo[:, k, q * WIDE:(q + 1) * WIDE],
                                        start=k == 0, stop=k == KT - 1)
                    if q == 1:
                        mul.then_inc(mixed, 1)

                def turn_h(m, a):
                    n = m * TPW + a
                    pe.wait_ge(h_made, n * 2 + 2)
                    pe.wait_ge(h_taken, n * 2)
                    pe.wait_ge(kept, n)
                    for q in range(2):
                        for k in range(4):
                            tr = pe.transpose(C.bank[6 + q][:, k * P:(k + 1) * P], h[:, a % 2, (q * 4 + k) * P:(q * 4 + k + 1) * P], C.ident[:])
                        tr.then_inc(h_turned, 1)

                def logits(m, a):
                    n = m * TPW + a
                    pe.wait_ge(h_taken, n * 2 + 2)
                    for k in range(KT):
                        mul = pe.matmul(C.bank[6][:, 0:NE], ht[:, k, :], wr[:, k, :], start=k == 0, stop=k == KT - 1)
                    mul.then_inc(routed, 1)

                pe.wait_ge(gate_here, C.mix_gate_loads)
                wide = in_order(turn_gate, products, turn_h, logits)
                turn_gate(0, 0)
                pe.wait_ge(w_here, C.mix_loads)
                wide(0, 0, first=True)
                wide(1, 1)
                with pe.Fori(1, TURNS - 1) as t:
                    for j in range(2):
                        wide(t * 2 + j, j)
                wide(NWIDE - 2, 0)
                wide(NWIDE - 1, 1, more=False)
                logits(NWIDE - 1, TPW - 2)
                turn_h(NWIDE - 1, TPW - 1)
                logits(NWIDE - 1, TPW - 1)

            @block.scalar
            def _(act):
                def turn_gate(m, j):
                    act.wait_ge(gated, m * KY)
                    for e in range(EVENTS):
                        act.wait_ge(turned, m * EVENTS + e + 1)
                        k, bank = e % KY, C.bank[e % 2][:, :]
                        if e < KY:
                            take = act.activation(gt[:, k, :], bank, ACT.Copy)
                        elif e < 2 * KY:
                            take = act.activation(yt[:, j, k, :], bank, ACT.Copy, scale=norm_w[:, k:k + 1])
                        else:
                            take = act.activation(sg[:, k, :], bank, ACT.Sigmoid, bias=b_glu[:, k:k + 1])
                        take.then_inc(taken, 1)

                def products(m, j, a, q):
                    pass

                def turn_h(m, a):
                    n, r = m * TPW + a, a % 2
                    rows = bass.ds(n * P, P) if not isinstance(n, int) else slice(n * P, (n + 1) * P)
                    act.wait_ge(ln, (n + 1) * LN)
                    act.nop(nofuse=True)
                    act.dma_start(x1_dram[rows, :], v[:, r, :]).then_inc(x1_stored[r], 16)
                    act.wait_ge(h_made, n * 2 + 2)
                    act.nop(nofuse=True)
                    act.dma_start(h_dram[rows, :], h[:, r, :]).then_inc(h_stored[r], 16)
                    act.wait_ge(routed, n)
                    for q in range(2):
                        act.wait_ge(h_turned, n * 2 + q + 1)
                        act.activation(ht[:, q * 4:q * 4 + 4, :].rearrange("p k n -> p (k n)"), C.bank[6 + q][:, :], ACT.Copy).then_inc(h_taken, 1)

                def logits(m, a):
                    n = m * TPW + a
                    act.wait_ge(routed, n + 1)
                    act.nop(nofuse=True)
                    where = bass.ds(n, 1) if not isinstance(n, int) else slice(n, n + 1)
                    act.activation(flat(C.logits[:, where, :]), C.bank[6][:, 0:NE], ACT.Copy).then_inc(kept, 1)

                act.wait_ge(gate_here, C.mix_gate_loads)
                wide = in_order(turn_gate, products, turn_h, logits)
                turn_gate(0, 0)
                wide(0, 0, first=True)
                wide(1, 1)
                with act.Fori(1, TURNS - 1) as t:
                    for j in range(2):
                        wide(t * 2 + j, j)
                wide(NWIDE - 2, 0)
                wide(NWIDE - 1, 1, more=False)
                logits(NWIDE - 1, TPW - 2)
                turn_h(NWIDE - 1, TPW - 1)
                logits(NWIDE - 1, TPW - 1)
                for r in range(2):
                    act.wait_ge(x1_stored[r], NT // 2 * 16)
                    act.wait_ge(h_stored[r], NT // 2 * 16)
    S.clear()


def route(nc, C, S, b_router, row_token):
    with ExitStack() as ctx:
        sb = lambda n, s, dt=F32: ctx.enter_context(nc.sbuf_tensor("rou_" + n, s, dt))
        b = sb("b", [P, NE])
        prob, masked, tie, both = (sb(n, [P, NT, NE]) for n in ("prob", "masked", "tie", "both"))
        first, second = sb("first", [P, NT, NE]), sb("second", [P, NT, NE])
        top, top2, one = sb("top", [P, NT]), sb("top2", [P, NT]), sb("one", [P, NT])
        group, group_tie = sb("group", [P, NT, NG]), sb("group_tie", [P, NT, NG])
        down_i, down = sb("down_i", [P, NE], I32), sb("down", [P, NE])
        base, base_b = sb("base", [P, NT + 1, NE]), sb("base_b", [P, NT + 1, NE])
        filled, filled_i = sb("filled", [P, NE]), sb("filled_i", [P, NE], I32)
        ends_a, ends_b = sb("ends_a", [P, NE]), sb("ends_b", [P, NE])
        blocks, used, seen_a, seen_b, nth = (sb(n, [P, NE]) for n in ("blocks", "used", "seen_a", "seen_b", "nth"))
        is_nth, by_rank = sb("is_nth", [P, NE, NE]), sb("by_rank", [P, NE, NE])
        place = sb("place", [P, NT, 2])
        starts_i, starts = sb("starts_i", [P, NBLK], I32), sb("starts", [P, NBLK])
        behind, owner = sb("behind", [P, NBLK, NE]), sb("owner", [P, NBLK])
        token, zero = sb("token", [P, NT], I32), sb("zero", [P, ROWS // P], I32)
        index, value = sb("index", [P, 8], I32), sb("value", [P, 8], I32)
        rows_i, rows_f = sb("rows_i", [NBLK, BLK], I32), sb("rows_f", [NBLK, BLK])
        b_here, made, steps_done, expd, counted, cleared, read_back, rows_turned, picked = (
            S(n) for n in ("b_here", "made", "steps_done", "expd", "counted", "cleared", "read_back", "rows_turned", "picked"))
        scattered = S("scattered", pool_dma=True)
        with nc.Block() as block:
            @block.sync
            def _(sp):
                sp.dma_start(b[:], b_router.to_broadcast([P, NE])).then_inc(b_here, 16)
                sp.wait_ge(made, 4)
                sp.dma_start(row_token.rearrange("(p n) a -> p (n a)", p=P), zero[:]).then_inc(cleared, 16)
                sp.wait_ge(scattered, 16 * 2 * NT)
                sp.dma_start(rows_i[:], row_token.rearrange("(b p) a -> b (p a)", p=BLK)).then_inc(read_back, 16)

            @block.gpsimd
            def _(pool):
                pool.iota(down_i[:], pattern=[[-1, NE]], base=NE, channel_multiplier=0).then_inc(made, 1)
                pool.iota(starts_i[:], pattern=[[BLK, NBLK]], base=0, channel_multiplier=0).then_inc(made, 1)
                pool.iota(token[:], pattern=[[P, NT]], base=0, channel_multiplier=1).then_inc(made, 1)
                pool.memset(zero[:], 0).then_inc(made, 1)
                pool.wait_ge(cleared, 16)
                pool.wait_ge(made, 4)
                pool.wait_ge(steps_done, C.route_placed)
                with pool.Fori(0, NT // 4) as t:
                    pool.wait_ge(scattered, t * 8 * 16)
                    pool.nop(nofuse=True)
                    dest = C.dest[:, bass.ds(t * 4, 4), :].rearrange("p t k -> p (t k)")
                    pool.tensor_copy(index[:], dest).then_inc(picked, 1)
                    pool.tensor_copy(value[:].rearrange("p (t k) -> p t k", k=2),
                                     token[:, bass.ds(t * 4, 4)].unsqueeze(2).to_broadcast([P, 4, 2])).then_inc(picked, 1)
                    pool.wait_ge(picked, t * 2 + 2)
                    pool.nop(nofuse=True)
                    for n in range(8):
                        pool.indirect_dma_start(out=row_token, out_offset=bass.IndirectOffsetOnAxis(ap=index[:, n:n + 1], axis=0),
                                                in_=value[:, n:n + 1], in_offset=None).then_inc(scattered, 16)

            @block.vector
            def _(dve):
                steps = Steps(dve, steps_done)
                tt = lambda o, a, c, op: steps.then(dve.tensor_tensor(o, a, c, op))
                ts = lambda o, a, s1, op0, s2=None, op1=ALU.bypass: steps.then(dve.tensor_scalar(o, a, s1, s2, op0, op1))
                red = lambda o, a, op: steps.then(dve.tensor_reduce(o, a, AX.X, op))
                per = lambda a, n: a.unsqueeze(2).to_broadcast([P, NT, n])
                row = lambda a: a.unsqueeze(1).to_broadcast([P, NT, NE])
                dve.wait_ge(b_here, 16)
                dve.wait_ge(made, 4)
                steps.then(dve.tensor_copy(down[:], down_i[:]))
                steps.then(dve.tensor_copy(starts[:], starts_i[:]))
                tt(prob[:], C.logits[:], row(b[:]), ALU.add)
                red(top[:], prob[:], ALU.max)
                tt(prob[:], prob[:], per(top[:], NE), ALU.subtract)
                C.route_shifted = steps.n
                dve.wait_ge(expd, 1)
                red(one[:], prob[:], ALU.add)
                steps.then(dve.reciprocal(one[:], one[:]))
                tt(prob[:], prob[:], per(one[:], NE), ALU.mult)
                red(group[:], prob[:].rearrange("p t (g e) -> p t g e", g=NG), ALU.max)
                red(top[:], group[:], ALU.max)
                tt(group_tie[:], group[:], per(top[:], NG), ALU.is_equal)
                tt(group_tie[:], group_tie[:], down[:, NE - NG:NE].unsqueeze(1).to_broadcast([P, NT, NG]), ALU.mult)
                red(one[:], group_tie[:], ALU.max)
                tt(group[:], group_tie[:], per(one[:], NG), ALU.is_equal)
                inside = group[:].unsqueeze(3).to_broadcast([P, NT, NG, EPG])
                four = lambda a: a.rearrange("p t (g e) -> p t g e", g=NG)
                tt(four(masked[:]), four(prob[:]), inside, ALU.mult)
                steps.then(dve.tensor_copy(four(tie[:]), inside))
                steps.then(dve.scalar_tensor_tensor(out=masked[:], in0=tie[:], scalar=-1.0, in1=masked[:], op0=ALU.add, op1=ALU.add))
                for best, pick in ((top, first), (top2, second)):
                    red(best[:], masked[:], ALU.max)
                    tt(tie[:], masked[:], per(best[:], NE), ALU.is_equal)
                    tt(tie[:], tie[:], row(down[:]), ALU.mult)
                    red(one[:], tie[:], ALU.max)
                    tt(pick[:], tie[:], per(one[:], NE), ALU.is_equal)
                    if pick is first:
                        steps.then(dve.scalar_tensor_tensor(out=masked[:], in0=first[:], scalar=-4.0, in1=masked[:], op0=ALU.mult, op1=ALU.add))
                tt(one[:], top[:], top2[:], ALU.add)
                steps.then(dve.reciprocal(one[:], one[:]))
                tt(C.gate[:, :, 0], top[:], one[:], ALU.mult)
                tt(C.gate[:, :, 1], top2[:], one[:], ALU.mult)
                tt(both[:], first[:], second[:], ALU.add)
                C.route_chosen = steps.n

                def running_sums(x, y, n, at):
                    step = 1
                    while step < n:
                        steps.done(dve.tensor_copy(at(y, 0, step), at(x, 0, step)))
                        tt(at(y, step, n), at(x, step, n), at(x, 0, n - step), ALU.add)
                        x, y, step = y, x, 2 * step
                    return x

                steps.done(dve.memset(base[:, 0, :], 0.0))
                dve.wait_ge(counted, 2)
                total = C.bank[1][:, 0:NT * NE].rearrange("p (t e) -> p t e", e=NE)
                steps.then(dve.tensor_copy(base[:, 1:NT + 1, :], total))
                sums = running_sums(base, base_b, NT + 1, lambda x, lo, hi: x[:, lo:hi, :])
                ts(filled[:], sums[:, NT, :], float(BLK - 1), ALU.add)
                steps.then(dve.tensor_copy(filled_i[:], filled[:]))
                ts(filled_i[:], filled_i[:], 7, ALU.logical_shift_right, 7, ALU.logical_shift_left)
                steps.then(dve.tensor_copy(filled[:], filled_i[:]))
                steps.then(dve.tensor_copy(ends_a[:], filled[:]))
                steps.then(dve.tensor_copy(blocks[:], filled[:]))
                ends = running_sums(ends_a, ends_b, NE, lambda x, lo, hi: x[:, lo:hi])
                tt(filled[:], ends[:], filled[:], ALU.subtract)
                before = C.bank[0][:, 0:NT * NE].rearrange("p (t e) -> p t e", e=NE)
                tt(sums[:, 0:NT, :], sums[:, 0:NT, :], row(filled[:]), ALU.add)
                tt(sums[:, 0:NT, :], sums[:, 0:NT, :], before, ALU.add)
                for k, pick in enumerate((first, second)):
                    tt(tie[:], pick[:], sums[:, 0:NT, :], ALU.mult)
                    red(place[:, :, k], tie[:], ALU.add)
                steps.then(dve.tensor_copy(C.dest[:], place[:]))
                assert steps.n == C.route_placed, steps.n
                ts(used[:], blocks[:], 0.0, ALU.is_gt)
                steps.then(dve.tensor_copy(seen_a[:], used[:]))
                seen = running_sums(seen_a, seen_b, NE, lambda x, lo, hi: x[:, lo:hi])
                tt(behind[:], ends[:].unsqueeze(1).to_broadcast([P, NBLK, NE]), starts[:].unsqueeze(2).to_broadcast([P, NBLK, NE]), ALU.is_le)
                tt(behind[:], behind[:], used[:].unsqueeze(1).to_broadcast([P, NBLK, NE]), ALU.mult)
                red(owner[:], behind[:], ALU.add)
                ts(one[:, 0:1], seen[:, NE - 1:NE], -1.0, ALU.add)
                tt(owner[:], owner[:], one[:, 0:1].to_broadcast([P, NBLK]), ALU.min)
                steps.then(dve.tensor_copy(C.rank[:], owner[:]))
                ts(nth[:], down[:], -1.0, ALU.mult, float(NE + 1), ALU.add)
                tt(is_nth[:], seen[:].unsqueeze(1).to_broadcast([P, NE, NE]), nth[:].unsqueeze(2).to_broadcast([P, NE, NE]), ALU.is_equal)
                tt(is_nth[:], is_nth[:], used[:].unsqueeze(1).to_broadcast([P, NE, NE]), ALU.mult)
                ts(blocks[:], nth[:], -1.0, ALU.add)
                tt(by_rank[:], is_nth[:], blocks[:].unsqueeze(1).to_broadcast([P, NE, NE]), ALU.mult)
                red(blocks[:], by_rank[:], ALU.add)
                steps.then(dve.tensor_copy(C.expert[:], blocks[:]))
                steps.then(dve.tensor_copy(filled_i[:], ends[:]))
                ts(filled_i[:], filled_i[:], 7, ALU.logical_shift_right)
                steps.then(dve.tensor_copy(blocks[:], filled_i[:]))
                tt(by_rank[:], is_nth[:], blocks[:].unsqueeze(1).to_broadcast([P, NE, NE]), ALU.mult)
                red(blocks[:], by_rank[:], ALU.add)
                tt(nth[:], nth[:], seen[:, NE - 1:NE].to_broadcast([P, NE]), ALU.is_ge)
                ts(nth[:], nth[:], float(NBLK), ALU.mult)
                tt(blocks[:], blocks[:], nth[:], ALU.max)
                steps.then(dve.tensor_copy(C.blocks_end[:], blocks[:]))
                dve.wait_ge(read_back, 16)
                steps.then(dve.tensor_copy(rows_f[:], rows_i[:]))
                C.route_read = steps.n
                dve.wait_ge(rows_turned, 1)
                steps.then(dve.tensor_copy(C.source[:], C.bank[2][:, 0:NBLK]))

            @block.scalar
            def _(act):
                act.wait_ge(steps_done, C.route_shifted)
                act.activation(prob[:], prob[:], ACT.Exp).then_inc(expd, 1)

            @block.tensor
            def _(pe):
                pe.wait_ge(steps_done, C.route_chosen)
                for n, mask in enumerate((C.lt, C.ones)):
                    pe.matmul(C.bank[n][:, 0:NT * NE].rearrange("p (t e) -> p t e", e=NE), mask[:], both[:], start=True, stop=True).then_inc(counted, 1)
                pe.wait_ge(steps_done, C.route_read)
                pe.transpose(C.bank[2][:, 0:NBLK], rows_f[:], C.ident[0:NBLK, 0:NBLK]).then_inc(rows_turned, 1)
    S.clear()


def experts(nc, C, S, h_dram, w_gate, w_up, w_down, rows_out):
    TURNS = (NBLK - 3) // 2
    assert NBLK == 2 * TURNS + 3
    KD = DE // P
    with ExitStack() as ctx:
        sb = lambda n, s, dt=F32: ctx.enter_context(nc.sbuf_tensor("exp_" + n, s, dt))
        wg, wu, wd = sb("wg", [P, 2, KT * DE]), sb("wu", [P, 2, KT * DE]), sb("wd", [P, 2, KD * D])
        index = sb("index", [P, 2], I32)
        h, ht = sb("h", [P, 2, D]), sb("ht", [P, 2, KT, P])
        silu, hid, hid_t = sb("silu", [P, DE]), sb("hid", [P, DE]), sb("hid_t", [P, 2, KD, P])
        out = sb("out", [P, 2, D])
        x0, x1, gate_b, up_b, hid_b, out0, out1 = (C.bank[n] for n in range(7))
        picked, turned, taken0, taken1, gate_mm, up_mm, down_mm, silu_done, hid_done, hid_turned, hid_taken, out0_read, out1_read = (
            S(n) for n in ("picked", "turned", "taken0", "taken1", "gate_mm", "up_mm", "down_mm", "silu_done", "hid_done",
                           "hid_turned", "hid_taken", "out0_read", "out1_read"))
        wg_here, wu_here, wd_here, h_here, stored = (
            [S(f"{n}{j}", pool_dma=n in ("h_here", "stored")) for j in range(2)] for n in ("wg_here", "wu_here", "wd_here", "h_here", "stored"))
        gv = w_gate.rearrange("e (p k) n -> e p (k n)", p=P)
        uv = w_up.rearrange("e (p k) n -> e p (k n)", p=P)
        dv = w_down.rearrange("e (p k) n -> e p (k n)", p=P)

        flat = lambda a: a.rearrange("p a n -> p (a n)")

        flat_w = lambda a: a.rearrange("a p n -> p (a n)")

        def blocks(eng, body, first, last):
            first()
            body(1, 1)
            with eng.Fori(1, TURNS + 1) as t:
                for j in range(2):
                    body(t * 2 + j, j)
            last()

        with nc.Block() as block:
            @block.sync
            def _(sp):
                streams = ((wg, gv, wg_here, gate_mm), (wu, uv, wu_here, up_mm), (wd, dv, wd_here, down_mm))

                def expert_of(rank):
                    one = bass.ds(rank, 1) if not isinstance(rank, int) else slice(rank, rank + 1)
                    return sp.value_load(C.expert[0:1, one], min_val=0, max_val=NE - 1)

                for rank in range(2):
                    e = expert_of(rank)
                    for to, of, here, _ in streams:
                        sp.dma_start(to[:, rank, :], flat_w(of[bass.ds(e, 1)])).then_inc(here[rank], 16)
                with sp.Fori(1, NE // 2) as t:
                    for j in range(2):
                        rank = t * 2 + j
                        e = expert_of(rank)
                        last = sp.value_load(C.blocks_end[0:1, bass.ds(rank - 2, 1)], min_val=0, max_val=NBLK)
                        for to, of, here, free in streams:
                            sp.wait_ge(here[j], t * 16)
                            sp.nop(nofuse=True)
                            sp.wait_ge(free, last)
                            sp.nop(nofuse=True)
                            sp.dma_start(to[:, j, :], flat_w(of[bass.ds(e, 1)])).then_inc(here[j], 16)
                for _, _, here, _ in streams:
                    for j in range(2):
                        sp.wait_ge(here[j], NE // 2 * 16)

            @block.gpsimd
            def _(pool):
                def gather(b, j, wait=True):
                    if wait:
                        pool.wait_ge(turned, (b - 1) * 2)
                        pool.nop(nofuse=True)
                    one = bass.ds(b, 1) if not isinstance(b, int) else slice(b, b + 1)
                    pool.tensor_copy(index[:, j:j + 1], C.source[:, one]).then_inc(picked, 1)
                    pool.wait_ge(picked, b + 1)
                    pool.nop(nofuse=True)
                    pool.indirect_dma_start(out=h[:, j, :], out_offset=None, in_=h_dram,
                                            in_offset=bass.IndirectOffsetOnAxis(ap=index[:, j:j + 1], axis=0)).then_inc(h_here[j], 16)

                def store(b, j):
                    pool.wait_ge(out0_read, b + 1)
                    pool.nop(nofuse=True)
                    pool.wait_ge(out1_read, b + 1)
                    pool.nop(nofuse=True)
                    rows = bass.ds(b * BLK, BLK) if not isinstance(b, int) else slice(b * BLK, (b + 1) * BLK)
                    pool.dma_start(rows_out[rows, :], out[:, j, :]).then_inc(stored[j], 16)

                gather(0, 0, wait=False)
                gather(1, 1, wait=False)
                with pool.Fori(1, NBLK // 2) as t:
                    for j in range(2):
                        b = t * 2 + j
                        gather(b, j)
                        store(b - 2, j)
                gather(NBLK - 1, 0)
                store(NBLK - 3, 0)
                store(NBLK - 2, 1)
                store(NBLK - 1, 0)
                for j in range(2):
                    pool.wait_ge(stored[j], (NBLK + 1 - j) // 2 * 16)

            @block.tensor
            def _(pe):
                def turn(b, j):
                    pe.wait_ge(h_here[j], b // 2 * 16 + 16)
                    pe.wait_ge(taken0, b)
                    for k in range(4):
                        tr = pe.transpose(x0[:, k * P:(k + 1) * P], h[:, j, k::KT], C.ident[:])
                    tr.then_inc(turned, 1)
                    pe.wait_ge(taken1, b)
                    for k in range(4, KT):
                        tr = pe.transpose(x1[:, (k - 4) * P:(k - 3) * P], h[:, j, k::KT], C.ident[:])
                    tr.then_inc(turned, 1)

                def rank_of(b):
                    one = bass.ds(b, 1) if not isinstance(b, int) else slice(b, b + 1)
                    return pe.value_load(C.rank[0:1, one], min_val=0, max_val=NE - 1)

                def wait_for_weights(here, e):
                    pe.wait_ge(here[0], (e // 2 + 1) * 16)
                    pe.wait_ge(here[1], (e + 1) // 2 * 16)
                    pe.nop(nofuse=True)

                def hidden(b, j, e, of, bank, here, done, read, between=None):
                    wait_for_weights(here, e)
                    pe.wait_ge(read, b)
                    pe.wait_ge(taken0, b + 1)
                    pe.wait_ge(taken1, b + 1)
                    pe.nop(nofuse=True)
                    for k in range(KT):
                        if between and k == KT // 2:
                            between()
                        mul = pe.matmul(bank[:, :], ht[:, j, k, :], flat(of[:, bass.ds(e % 2, 1), k * DE:(k + 1) * DE]),
                                        start=k == 0, stop=k == KT - 1)
                    mul.then_inc(done, 1)

                def turn_hidden(b, j):
                    pe.wait_ge(hid_done, b + 1)
                    pe.wait_ge(hid_taken, b)
                    for k in range(KD):
                        tr = pe.transpose(hid_b[:, k * P:(k + 1) * P], hid[:, k::KD], C.ident[:])
                    tr.then_inc(hid_turned, 1)

                def down(b, j, e):
                    wait_for_weights(wd_here, e)
                    pe.wait_ge(hid_taken, b + 1)
                    for bank, read, q in ((out0, out0_read, 0), (out1, out1_read, 1)):
                        pe.wait_ge(read, b)
                        pe.nop(nofuse=True)
                        for k in range(KD):
                            mul = pe.matmul(bank[:, :], hid_t[:, j, k, :],
                                            flat(wd[:, bass.ds(e % 2, 1), k * D + q * WIDE:k * D + (q + 1) * WIDE]),
                                            start=k == 0, stop=k == KD - 1)
                    mul.then_inc(down_mm, 1)

                def part(b, j, e):
                    down(b - 1, 1 - j, e[0])
                    hidden(b, j, e[1], wu, up_b, wu_here, up_mm, hid_done, between=lambda: turn(b + 1, 1 - j))
                    hidden(b + 1, 1 - j, e[2], wg, gate_b, wg_here, gate_mm, silu_done, between=lambda: turn_hidden(b, j))

                turn(0, 0)
                e = [rank_of(b) for b in range(3)]
                hidden(0, 0, e[0], wg, gate_b, wg_here, gate_mm, silu_done)
                hidden(0, 0, e[0], wu, up_b, wu_here, up_mm, hid_done, between=lambda: turn(1, 1))
                hidden(1, 1, e[1], wg, gate_b, wg_here, gate_mm, silu_done, between=lambda: turn_hidden(0, 0))
                part(1, 1, e)
                with pe.Fori(1, TURNS + 1) as t:
                    e = [rank_of(t * 2 - 1 + n) for n in range(4)]
                    for j in range(2):
                        part(t * 2 + j, j, e[j:])
                e = [rank_of(b) for b in (NBLK - 2, NBLK - 1)]
                down(NBLK - 2, 1, e[0])
                hidden(NBLK - 1, 0, e[1], wu, up_b, wu_here, up_mm, hid_done)
                turn_hidden(NBLK - 1, 0)
                down(NBLK - 1, 0, e[1])

            @block.scalar
            def _(act):
                def take(b, j):
                    act.wait_ge(turned, b * 2 + 1)
                    act.activation(ht[:, j, 0:4, :].rearrange("p k n -> p (k n)"), x0[:, :], ACT.Copy).then_inc(taken0, 1)

                def gate(b):
                    act.wait_ge(gate_mm, b + 1)
                    act.wait_ge(hid_done, b)
                    act.activation(silu[:], gate_b[:, :], ACT.Silu).then_inc(silu_done, 1)

                def hidden(b, j):
                    act.wait_ge(hid_turned, b + 1)
                    act.activation(hid_t[:, j].rearrange("p k n -> p (k n)"), hid_b[:, :], ACT.Copy).then_inc(hid_taken, 1)

                def result(b, j):
                    act.wait_ge(down_mm, b + 1)
                    act.wait_ge(stored[j], b // 2 * 16)
                    act.activation(out[:, j, 0:WIDE], out0[:, :], ACT.Copy).then_inc(out0_read, 1)

                def first():
                    take(0, 0)
                    gate(0)
                    take(1, 1)
                    hidden(0, 0)

                def body(b, j, more=True):
                    gate(b)
                    result(b - 1, 1 - j)
                    if more:
                        take(b + 1, 1 - j)
                    hidden(b, j)

                def last():
                    body(NBLK - 1, 0, more=False)
                    result(NBLK - 1, 0)
                blocks(act, body, first, last)

            @block.vector
            def _(dve):
                def take(b, j):
                    dve.wait_ge(turned, b * 2 + 2)
                    dve.tensor_copy(ht[:, j, 4:KT, :].rearrange("p k n -> p (k n)"), x1[:, :]).then_inc(taken1, 1)

                def hidden(b):
                    dve.wait_ge(up_mm, b + 1)
                    dve.wait_ge(silu_done, b + 1)
                    dve.wait_ge(hid_turned, b)
                    dve.tensor_tensor(hid[:], silu[:], up_b[:, :], ALU.mult).then_inc(hid_done, 1)

                def result(b, j):
                    dve.wait_ge(down_mm, b + 1)
                    dve.wait_ge(stored[j], b // 2 * 16)
                    dve.tensor_copy(out[:, j, WIDE:D], out1[:, :]).then_inc(out1_read, 1)

                def first():
                    take(0, 0)
                    take(1, 1)
                    hidden(0)

                def body(b, j, more=True):
                    result(b - 1, 1 - j)
                    if more:
                        take(b + 1, 1 - j)
                    hidden(b)

                def last():
                    body(NBLK - 1, 0, more=False)
                    result(NBLK - 1, 0)
                blocks(dve, body, first, last)
    S.clear()


def combine(nc, C, S, rows_out, x1_dram, mod, ln_g_row, ln_b_row, out_sample, out_prompt):
    TURNS = NT // 2
    with ExitStack() as ctx:
        sb = lambda n, s, dt=F32: ctx.enter_context(nc.sbuf_tensor("com_" + n, s, dt))
        g2, ln_g, ln_b = sb("g2", [P, 2, D]), sb("ln_g", [P, D]), sb("ln_b", [P, D])
        index = sb("index", [P, 2, 2], I32)
        r, x1, v = sb("r", [P, 2, 2, D]), sb("x1", [P, 2, D]), sb("v", [P, 2, D])
        stats, mean, y = sb("stats", [P, 2, 6]), sb("mean", [P, 2, 2]), sb("y", [P, 2, D])
        flat = lambda a: a.rearrange("p a n -> p (a n)")
        scaled_v = sb("scaled_v", [P, 2, D])
        minus = sb("minus", [P, 2, 1])
        w_here, picked, weighted, ln, rooted, normed, scaled, shifted = (
            S(n) for n in ("w_here", "picked", "weighted", "ln", "rooted", "normed", "scaled", "shifted"))
        x1_here, stored = ([S(f"{n}{j}") for j in range(2)] for n in ("x1_here", "stored"))
        r_here = [S(f"r_here{j}", pool_dma=True) for j in range(2)]
        SUM, GATED, X1_ADDED, STATS0, STATS1, MEAN = range(1, 7)
        LN = MEAN
        one = lambda n: bass.ds(n, 1) if not isinstance(n, int) else slice(n, n + 1)

        def tiles(eng, body, first=2):
            with eng.Fori(first // 2, TURNS) as t:
                for j in range(2):
                    body(t * 2 + j, j)

        with nc.Block() as block:
            @block.sync
            def _(sp):
                def store(n, j, to):
                    sp.wait_ge(shifted, n + 1)
                    sp.nop(nofuse=True)
                    sp.dma_start(to, y[:, j, :]).then_inc(stored[j], 16)

                for j in range(2):
                    sp.dma_start(x1[:, j, :], x1_dram[j * P:(j + 1) * P, :]).then_inc(x1_here[j], 16)
                for s in range(2):
                    sp.dma_start(g2[:, s, :], mod[s:s + 1, 5 * D:6 * D].to_broadcast([P, D])).then_inc(w_here, 16)
                sp.dma_start(ln_g[:], ln_g_row.to_broadcast([P, D])).then_inc(w_here, 16)
                sp.dma_start(ln_b[:], ln_b_row.to_broadcast([P, D])).then_inc(w_here, 16)
                for lo, hi, start, out in ((1, NT_SAMPLE // 2 + 1, 0, out_sample), (NT_SAMPLE // 2 + 1, TURNS, NT_SAMPLE, out_prompt)):
                    with sp.Fori(lo, hi) as t:
                        for j in range(2):
                            n = t * 2 + j
                            sp.wait_ge(ln, (n - 2) * LN + X1_ADDED)
                            sp.nop(nofuse=True)
                            sp.dma_start(x1[:, j, :], x1_dram[bass.ds(n * P, P), :]).then_inc(x1_here[j], 16)
                            store(n - 2, j, out[0, bass.ds((n - 2 - start) * P, P), :])
                for j in range(2):
                    store(NT - 2 + j, j, out_prompt[0, PROMPT - (2 - j) * P:PROMPT - (1 - j) * P, :])
                for j in range(2):
                    sp.wait_ge(stored[j], TURNS * 16)

            @block.gpsimd
            def _(pool):
                def gather(n, j, wait=True):
                    if wait:
                        pool.wait_ge(ln, (n - 2) * LN + SUM)
                        pool.nop(nofuse=True)
                    pool.tensor_copy(index[:, j, :], flat(C.dest[:, one(n), :])).then_inc(picked, 1)
                    pool.wait_ge(picked, n + 1)
                    pool.nop(nofuse=True)
                    for k in range(2):
                        pool.indirect_dma_start(out=r[:, j, k, :], out_offset=None, in_=rows_out,
                                                in_offset=bass.IndirectOffsetOnAxis(ap=index[:, j, k:k + 1], axis=0)).then_inc(r_here[j], 16)

                def shift(n, j):
                    pool.wait_ge(scaled, n + 1)
                    pool.wait_ge(stored[j], n // 2 * 16)
                    pool.tensor_tensor(y[:, j, :], scaled_v[:, j, :], ln_b[:], ALU.add).then_inc(shifted, 1)

                def root(n, j):
                    pool.wait_ge(ln, n * LN + MEAN)
                    pool.wait_ge(normed, n)
                    pool.nop(nofuse=True)
                    pool.tensor_scalar(mean[:, j, 1:2], mean[:, j, 1:2], EPS, None, ALU.add).then_inc(rooted, 1)
                    pool.wait_ge(rooted, n * 3 + 1)
                    pool.tensor_tensor(mean[:, j, 1:2], mean[:, j, 1:2], C.minus_half[:], ALU.pow).then_inc(rooted, 1)
                    pool.wait_ge(rooted, n * 3 + 2)
                    pool.nop(nofuse=True)
                    pool.tensor_scalar(minus[:, j, :], mean[:, j, 0:1], mean[:, j, 1:2], -1.0, ALU.mult, ALU.mult).then_inc(rooted, 1)

                gather(0, 0, wait=False)
                gather(1, 1, wait=False)
                pool.wait_ge(w_here, 64)
                gather(2, 0)
                root(0, 0)
                gather(3, 1)
                shift(0, 0)
                root(1, 1)

                def tile(n, j):
                    gather(n, j)
                    shift(n - 3, 1 - j)
                    root(n - 2, j)
                tiles(pool, tile, first=4)
                shift(NT - 3, 1)
                root(NT - 2, 0)
                shift(NT - 2, 0)
                root(NT - 1, 1)
                shift(NT - 1, 1)

            @block.scalar
            def _(act):
                def weight(n, j):
                    act.wait_ge(r_here[j], n // 2 * 32 + 32)
                    act.nop(nofuse=True)
                    act.activation(r[:, j, 0, :], r[:, j, 0, :], ACT.Copy, scale=flat(C.gate[:, one(n), 0:1])).then_inc(weighted, 1)

                def norm(n, j):
                    act.wait_ge(rooted, n * 3 + 3)
                    if not isinstance(n, int) or n >= 2:
                        act.wait_ge(shifted, n - 1)
                    act.activation(scaled_v[:, j, :], v[:, j, :], ACT.Identity, scale=mean[:, j, 1:2], bias=minus[:, j, :]).then_inc(normed, 1)

                weight(0, 0)
                weight(1, 1)
                norm(0, 0)

                def tile(n, j):
                    weight(n, j)
                    norm(n - 1, 1 - j)
                tiles(act, tile)
                norm(NT - 1, 1)

            @block.vector
            def _(dve):
                def scale(n, j):
                    dve.wait_ge(normed, n + 1)
                    dve.tensor_tensor(scaled_v[:, j, :], scaled_v[:, j, :], ln_g[:], ALU.mult).then_inc(scaled, 1)

                def tile(n, j, before=True):
                    dve.wait_ge(weighted, n + 1)
                    if not isinstance(n, int):
                        dve.wait_ge(normed, n - 1)
                        dve.nop(nofuse=True)
                    s = dve.snap(seq_of(n, NT_SAMPLE)) if not isinstance(n, int) else 0
                    dve.scalar_tensor_tensor(out=v[:, j, :], in0=r[:, j, 1, :], scalar=flat(C.gate[:, one(n), 1:2]),
                                             in1=r[:, j, 0, :], op0=ALU.mult, op1=ALU.add).then_inc(ln, 1)
                    dve.wait_ge(ln, n * LN + SUM)
                    dve.nop(nofuse=True)
                    dve.tensor_tensor(v[:, j, :], v[:, j, :], flat(g2[:, one(s), :]), ALU.mult).then_inc(ln, 1)
                    dve.wait_ge(ln, n * LN + GATED)
                    dve.wait_ge(x1_here[j], n // 2 * 16 + 16)
                    dve.scalar_tensor_tensor(out=v[:, j, :], in0=x1[:, j, :], scalar=ALPHA, in1=v[:, j, :], op0=ALU.mult, op1=ALU.add).then_inc(ln, 1)
                    if before:
                        scale(n - 1, 1 - j)
                    dve.wait_ge(ln, n * LN + X1_ADDED)
                    for q in range(2):
                        dve.bn_stats(stats[:, q, :], v[:, j, q * WIDE:(q + 1) * WIDE]).then_inc(ln, 1)
                    dve.wait_ge(ln, n * LN + STATS1)
                    dve.nop(nofuse=True)
                    dve.bn_aggr(mean[:, j, :], flat(stats[:])).then_inc(ln, 1)

                dve.wait_ge(w_here, 64)
                tile(0, 0, before=False)
                tile(1, 1)
                tiles(dve, tile)
                scale(NT - 1, 1)
    S.clear()


class Kept:
    pass


def encoder(nc, A, out_sample, out_prompt):
    def scratch(name, shape, dt=F32):
        return nc.dram_tensor(name, shape, dt, kind="Internal").ap()

    with ExitStack() as ctx:
        C = Kept()
        S = Semaphores(nc, ctx)
        kept = lambda name, shape, dt=F32: ctx.enter_context(nc.sbuf_tensor(name, shape, dt))
        C.ident, C.le, C.ge, C.gt, C.lt, C.ones = (kept(n, [P, P]) for n in ("ident", "le", "ge", "gt", "lt", "ones"))
        C.minus_half = kept("minus_half", [P, 1])
        C.dt_raw = kept("dt_raw", [P, NT, 2 * HEADS])
        C.bank = [ctx.enter_context(nc.psum_tensor(f"bank{b}", [P, WIDE], F32)) for b in range(8)]
        C.dt, C.adt, C.dt_to_end, C.from_start, C.whole = (
            kept(n, [P, NT, 2 * HEADS]) for n in ("dt", "adt", "dt_to_end", "from_start", "whole"))
        mod = scratch("mod", [2, 6 * D])
        zs, u = scratch("zs", [TOK, SSD]), scratch("u", [TOK, SSD])
        raw, bc = scratch("raw", [CONV_CH, RAW_COLS]), scratch("bc", [CT - SSD // P, P, TOK])
        xb, y_ssd = scratch("xb", [TOK, SSD + 2 * STATE]), scratch("y_ssd", [TOK, SSD])
        constants(nc, C, S)
        with ExitStack() as of_w_in:
            C.w_in = of_w_in.enter_context(nc.sbuf_tensor("w_in", [P, KT, IN_COLS], F32))
            C.w_in_here = ctx.enter_context(nc.semaphore("w_in_here"))

            def load_w_in(sp):
                sp.dma_start(C.w_in[:], A["w_in"][0].rearrange("(p k) n -> p k n", p=P)).then_inc(C.w_in_here, 16)

            adapt(nc, C, S, A["c"], A["w_ada"][0], A["b_ada"], mod, range(0, 2), ahead=load_w_in)
            project(nc, C, S, A["x"], mod, zs, raw, u)
        convolve(nc, C, S, raw, A["conv_w"], A["conv_b"], xb, bc)
        decays(nc, C, S, A["ssd_dt_bias"], A["ssd_a_log"])
        with ExitStack() as of_ssd:
            C.h_back = of_ssd.enter_context(nc.sbuf_tensor("h_back", [P, NT + 2, SSD], F32))
            scan_back(nc, C, S, xb)
            scan_forward(nc, C, S, xb, bc, zs, A["ssd_d"], y_ssd)
        yg = scratch("yg", [TOK, SSD])
        with ExitStack() as of_s5:
            sb = lambda n, s: of_s5.enter_context(nc.sbuf_tensor(n, s, F32))
            C.states = sb("states", [P, C_S, 2, 2, 2 * PAIRS])
            C.power_y = [sb(f"power_y{c}", [P, PAIRS, 2, T5 + 1]) for c in range(2)]
            C.b_bar = sb("b_bar", [P, PAIRS, 2, 2, CH5])
            C.d5_diag = sb("d5_diag", [CH5, G5, CH5])
            turned = scratch("turned", [PAIRS, P, 2 * HALF * C_ALL])
            kernels = scratch("kernels", [2, 2, CH5, (2 * T5 - 1) * CH5])
            with ExitStack() as of_states:
                sb = lambda n, s: of_states.enter_context(nc.sbuf_tensor(n, s, F32))
                C.power_w = [sb(f"power_w{c}", [P, PAIRS, 2, T5]) for c in range(2)]
                C.carry_re, C.carry_im = sb("carry_re", [P, 2, 2 * PAIRS]), sb("carry_im", [P, 2, 2 * PAIRS])
                s5_tables(nc, C, S, A["s5_lam_re"], A["s5_lam_im"], A["s5_log_step"], A["s5_b_re"], A["s5_b_im"], A["s5_d"])
                s5_states_in(nc, C, S, u, turned)
                t1, t2 = sb("car_t1", [P, 2, 2, 2 * PAIRS]), sb("car_t2", [P, 2, 2, 2 * PAIRS])
                carried = S("carried")
                adapt(nc, C, S, A["c"], A["w_ada"][0], A["b_ada"], mod, range(2, 6), beside=lambda dve: s5_carry(dve, C, carried, t1, t2))
            s5_outputs(nc, C, S, turned, kernels, A["s5_c_re"], A["s5_c_im"], yg)
        C.logits, C.gate = kept("logits", [P, NT, NE]), kept("gate", [P, NT, 2])
        C.blocks_end, C.rank = kept("blocks_end", [P, NE], I32), kept("rank", [P, NBLK], I32)
        C.dest, C.expert, C.source = kept("dest", [P, NT, 2], I32), kept("expert", [P, NE], I32), kept("source", [P, NBLK], I32)
        C.mix_gate_loads, C.mix_loads = 16 * 3, 16 * 10
        x1, h = scratch("x1", [TOK, D]), scratch("h", [TOK, D])
        mix_out(nc, C, S, y_ssd, yg, A["x"], mod, A, x1, h)
        C.route_placed = 67
        row_token = scratch("row_token", [ROWS, 1], I32)
        route(nc, C, S, A["b_router"], row_token)
        rows_out = scratch("rows_out", [ROWS, D])
        experts(nc, C, S, h, A["w_gate"][0], A["w_up"][0], A["w_down"][0], rows_out)
        combine(nc, C, S, rows_out, x1, mod, A["ln2_g"], A["ln2_b"], out_sample, out_prompt)


def layout(a):
    a = dict(a)
    t = np.ascontiguousarray
    for n in ("x", "c"):
        if n not in a:
            a[n] = np.concatenate([a[n + "_sample"].reshape(-1, D), a[n + "_prompt"].reshape(-1, D)])
            del a[n + "_sample"], a[n + "_prompt"]
    a["conv_w"] = t(a["conv_w"][0].T.reshape(CT, P, TAPS).transpose(1, 0, 2))
    a["conv_b"] = t(a["conv_b"][0].reshape(CT, P).T)
    for n in ("ssd_dt_bias", "ssd_a_log"):
        a[n] = a[n].reshape(1, 2 * HEADS)
    for n in ("ssd_norm_w", "s5_b_glu"):
        a[n] = t(a[n][0].reshape(-1, P).T)
    a["b_router"] = a["b_router"].reshape(1, NE)
    by_state = lambda x: t(x.reshape(2, PAIRS, 2, N5).transpose(2, 3, 1, 0).reshape(P, 2 * PAIRS))
    a["s5_lam_re"], a["s5_lam_im"] = by_state(a["s5_lam_re"][0]), by_state(a["s5_lam_im"][0])
    a["s5_log_step"] = t(a["s5_log_step"][0].reshape(2, PAIRS, 2).transpose(2, 1, 0).reshape(2, 2 * PAIRS))
    for n in ("s5_b_re", "s5_b_im"):
        a[n] = t(a[n][0].reshape(PAIRS, 2, N5, CH5).transpose(1, 2, 0, 3).reshape(P, PAIRS, CH5))
    for n in ("s5_c_re", "s5_c_im"):
        a[n] = t(a[n][0].reshape(2, PAIRS, 2, CH5, N5).transpose(2, 4, 1, 0, 3).reshape(P, PAIRS, 2, CH5))
    return a


OUTPUTS = ((1, PROMPT, D), (1, SAMPLE, D))


def kernel(**inputs):
    import concourse.bacc as bacc
    from concourse.bass_utils import run_bass_kernel_spmd

    nc = bacc.Bacc("TRN2", target_bir_lowering=False, num_devices=1)
    arrays, aps = {}, {}
    for name, a in layout({n: np.asarray(v) for n, v in inputs.items()}).items():
        arrays[f"in_{name}"] = np.ascontiguousarray(a)
        aps[name] = nc.dram_tensor(f"in_{name}", a.shape, mybir.dt.from_np(a.dtype), kind="ExternalInput").ap()
    outs = [nc.dram_tensor(f"out_{i}", s, F32, kind="ExternalOutput").ap() for i, s in enumerate(OUTPUTS)]
    encoder(nc, aps, outs[1], outs[0])
    r = run_bass_kernel_spmd(nc, [arrays], core_ids=[0]).results[0]
    return r["out_0"], r["out_1"]
```
